# Optimizing a Trainium2 kernel written in Bass

```python
import jax, jax.numpy as jnp
from jax import lax
import numpy as np

D_MODEL = 1024
BATCH = 1
SEQ = 512
DEPTH = 1

CHUNK = 64
ATT_HEADS = 8
ATT_HEAD_DIM = 64
ATT_WIDTH = ATT_HEADS * ATT_HEAD_DIM
N_PREV_CHUNKS = 8
BAND_CHUNKS = N_PREV_CHUNKS + 1
REL_CLIP = 256
SSD_HEAD_DIM = 64
SSD_WIDTH = D_MODEL
SSD_HEADS = SSD_WIDTH // SSD_HEAD_DIM
SSD_GROUPS = 2
SSD_STATE = 128
SSD_CONV = 4
SSD_CHUNK = CHUNK
CONV_DIM = SSD_WIDTH + 2 * SSD_GROUPS * SSD_STATE
MIX_WIDTH = ATT_WIDTH + SSD_WIDTH
IN_PROJ = 3 * ATT_WIDTH + SSD_WIDTH + CONV_DIM + SSD_HEADS
SPLITS = [ATT_WIDTH, 2 * ATT_WIDTH, 3 * ATT_WIDTH,
          3 * ATT_WIDTH + SSD_WIDTH,
          3 * ATT_WIDTH + SSD_WIDTH + CONV_DIM]
D_FF = 4 * D_MODEL
EPS = 1e-5


def rmsnorm(x, w):
    xf = x.astype(jnp.float32)
    y = xf * lax.rsqrt(jnp.mean(xf * xf, axis=-1, keepdims=True) + EPS)
    return (y * w.astype(jnp.float32)).astype(x.dtype)

def chunk_band_attention(q, k, v, rel_bias):
    bsz, seq = q.shape[0], q.shape[1]
    nc = seq // CHUNK
    shp = (bsz, nc, CHUNK, ATT_HEADS, ATT_HEAD_DIM)
    q = q.reshape(shp)
    k = k.reshape(shp)
    v = v.reshape(shp)
    pad = ((0, 0), (N_PREV_CHUNKS, 0), (0, 0), (0, 0), (0, 0))
    kp = jnp.pad(k, pad)
    vp = jnp.pad(v, pad)
    kb = jnp.concatenate([kp[:, j:j + nc] for j in range(BAND_CHUNKS)], axis=2)
    vb = jnp.concatenate([vp[:, j:j + nc] for j in range(BAND_CHUNKS)], axis=2)
    scale = ATT_HEAD_DIM ** -0.5
    scores = jnp.einsum('bcqhd,bckhd->bhcqk', q, kb).astype(jnp.float32) * scale
    qi = jnp.arange(CHUNK)[:, None]
    kj = jnp.arange(BAND_CHUNKS * CHUNK)[None, :]
    rel = N_PREV_CHUNKS * CHUNK + qi - kj
    idx = jnp.clip(rel, -REL_CLIP, REL_CLIP) + REL_CLIP
    bias = jnp.transpose(rel_bias.astype(jnp.float32)[idx], (2, 0, 1))
    key_chunk = jnp.arange(nc)[:, None] - N_PREV_CHUNKS + jnp.arange(BAND_CHUNKS)[None, :]
    valid = jnp.repeat(key_chunk >= 0, CHUNK, axis=1)
    scores = scores + bias[None, :, None]
    scores = jnp.where(valid[None, None, :, None, :], scores, -1e30)
    probs = jax.nn.softmax(scores, axis=-1).astype(v.dtype)
    out = jnp.einsum('bhcqk,bckhd->bcqhd', probs, vb)
    return out.reshape(bsz, seq, ATT_WIDTH)

def causal_depthwise_conv(u, w, b):
    out = lax.conv_general_dilated(
        u, w[:, None, :].astype(u.dtype), window_strides=(1,),
        padding=[(SSD_CONV - 1, 0)], dimension_numbers=('NWC', 'WIO', 'NWC'),
        feature_group_count=u.shape[-1])
    return out + b.astype(u.dtype)

def ssd_scan(x, dt, A, Bm, Cm):
    bsz, seq = x.shape[0], x.shape[1]
    nc = seq // SSD_CHUNK
    L = SSD_CHUNK
    r = SSD_HEADS // SSD_GROUPS
    X = (x * dt[..., None]).reshape(bsz, nc, L, SSD_GROUPS, r, SSD_HEAD_DIM)
    a = jnp.moveaxis((dt * A).reshape(bsz, nc, L, SSD_GROUPS, r), 2, -1)
    a_cum = jnp.cumsum(a, axis=-1)
    Bc = Bm.reshape(bsz, nc, L, SSD_GROUPS, SSD_STATE)
    Cc = Cm.reshape(bsz, nc, L, SSD_GROUPS, SSD_STATE)
    tril = jnp.tril(jnp.ones((L, L), dtype=bool))
    seg = a_cum[..., :, None] - a_cum[..., None, :]
    decay_in = jnp.exp(jnp.where(tril, seg, -jnp.inf))
    cb = jnp.einsum('bclgn,bcsgn->bcgls', Cc, Bc)
    y_diag = jnp.einsum('bcgls,bcgrls,bcsgrp->bclgrp', cb, decay_in, X)
    decay_out = jnp.exp(a_cum[..., -1:] - a_cum)
    states = jnp.einsum('bcsgn,bcgrs,bcsgrp->bcgrpn', Bc, decay_out, X)
    chunk_decay = jnp.exp(a_cum[..., -1])

    def step(carry, inp):
        st, dec = inp
        return carry * dec[..., None, None] + st, carry

    init = jnp.zeros_like(states[:, 0])
    _, prev = lax.scan(step, init, (jnp.moveaxis(states, 1, 0), jnp.moveaxis(chunk_decay, 1, 0)))
    prev = jnp.moveaxis(prev, 0, 1)
    y_off = jnp.einsum('bclgn,bcgrpn,bcgrl->bclgrp', Cc, prev, jnp.exp(a_cum))
    return (y_diag + y_off).reshape(bsz, seq, SSD_HEADS, SSD_HEAD_DIM)

def ssd_mixer(z, xbc, dt_raw, conv_w, conv_b, dt_bias, a_log, d_skip, norm_w):
    bsz, seq = z.shape[0], z.shape[1]
    xbc = jax.nn.silu(causal_depthwise_conv(xbc, conv_w, conv_b)).astype(jnp.float32)
    xs = xbc[..., :SSD_WIDTH]
    Bm = xbc[..., SSD_WIDTH:SSD_WIDTH + SSD_GROUPS * SSD_STATE].reshape(bsz, seq, SSD_GROUPS, SSD_STATE)
    Cm = xbc[..., SSD_WIDTH + SSD_GROUPS * SSD_STATE:].reshape(bsz, seq, SSD_GROUPS, SSD_STATE)
    dt = jax.nn.softplus(dt_raw.astype(jnp.float32) + dt_bias.astype(jnp.float32))
    A = -jnp.exp(a_log.astype(jnp.float32))
    xh = xs.reshape(bsz, seq, SSD_HEADS, SSD_HEAD_DIM)
    y = ssd_scan(xh, dt, A, Bm, Cm) + d_skip.astype(jnp.float32)[:, None] * xh
    y = y.reshape(bsz, seq, SSD_WIDTH) * jax.nn.silu(z.astype(jnp.float32))
    yg = y.reshape(bsz, seq, SSD_GROUPS, SSD_WIDTH // SSD_GROUPS)
    yg = yg * lax.rsqrt(jnp.mean(yg * yg, axis=-1, keepdims=True) + EPS)
    y = yg.reshape(bsz, seq, SSD_WIDTH) * norm_w.astype(jnp.float32)
    return y.astype(z.dtype)

def first_inputs(seed: int = 0) -> dict:
    key = jax.random.key(seed)
    ks = jax.random.split(key, 16)
    f32 = jnp.float32
    x = jax.random.normal(ks[0], (BATCH, SEQ, D_MODEL), f32)
    norm_mix_w = 1.0 + 0.05 * jax.random.normal(ks[1], (DEPTH, D_MODEL), f32)
    w_in = jax.random.normal(ks[2], (DEPTH, D_MODEL, IN_PROJ), f32) * D_MODEL ** -0.5
    rel_bias = 0.1 * jax.random.normal(ks[3], (DEPTH, 2 * REL_CLIP + 1, ATT_HEADS), f32)
    conv_w = jax.random.normal(ks[4], (DEPTH, SSD_CONV, CONV_DIM), f32) * SSD_CONV ** -0.5
    conv_b = 0.01 * jax.random.normal(ks[5], (DEPTH, CONV_DIM), f32)
    dt0 = jnp.exp(jax.random.uniform(ks[6], (DEPTH, SSD_HEADS), f32,
                                     minval=np.log(1e-3), maxval=np.log(1e-1)))
    dt_bias = dt0 + jnp.log(-jnp.expm1(-dt0))
    a_log = jnp.log(jax.random.uniform(ks[7], (DEPTH, SSD_HEADS), f32, minval=1.0, maxval=16.0))
    d_skip = 1.0 + 0.1 * jax.random.normal(ks[8], (DEPTH, SSD_HEADS), f32)
    ssd_norm_w = 1.0 + 0.05 * jax.random.normal(ks[9], (DEPTH, SSD_WIDTH), f32)
    w_out = jax.random.normal(ks[10], (DEPTH, MIX_WIDTH, D_MODEL), f32) * MIX_WIDTH ** -0.5
    norm_mlp_w = 1.0 + 0.05 * jax.random.normal(ks[11], (DEPTH, D_MODEL), f32)
    w_ff1 = jax.random.normal(ks[12], (DEPTH, D_MODEL, D_FF), f32) * D_MODEL ** -0.5
    w_ff2 = jax.random.normal(ks[13], (DEPTH, D_FF, D_MODEL), f32) * D_FF ** -0.5
    norm_final_w = 1.0 + 0.05 * jax.random.normal(ks[14], (D_MODEL,), f32)
    return {"x": x, "norm_mix_w": norm_mix_w, "w_in": w_in, "rel_bias": rel_bias,
            "conv_w": conv_w, "conv_b": conv_b, "dt_bias": dt_bias, "a_log": a_log,
            "d_skip": d_skip, "ssd_norm_w": ssd_norm_w, "w_out": w_out,
            "norm_mlp_w": norm_mlp_w, "w_ff1": w_ff1, "w_ff2": w_ff2,
            "norm_final_w": norm_final_w}

def first_block(x, norm_mix_w, w_in, rel_bias, conv_w, conv_b, dt_bias, a_log, d_skip,
              ssd_norm_w, w_out, norm_mlp_w, w_ff1, w_ff2, norm_final_w):
    h = x
    for i in range(DEPTH):
        hn = rmsnorm(h, norm_mix_w[i])
        proj = hn @ w_in[i]
        q, k, v, z, xbc, dt_raw = jnp.split(proj, SPLITS, axis=-1)
        att = chunk_band_attention(q, k, v, rel_bias[i])
        ssd = ssd_mixer(z, xbc, dt_raw, conv_w[i], conv_b[i], dt_bias[i],
                        a_log[i], d_skip[i], ssd_norm_w[i])
        h = h + jnp.concatenate([att, ssd], axis=-1) @ w_out[i]
        hn = rmsnorm(h, norm_mlp_w[i])
        h = h + jnp.square(jax.nn.relu(hn @ w_ff1[i])) @ w_ff2[i]
    return rmsnorm(h, norm_final_w)


PLE_DIM = 256
EPS_2 = 1e-6
GMLP_GROUPS = 8
GMLP_GROUP_DIM = 128
GMLP_WIDTH = GMLP_GROUPS * GMLP_GROUP_DIM
GMLP_BLOCK = 128
FOX_HEADS = 16
FOX_HEAD_DIM = 64
FOX_WIDTH = FOX_HEADS * FOX_HEAD_DIM
Q_BLOCK = 128
D_FF_2 = 2816
CONV_WIDTH = 3
N_BRANCH = 2
IN_COLS = 2 * GMLP_WIDTH + 3 * FOX_WIDTH + FOX_HEADS + N_BRANCH * D_MODEL


def rmsnorm_2(x, g):
    x32 = x.astype(jnp.float32)
    y = x32 * lax.rsqrt(jnp.mean(x32 * x32, axis=-1, keepdims=True) + EPS_2)
    return (y * g.astype(jnp.float32)).astype(x.dtype)

def layernorm(x, g, b):
    x32 = x.astype(jnp.float32)
    mu = jnp.mean(x32, axis=-1, keepdims=True)
    xc = x32 - mu
    y = xc * lax.rsqrt(jnp.mean(xc * xc, axis=-1, keepdims=True) + EPS_2)
    return (y * g.astype(jnp.float32) + b.astype(jnp.float32)).astype(x.dtype)

def gmlp_spatial_gating(z_u, z_v, ln_g, ln_b, w_s, b_s):
    B, S, _ = z_u.shape
    v = layernorm(z_v, ln_g, ln_b)
    v = v.reshape(B, S // GMLP_BLOCK, GMLP_BLOCK, GMLP_GROUPS, GMLP_GROUP_DIM)
    pos = jnp.arange(GMLP_BLOCK)
    mask = (pos[None, :] // CHUNK) <= (pos[:, None] // CHUNK)
    w = jnp.where(mask[None], w_s, jnp.zeros_like(w_s))
    mixed = jnp.einsum('gts,bnsgc->bntgc', w, v) + b_s.T[None, None, :, :, None]
    return z_u * mixed.reshape(B, S, GMLP_WIDTH)

def forgetting_attention(q, k, v, f_logit, b_f):
    B, S, _ = q.shape
    def heads(t):
        return t.reshape(B, S, FOX_HEADS, FOX_HEAD_DIM).transpose(0, 2, 1, 3)
    q, k, v = heads(q), heads(k), heads(v)
    log_f = jax.nn.log_sigmoid(f_logit.astype(jnp.float32) + b_f.astype(jnp.float32))
    cum = jnp.cumsum(log_f, axis=1).transpose(0, 2, 1)
    scale = FOX_HEAD_DIM ** -0.5
    outs = []
    for i in range(S // Q_BLOCK):
        lo, hi = i * Q_BLOCK, (i + 1) * Q_BLOCK
        s = jnp.einsum('bhqd,bhkd->bhqk', q[:, :, lo:hi], k[:, :, :hi]).astype(jnp.float32) * scale
        s = s + cum[:, :, lo:hi, None] - cum[:, :, None, :hi]
        qpos = jnp.arange(lo, hi)
        kpos = jnp.arange(hi)
        s = jnp.where(kpos[None, :] <= qpos[:, None], s, -1e30)
        prob = jax.nn.softmax(s, axis=-1).astype(v.dtype)
        outs.append(jnp.einsum('bhqk,bhkd->bhqd', prob, v[:, :, :hi]))
    o = jnp.concatenate(outs, axis=2)
    return o.transpose(0, 2, 1, 3).reshape(B, S, FOX_WIDTH)

def causal_depthwise_conv_2(u, w, b):
    S = u.shape[1]
    up = jnp.pad(u, ((0, 0), (CONV_WIDTH - 1, 0), (0, 0)))
    out = b + w[0] * up[:, 0:S]
    for j in range(1, CONV_WIDTH):
        out = out + w[j] * up[:, j:j + S]
    return out

def second_inputs(seed: int = 0) -> dict:
    key = jax.random.key(seed)
    ks = jax.random.split(key, 24)
    f32 = jnp.float32
    def nrm(k, shape, scale):
        return jax.random.normal(k, shape, f32) * scale
    L = DEPTH
    return {
        "x": nrm(ks[0], (BATCH, SEQ, D_MODEL), 1.0),
        "p": nrm(ks[1], (DEPTH, BATCH, SEQ, PLE_DIM), 1.0),
        "norm_mix_g": 1.0 + nrm(ks[2], (L, D_MODEL), 0.02),
        "w_in": nrm(ks[3], (L, D_MODEL, IN_COLS), D_MODEL ** -0.5),
        "b_f": 2.0 + nrm(ks[4], (L, FOX_HEADS), 0.5),
        "gmlp_ln_g": 1.0 + nrm(ks[5], (L, GMLP_WIDTH), 0.02),
        "gmlp_ln_b": nrm(ks[6], (L, GMLP_WIDTH), 0.02),
        "gmlp_w_s": nrm(ks[7], (L, GMLP_GROUPS, GMLP_BLOCK, GMLP_BLOCK), GMLP_BLOCK ** -0.5),
        "gmlp_b_s": 1.0 + nrm(ks[8], (L, GMLP_GROUPS, GMLP_BLOCK), 0.1),
        "w_branch_a": nrm(ks[9], (L, GMLP_WIDTH, D_MODEL), GMLP_WIDTH ** -0.5),
        "w_branch_b": nrm(ks[10], (L, FOX_WIDTH, D_MODEL), FOX_WIDTH ** -0.5),
        "w_out": nrm(ks[11], (L, D_MODEL, D_MODEL), D_MODEL ** -0.5),
        "norm_ffn_g": 1.0 + nrm(ks[12], (L, D_MODEL), 0.02),
        "w_up": nrm(ks[13], (L, D_MODEL, 2 * D_FF_2), D_MODEL ** -0.5),
        "conv_w": nrm(ks[14], (L, CONV_WIDTH, 2 * D_FF_2), CONV_WIDTH ** -0.5),
        "conv_b": nrm(ks[15], (L, 2 * D_FF_2), 0.02),
        "w_down": nrm(ks[16], (L, D_FF_2, D_MODEL), D_FF_2 ** -0.5),
        "norm_ple_g": 1.0 + nrm(ks[17], (L, D_MODEL), 0.02),
        "w_ple": nrm(ks[18], (L, PLE_DIM, D_MODEL), PLE_DIM ** -0.5),
        "w_ple_gate": nrm(ks[19], (L, D_MODEL, D_MODEL), D_MODEL ** -0.5),
        "norm_final_g": 1.0 + nrm(ks[20], (D_MODEL,), 0.02),
    }

def second_block(x, p, norm_mix_g, w_in, b_f, gmlp_ln_g, gmlp_ln_b, gmlp_w_s, gmlp_b_s,
              w_branch_a, w_branch_b, w_out, norm_ffn_g, w_up, conv_w, conv_b, w_down,
              norm_ple_g, w_ple, w_ple_gate, norm_final_g):
    o1 = 2 * GMLP_WIDTH
    o2 = o1 + 3 * FOX_WIDTH
    o3 = o2 + FOX_HEADS
    for i in range(DEPTH):
        h = rmsnorm_2(x, norm_mix_g[i])
        z = jnp.einsum('bsd,dc->bsc', h, w_in[i])
        uv = jax.nn.gelu(z[..., :o1])
        z_u, z_v = uv[..., :GMLP_WIDTH], uv[..., GMLP_WIDTH:]
        q = z[..., o1:o1 + FOX_WIDTH]
        k = z[..., o1 + FOX_WIDTH:o1 + 2 * FOX_WIDTH]
        v = z[..., o1 + 2 * FOX_WIDTH:o2]
        f_logit = z[..., o2:o3]
        gates = jax.nn.sigmoid(z[..., o3:])
        gate_a, gate_b = gates[..., :D_MODEL], gates[..., D_MODEL:]

        a = gmlp_spatial_gating(z_u, z_v, gmlp_ln_g[i], gmlp_ln_b[i], gmlp_w_s[i], gmlp_b_s[i])
        b = forgetting_attention(q, k, v, f_logit, b_f[i])
        y_a = jnp.einsum('bsc,cd->bsd', a, w_branch_a[i])
        y_b = jnp.einsum('bsc,cd->bsd', b, w_branch_b[i])
        merged = gate_a * y_a + gate_b * y_b
        x = x + jnp.einsum('bsd,de->bse', merged, w_out[i])

        h2 = rmsnorm_2(x, norm_ffn_g[i])
        up = jnp.einsum('bsd,df->bsf', h2, w_up[i])
        up = causal_depthwise_conv_2(up, conv_w[i], conv_b[i])
        act = jax.nn.gelu(up[..., :D_FF_2]) * up[..., D_FF_2:]
        x = x + jnp.einsum('bsf,fd->bsd', act, w_down[i])

        h3 = rmsnorm_2(x, norm_ple_g[i])
        ple = jnp.einsum('bse,ed->bsd', p[i], w_ple[i])
        x = x + ple * jax.nn.sigmoid(jnp.einsum('bsd,de->bse', h3, w_ple_gate[i]))
    return rmsnorm_2(x, norm_final_g)


def setup_inputs(seed=0):
    out = dict(first_inputs(seed))
    for name, value in second_inputs(seed + 1).items():
        if name != "x":
            out[name + "_2"] = value
    return out


def reference(
    x, norm_mix_w, w_in, rel_bias, conv_w, conv_b, dt_bias, a_log, d_skip, ssd_norm_w, w_out,
    norm_mlp_w, w_ff1, w_ff2, norm_final_w, p_2, norm_mix_g_2, w_in_2, b_f_2, gmlp_ln_g_2,
    gmlp_ln_b_2, gmlp_w_s_2, gmlp_b_s_2, w_branch_a_2, w_branch_b_2, w_out_2, norm_ffn_g_2,
    w_up_2, conv_w_2, conv_b_2, w_down_2, norm_ple_g_2, w_ple_2, w_ple_gate_2, norm_final_g_2,
):
    x = first_block(
        x, norm_mix_w, w_in, rel_bias, conv_w, conv_b, dt_bias, a_log, d_skip, ssd_norm_w,
        w_out, norm_mlp_w, w_ff1, w_ff2, norm_final_w,
    )
    return second_block(
        x, p_2, norm_mix_g_2, w_in_2, b_f_2, gmlp_ln_g_2, gmlp_ln_b_2, gmlp_w_s_2, gmlp_b_s_2,
        w_branch_a_2, w_branch_b_2, w_out_2, norm_ffn_g_2, w_up_2, conv_w_2, conv_b_2, w_down_2,
        norm_ple_g_2, w_ple_2, w_ple_gate_2, norm_final_g_2,
    )


_drawn_inputs = setup_inputs


def setup_inputs(seed=0):
    import zlib

    import numpy as np

    out = dict(_drawn_inputs(seed))
    spreads = {}
    factors = {'rel_bias': 8.0,
     'conv_b': 4.996,
     'norm_mix_g_2': 4.284,
     'gmlp_ln_g_2': 8.0,
     'gmlp_ln_b_2': 8.0,
     'norm_ffn_g_2': 12.184,
     'conv_b_2': 12.424,
     'norm_ple_g_2': 200.0,
     'norm_final_g_2': 22.709,
     'gmlp_b_s_2': 3.01,
     'p_2': 8.0,
     'w_ple_2': 8.0,
     'w_ple_gate_2': 8.0}
    for name, (base, spread) in spreads.items():
        noise = np.random.default_rng([zlib.crc32(name.encode()), seed]).standard_normal(out[name].shape)
        drawn = base * np.exp(spread * noise) if base else spread * noise
        out[name] = __import__('jax').numpy.asarray(drawn.astype(out[name].dtype))
    for name, factor in factors.items():
        out[name] = (out[name] * factor).astype(out[name].dtype)
    return out
```

```python
from contextlib import ExitStack

import numpy as np

import concourse.bass as bass
from concourse import mybir

F32 = mybir.dt.float32
F32R = mybir.dt.float32r
BF16 = mybir.dt.bfloat16
ALU = mybir.AluOpType
ACT = mybir.ActivationFunctionType
AX_X = mybir.AxisListType.X

P = 128
D = 1024
T = 512
KT = D // P
TT = T // P
STRIP = 256
SW = KT * STRIP
EPS1 = 1e-5
EPS2 = 1e-6
HEAD = 64
H1 = 8
H2 = 16
H_SSD = 16
GROUPS = 2
CONV1 = 4
CONV2 = 3
NXBC = 12
D_FF = 4096
FF_GROUPS = D_FF // D
UP_TILES = 2816 // P
BIG = 1e30
QUAD = 4
STEPS = QUAD * TT
REL = 256

PHASES = [("qk", 4), ("v", 2), ("xbc", 6), ("z", 4), ("wo_att", 2), ("wo_ssd", 4)]
PHASES += [(f"{w}{g}", 4) for g in range(FF_GROUPS) for w in ("ff1_", "ff2_")]
PHASES += [(w + h, n) for h in "ab" for w, n in (("qk2", 4), ("v2", 2))]
PHASES += [("gate_b", 4), ("branch_b", 4), ("zv", 4), ("u", 4), ("gate_a", 4), ("branch_a", 4), ("out2", 4)]
PHASES += [("up0", 8), ("down0", 4), ("up1", 8), ("down1", 4), ("up2", 6), ("down2", 4), ("ple", 1), ("gate", 4)]
FIRST = {}
for _name, _n in PHASES:
    FIRST[_name] = sum(n for _, n in PHASES[:len(FIRST)])
N_STRIPS = sum(n for _, n in PHASES)

ON_ACT = {"v", "z", "v2a", "v2b", "zv", "ple"}
FILLS = {name: 2 * n for name, n in PHASES} | {"wo_att": 8, "ple": 8}


def evac_base():
    seen, base = {True: 0, False: 0}, {}
    for name, _ in PHASES:
        on_act = name in ON_ACT
        base[name] = seen[on_act]
        seen[on_act] += FILLS[name]
    return base


EVAC0 = evac_base()


def build(nc, d, out):
    ctx = ExitStack()
    with ctx:
        base = (nc.sbuf_base + 63) // 64 * 64
        place = {}
        cursor = [0]

        def sb(name, shape, dt=F32, at=None):
            size = 2 if dt == BF16 else 4
            cols = -(-int(np.prod(shape[1:])) * size // 32) * 8
            off = cursor[0] if at is None else at
            if at is None:
                cursor[0] += cols
            place[name] = off
            assert base + 4 * (off + cols) <= nc.sbuf_usable_end, (name, off, cols)
            return nc.alloc_sbuf_tensor_at(name, list(shape), dt, offset=base + 4 * off).ap()

        def sem(name):
            return ctx.enter_context(nc.semaphore(name))

        x = sb("x", [P, KT, T])
        a_hi = sb("a_hi", [P, KT, T], F32R)
        a_lo = sb("a_lo", [P, KT, T], F32R)
        b_hi = sb("b_hi", [P, KT, T], F32R)
        b_lo = sb("b_lo", [P, KT, T], F32R)
        w_raw = [sb(f"w_raw{j}", [P, KT, STRIP]) for j in range(2)]
        w_hi = [sb(f"w_hi{j}", [P, KT, STRIP], F32R) for j in range(2)]
        w_lo = [sb(f"w_lo{j}", [P, KT, STRIP], F32R) for j in range(2)]
        ident = sb("ident", [P, P])
        steps01 = sb("steps01", [P, 7 * P])
        tri, ones = steps01[:, 3 * P:4 * P], steps01[:, 4 * P:5 * P]
        ident16 = sb("ident16", [P, P], BF16)
        future16 = sb("future16", [P, P], BF16)
        past16 = sb("past16", [P, P], BF16)
        gains = sb("gains", [P, 9, KT])
        conv1_w = sb("conv1_w", [P, NXBC, CONV1 + 1])
        conv2_w = sb("conv2_w", [P, 2 * UP_TILES, CONV2 + 1])
        heads1 = sb("heads1", [P, 3, H_SSD])
        bf2 = sb("bf2", [P, H2])
        w16_raw = [sb(f"w16_raw{j}", [P, KT, 16]) for j in range(2)]
        w16_hi = [sb(f"w16_hi{j}", [P, KT, 16], F32R) for j in range(2)]
        w16_lo = [sb(f"w16_lo{j}", [P, KT, 16], F32R) for j in range(2)]
        rstd = sb("rstd", [P, T])
        rstd_tok = sb("rstd_tok", [P, TT])
        exp_a = sb("exp_a", [P, H_SSD])
        row_max = sb("row_max", [P, STEPS])
        row_sum = sb("row_sum", [P, STEPS])
        row_inv = sb("row_inv", [P, STEPS])
        stats = sb("stats", [P, 3, 8])
        wait_note = sb("wait_note", [P, 1])
        work = cursor[0]

        A_HI, A_LO, B_HI, B_LO = (place[n] for n in ("a_hi", "a_lo", "b_hi", "b_lo"))
        sq = [sb(f"sq{j}", [P, T], at=work + j * T) for j in range(2)]
        head_bias = sb("head_bias", [P, H1 * T], at=B_HI)
        qk = sb("qk", [P, 8 * T], at=B_LO)
        o = work
        v_tok = sb("v_tok", [P, TT * 8 * HEAD], at=o); o += TT * 8 * HEAD
        att_tok = sb("att_tok", [P, TT, D], at=o); o += TT * D
        score = sb("score", [P, 4, T], at=o); o += 4 * T
        prob_t = sb("prob_t", [P, 2, T], at=o); o += 2 * T
        q_pair = sb("q_pair", [P, 2, T], at=o); o += 2 * T
        k_pair = sb("k_pair", [P, 2, T], at=o); o += 2 * T
        cum_t = sb("cum_t", [16, T], at=o); o += T
        sp = {n: sb(f"sp_{n}", [P, TT * 16], at=o + 64 * j) for j, n in enumerate(
            ("x", "na", "e", "d", "r", "s", "q", "p", "m", "val", "a", "nacum", "diff", "eac", "cdec", "dout"))}
        o += 64 * len(sp)
        o = work
        z_tok = sb("z_tok", [P, TT * D], at=o); o += TT * D
        xs_tok = sb("xs_tok", [P, TT * D], at=o); o += TT * D
        bc_t = sb("bc_t", [P, 4, T], at=o); o += 4 * T
        b_tok = sb("b_tok", [P, TT, 256], at=o); o += TT * 256
        assert o <= place["sp_x"]
        acum_t = sb("acum_t", [16, T], at=place["cum_t"])
        u_pad = [sb(f"u_pad{j}", [P, CONV1 - 1 + T], at=B_LO + 2048 + 520 * j) for j in range(2)]
        conv = [sb(f"conv{j}", [P, T], at=B_HI + 2048 + T * j) for j in range(2)]
        xs_t = [sb(f"xs_t{j}", [P, T], at=B_HI + 3072 + T * j) for j in range(2)]
        decay = sb("decay", [P, H_SSD, P], at=A_HI)
        x_dt = sb("x_dt", [P, D], at=A_HI + 2048)
        x_out = sb("x_out", [P, D], at=A_HI + 3072)
        state = sb("state", [P, D], at=A_LO)
        y_tmp = sb("y_tmp", [P, D], at=A_LO + 1024)
        x_skip = sb("x_skip", [P, D], at=A_LO + 2048)
        b_c = sb("b_c", [P, 2, P], at=A_LO + 3072)
        c_c = sb("c_c", [P, 2, P], at=A_LO + 3328)
        bt_c = sb("bt_c", [P, 256], at=A_LO + 3584)
        relu = [sb(f"relu{j}", [P, T], at=work + 2048 + T * j) for j in range(2)]
        relu2 = [sb(f"relu2_{j}", [P, T], at=work + 3072 + T * j) for j in range(2)]
        o = work
        merged = sb("merged", [P, KT * T], at=o); o += KT * T
        u_t = sb("u_t", [P, KT * T], at=o); o += KT * T
        zv_tok = sb("zv_tok", [P, TT * D], at=o); o += TT * D
        gate_t = sb("gate_t", [P, KT * T], at=place["zv_tok"])
        o = max(o, place["sp_x"] + 64 * len(sp))
        ln_gb = sb("ln_gb", [P, 2, D], at=o); o += 2 * D
        ws_t = sb("ws_t", [P, KT, P], at=o); o += KT * P
        bs_bc = sb("bs_bc", [P, KT, P], at=o); o += KT * P
        sq_wide = sb("sq_wide", [P, D], at=B_HI + 2048)
        lin2 = [sb(f"lin2_{j}", [P, T], at=place["ln_gb"] + T * j) for j in range(2)]
        lin = [sb(f"lin{j}", [P, T], at=B_HI + T * j) for j in range(2)]
        up_pad = [sb(f"up_pad{j}", [P, CONV2 - 1 + T], at=work + 2048 + 520 * j) for j in range(4)]
        up_c = [sb(f"up_c{j}", [P, T], at=work + 4608 + T * j) for j in range(4)]
        up_g = [sb(f"up_g{j}", [P, T], at=work + 6656 + T * j) for j in range(2)]
        ple_t = sb("ple_t", [P, KT * T], at=work + 8192)
        p_raw = sb("p_raw", [P, 2, T], at=work + 12288)
        p_hi = sb("p_hi", [P, 2, T], F32R, at=work + 13312)
        p_lo = sb("p_lo", [P, 2, T], F32R, at=work + 14336)
        sig = [sb(f"sig{j}", [P, T], at=work + 2048 + T * j) for j in range(2)]
        out_t = [sb(f"out_t{j}", [P, T], at=work + 3072 + T * j) for j in range(8)]

        bank = [ctx.enter_context(nc.psum_tensor(f"bank{j}", [P, T], F32)) for j in range(8)]
        STAT = bank[4]

        x_loaded = [sem(f"x_loaded{j}") for j in range(2)]
        consts_loaded = sem("consts_loaded")
        bias_loaded = sem("bias_loaded")
        p_loaded = sem("p_loaded")
        raw_loaded = [sem(f"raw_loaded{j}") for j in range(2)]
        masks_ready = sem("masks_ready")
        mask_step = sem("mask_step")
        hi_split = sem("hi_split")
        strip_split = sem("strip_split")
        unit_done = sem("unit_done")
        act_evac = sem("act_evac")
        dve_evac = sem("dve_evac")

        def norm_sems(n):
            keys = ["sq", "stat", "var", "std", "rstd"]
            keys += ["hi", "lo"] if not n.startswith("end") else []
            keys += ["turned", "tok"] if n.startswith("mix") else []
            keys += ["x"] if n == "end1" else []
            return {k: sem(f"{n}_{k}") for k in keys}

        NORMS = {n: norm_sems(n) for n in ("mix1", "mlp", "end1", "mix2", "ffn2", "ple", "end2")}
        ws_masked = sem("ws_masked")
        w16_hi_ready = sem("w16_hi_ready")
        w16_ready = sem("w16_ready")
        bias_masked = sem("bias_masked")
        qk_staged = sem("qk_staged")
        scored = sem("scored")
        biased = sem("biased")
        maxed = sem("maxed")
        exped = sem("exped")
        turned = sem("turned")
        prob_ready = sem("prob_ready")
        pv_done = sem("pv_done")
        inverted = sem("inverted")
        att_out = sem("att_out")
        att_turned = sem("att_turned")
        att_hi = sem("att_hi")
        att_lo = sem("att_lo")
        small_done = sem("small_done")
        sp_step = sem("sp_step")
        sp_exp = sem("sp_exp")
        cum_done = sem("cum_done")
        cum_act = sem("cum_act")
        cum_dve = sem("cum_dve")
        cum_spread = sem("cum_spread")
        cum_bias = sem("cum_bias")
        tap0 = sem("tap0")
        taps = sem("taps")
        conv_silu = sem("conv_silu")
        xs_turned = sem("xs_turned")
        xs_ready = sem("xs_ready")
        chunk_staged = sem("chunk_staged")
        x_scaled = sem("x_scaled")
        seg_done = sem("seg_done")
        cb_done = sem("cb_done")
        decayed = sem("decayed")
        mixed_ready = sem("mixed_ready")
        y_done = sem("y_done")
        state_done = sem("state_done")
        y_step = sem("y_step")
        state_ready = sem("state_ready")
        state_step = sem("state_step")
        y_sq = sem("y_sq")
        y_std = sem("y_std")
        y_stat = sem("y_stat")
        y_norm = sem("y_norm")
        y_turned = sem("y_turned")
        ssd_hi = sem("ssd_hi")
        ssd_lo = sem("ssd_lo")
        ff_sq = sem("ff_sq")
        ff_hi = sem("ff_hi")
        ff_lo = sem("ff_lo")
        gated = sem("gated")
        merged_ready = sem("merged_ready")
        m_hi = sem("m_hi")
        m_lo = sem("m_lo")
        ug = sem("ug")
        ln_step = sem("ln_step")
        ln_sq = sem("ln_sq")
        ln_std = sem("ln_std")
        ln_ready = sem("ln_ready")
        mixed_done = sem("mixed_done")
        mix_read = sem("mix_read")
        ln_mean = sem("ln_mean")
        a_ready = sem("a_ready")
        amix_hi = sem("amix_hi")
        amix_lo = sem("amix_lo")
        up_tap0 = sem("up_tap0")
        up_taps = sem("up_taps")
        up_gelu = sem("up_gelu")
        up_act = sem("up_act")
        up_hi = sem("up_hi")
        up_lo = sem("up_lo")
        p_hi_ready = sem("p_hi_ready")
        p_lo_ready = sem("p_lo_ready")
        ple_sig = sem("ple_sig")
        ple_mul = sem("ple_mul")
        out_ready = sem("out_ready")
        stored = sem("stored")

        QUAD0 = {"1": 0, "2a": 2, "2b": 4}
        ATT_T0 = {"1": 0, "2": 4}
        N_CONST = 13
        SP_LOG = 17
        SP_A = SP_LOG + 1
        SP_END = SP_A + SP_LOG

        block = ctx.enter_context(nc.Block())

        def evac_sem(phase):
            return act_evac if phase in ON_ACT else dve_evac

        @block.sync
        def _(sp_eng):
            for j in range(2):
                sp_eng.dma_start(x[:, 4 * j:4 * j + 4, :], d["x_t"][:, 4 * j:4 * j + 4, :]).then_inc(x_loaded[j], 16)
            for j in range(2):
                sp_eng.dma_start(w_raw[j].rearrange("p k n -> p (k n)"), d["strips"][j]).then_inc(raw_loaded[j], 16)
            with sp_eng.Fori(1, N_STRIPS // 2) as i:
                for j in range(2):
                    sp_eng.wait_ge(strip_split, 2 * i + j - 1)
                    sp_eng.dma_start(w_raw[j].rearrange("p k n -> p (k n)"),
                                     d["strips"][bass.ds(2 * i + j, 1)].rearrange("a p n -> (a p) n")).then_inc(raw_loaded[j], 16)
            sp_eng.wait_ge(strip_split, N_STRIPS - 2)
            sp_eng.dma_start(w_raw[0].rearrange("p k n -> p (k n)"), d["strips"][N_STRIPS - 1]).then_inc(raw_loaded[0], 16)
            for m in range(KT):
                sp_eng.wait_ge(out_ready, m + 1)
                sp_eng.dma_start(out[m], out_t[m]).then_inc(stored, 16)
            sp_eng.wait_ge(stored, 16 * KT)

        @block.gpsimd
        def _(pool):
            steps = [0]

            def step(ins):
                steps[0] += 1
                ins.then_inc(mask_step, 1)

            step(pool.memset(ident, 0.0))
            step(pool.memset(steps01[:, 0:3 * P], 0.0))
            step(pool.memset(steps01[:, 3 * P:7 * P], 1.0))
            step(pool.memset(ident16, 0.0))
            step(pool.memset(future16, 0.0))
            step(pool.memset(past16, 0.0))
            pool.wait_ge(mask_step, 6)
            for m in (ident, ident16):
                pool.affine_select(out=m, in_=m, compare_op=ALU.not_equal, fill=1.0, base=0,
                                   pattern=[[-1, P]], channel_multiplier=1).then_inc(masks_ready, 1)
            pool.affine_select(out=tri, in_=tri, compare_op=ALU.is_ge, fill=0.0, base=0,
                               pattern=[[1, P]], channel_multiplier=-1).then_inc(masks_ready, 1)
            pool.affine_select(out=future16, in_=future16, compare_op=ALU.is_ge, fill=-BIG, base=0,
                               pattern=[[-1, P]], channel_multiplier=1).then_inc(masks_ready, 1)
            pool.affine_select(out=past16, in_=past16, compare_op=ALU.is_ge, fill=-BIG, base=0,
                               pattern=[[1, P]], channel_multiplier=-1).then_inc(masks_ready, 1)

            pool.wait_ge(masks_ready, 5)

            def split_strip(j, loads, strip, first):
                pool.wait_ge(raw_loaded[j], 16 * loads)
                if not first:
                    pool.wait_ge(unit_done, 2 * strip - 2)
                pool.tensor_tensor(wait_note, ident[:, 0:1], ident[:, 0:1], ALU.mult)
                pool.tensor_scalar(w_hi[j], w_raw[j], 1.0, 1.0, ALU.mult, ALU.mult).then_inc(hi_split, 1)
                pool.wait_ge(hi_split, strip + 1)
                pool.tensor_tensor(w_lo[j], w_raw[j], w_hi[j].bitcast(F32), ALU.subtract).then_inc(strip_split, 1)

            for j in range(2):
                split_strip(j, 1, j, True)
            with pool.Fori(1, N_STRIPS // 2) as i:
                for j in range(2):
                    split_strip(j, i + 1, 2 * i + j, False)
            split_strip(0, N_STRIPS // 2 + 1, N_STRIPS - 1, False)

        @block.tensor
        def _(pe):
            mm, tr = nc.tensor.matmul, nc.tensor.transpose

            def bank_free(phase, j):
                if j >= 4:
                    pe.wait_ge(evac_sem(phase), EVAC0[phase] + j - 3)
                elif phase != PHASES[0][0]:
                    before = PHASES[[n for n, _ in PHASES].index(phase) - 1][0]
                    pe.wait_ge(evac_sem(before), EVAC0[before] + FILLS[before] + j - 3)

            def feature_unit(ps, slot, u, act, kt=KT, ready=None):
                cols = slice(u * P, u * P + P)
                hi, lo = act
                for k in range(kt):
                    if ready is not None:
                        ready(k)
                    mm(ps[:, :], w_hi[slot][:, k, cols], hi[:, k, :], start=(k == 0), stop=False)
                    mm(ps[:, :], w_hi[slot][:, k, cols], lo[:, k, :], start=False, stop=False)
                    last = mm(ps[:, :], w_lo[slot][:, k, cols], hi[:, k, :], start=False, stop=(k == kt - 1))
                return last

            def token_unit(ps, slot, u, act):
                hi, lo = act
                for t in range(2):
                    dst = ps[:, t * STRIP:(t + 1) * STRIP]
                    tok = slice((2 * u + t) * P, (2 * u + t + 1) * P)
                    for k in range(KT):
                        mm(dst, hi[:, k, tok], w_hi[slot][:, k, :], start=(k == 0), stop=False)
                        mm(dst, hi[:, k, tok], w_lo[slot][:, k, :], start=False, stop=False)
                        last = mm(dst, lo[:, k, tok], w_hi[slot][:, k, :], start=False, stop=(k == KT - 1))
                return last

            def stream(phase, unit, act, ready=None, after=None):
                for s in range(dict(PHASES)[phase]):
                    pe.wait_ge(strip_split, FIRST[phase] + s + 1)
                    for u in range(2):
                        j = 2 * s + u
                        bank_free(phase, j)
                        if unit is feature_unit:
                            ins = unit(bank[j % 4], s % 2, u, act, ready=ready if j == 0 else None)
                        else:
                            if j == 0 and ready is not None:
                                ready(KT - 1)
                            ins = unit(bank[j % 4], s % 2, u, act)
                        ins.then_inc(unit_done, 1)
                        if after is not None:
                            after(j)

            def looped(phase, unit, act, ready=None):
                before = PHASES[[n for n, _ in PHASES].index(phase) - 1][0]
                with pe.Fori(0, dict(PHASES)[phase] // 2) as i:
                    for s in range(2):
                        pe.wait_ge(strip_split, FIRST[phase] + s + 1 + 2 * i)
                        for u in range(2):
                            j = 2 * s + u
                            if evac_sem(before) is not evac_sem(phase):
                                pe.wait_ge(evac_sem(before), EVAC0[before] + FILLS[before] + j - 3)
                            pe.wait_ge(evac_sem(phase), EVAC0[phase] + j - 3 + 4 * i)
                            if unit is feature_unit:
                                ins = unit(bank[j], s, u, act, ready=ready if j == 0 else None)
                            else:
                                if j == 0 and ready is not None:
                                    ready(KT - 1)
                                ins = unit(bank[j], s, u, act)
                            ins.then_inc(unit_done, 1)

            def stat(norm, m):
                n = NORMS[norm]
                pe.wait_ge(n["sq"], m + 1)
                mm(STAT[:, :], ones, sq[m % 2], start=(m == 0), stop=(m == KT - 1)).then_inc(n["stat"], 1)

            def turn_rstd(norm):
                n = NORMS[norm]
                pe.wait_ge(n["rstd"], 1)
                for t in range(TT):
                    last = tr(bank[5][:, t * P:(t + 1) * P], rstd[:, t * P:(t + 1) * P], ident)
                last.then_inc(n["turned"], 1)

            def wait_tiles(s):
                return lambda k: pe.wait_ge(s, k + 1)

            def small_columns(which, act):
                pe.wait_ge(w16_ready, which + 1)
                hi, lo = act
                for t in range(TT):
                    tok = slice(t * P, (t + 1) * P)
                    dst = bank[6][:, t * 16:(t + 1) * 16]
                    for k in range(KT):
                        mm(dst, hi[:, k, tok], w16_hi[which][:, k, :], start=(k == 0), stop=False)
                        mm(dst, hi[:, k, tok], w16_lo[which][:, k, :], start=False, stop=False)
                        last = mm(dst, lo[:, k, tok], w16_hi[which][:, k, :], start=False, stop=(k == KT - 1))
                last.then_inc(small_done, 1)

            def attention(call, causal):
                v_phase = {"1": "v", "2a": "v2a", "2b": "v2b"}[call]
                pe.wait_ge(act_evac, EVAC0[v_phase] + FILLS[v_phase])

                def scores(n, q0):
                    head, i = n // TT, n % TT
                    rows, w = slice(HEAD * (head % 2), HEAD * (head % 2) + HEAD), P * (i + 1)
                    if n % (2 * TT) == 0:
                        pe.wait_ge(qk_staged, 4 * q0 + 2 * (head // 2) + 2)
                    if n >= 3:
                        pe.wait_ge(biased, STEPS * q0 + n - 2)
                    ps = bank[n % 3]
                    q_rows, k_rows = q_pair[rows, head // 2, i * P:(i + 1) * P], k_pair[rows, head // 2, 0:w]
                    if causal:
                        if i:
                            mm(ps[:, 0:w - P], q_rows, k_rows[:, 0:w - P], start=True, stop=True)
                        mm(ps[:, w - P:w], q_rows, k_rows[:, w - P:w], start=True, stop=False)
                        last = mm(ps[:, w - P:w], ident16, future16, start=False, stop=True)
                    else:
                        last = mm(ps[:, 0:w], q_rows, k_rows, start=True, stop=True)
                    last.then_inc(scored, 1)

                def turn(n, q0):
                    i = n % TT
                    pe.wait_ge(exped, STEPS * q0 + n + 1)
                    if n >= 2:
                        pe.wait_ge(prob_ready, STEPS * q0 + n - 1)
                    for j in range(i + 1):
                        last = tr(bank[4 + n % 2][:, j * P:(j + 1) * P], score[:, n % 4, j * P:(j + 1) * P], ident)
                    last.then_inc(turned, 1)

                def values(n, q0, it):
                    head, i = n // TT, n % TT
                    pe.wait_ge(prob_ready, STEPS * q0 + n + 1)
                    if n >= 2:
                        pe.wait_ge(att_out, STEPS * q0 + n - 1)
                    for j in range(i + 1):
                        last = mm(bank[6 + n % 2][:, 0:HEAD], prob_t[:, n % 2, j * P:(j + 1) * P],
                                  v_tok[:, bass.ds(j * 8 * HEAD + head * HEAD + it * (QUAD * HEAD), HEAD)],
                                  start=(j == 0), stop=(j == i))
                    last.then_inc(pv_done, 1)

                with pe.Fori(0, 2) as it:
                    q0 = QUAD0[call] + it
                    for n in range(STEPS + 3):
                        if n < STEPS:
                            scores(n, q0)
                        if 2 <= n < STEPS + 2:
                            turn(n - 2, q0)
                        if n >= 3:
                            values(n - 3, q0, it)
                    pe.wait_ge(att_out, STEPS * q0 + STEPS)

            def turn_attention(blk, tiles, done):
                for m in range(tiles):
                    n = ATT_T0[blk] + m
                    if m >= 2:
                        pe.wait_ge(att_lo, n - 1)
                    for t in range(TT):
                        last = tr(bank[4 + m % 2][:, t * P:(t + 1) * P], att_tok[:, t, m * P:(m + 1) * P], ident)
                    last.then_inc(att_turned, 1)

            A, B = (a_hi, a_lo), (b_hi, b_lo)
            pe.wait_ge(masks_ready, 5)

            for m in range(KT):
                stat("mix1", m)
            stream("qk", feature_unit, A, ready=wait_tiles(NORMS["mix1"]["lo"]))
            turn_rstd("mix1")
            stream("v", token_unit, A)
            attention("1", causal=False)
            turn_attention("1", 4, 32)

            def turn_xs(m):
                pe.wait_ge(conv_silu, m + 1)
                if m >= 2:
                    pe.wait_ge(xs_ready, m - 1)
                else:
                    pe.wait_ge(att_lo, 4)
                src = xs_t[m % 2] if m < 8 else bc_t[:, m - 8, :]
                for t in range(TT):
                    last = tr(bank[4 + m % 2][:, t * P:(t + 1) * P], src[:, t * P:(t + 1) * P], ident)
                last.then_inc(xs_turned, 1)

            stream("xbc", feature_unit, A, after=lambda j: turn_xs(j - 1) if 1 <= j <= 10 else None)
            small_columns(0, A)
            looped("z", token_unit, A)

            pe.wait_ge(sp_step, SP_A)
            mm(bank[6][:, 0:64], tri, sp["a"], start=True, stop=True)
            mm(bank[6][:, 64:128], ones, sp["a"], start=True, stop=True)
            for c in range(TT):
                last = mm(bank[7][0:16, c * P:(c + 1) * P], sp["a"][:, c * 16:(c + 1) * 16], tri, start=True, stop=True)
            last.then_inc(cum_done, 1)

            pe.wait_ge(act_evac, EVAC0["z"] + FILLS["z"])
            pe.wait_ge(cum_dve, 3)
            with pe.Fori(0, TT) as c:
                pe.wait_ge(chunk_staged, 3 * c + 3)
                for g in range(GROUPS):
                    last = mm(bank[4][:, g * P:(g + 1) * P], b_c[:, g, :], c_c[:, g, :], start=True, stop=True)
                last.then_inc(cb_done, 1)
                for q in range(4):
                    for h in range(4):
                        seg = bank[q][:, h * P:(h + 1) * P]
                        mm(seg, ident16, past16, start=True, stop=False)
                        last = mm(seg, ident[0:16, 4 * q + h:4 * q + h + 1].to_broadcast([16, P]),
                                  acum_t[:, bass.ds(c * P, P)], start=False, stop=True)
                    last.then_inc(seg_done, 1)
                for g in range(GROUPS):
                    pe.wait_ge(mixed_ready, 2 * c + g + 1)
                    for h in range(8):
                        last = mm(bank[5 + g][:, h * HEAD:(h + 1) * HEAD], decay[:, 8 * g + h, :],
                                  x_dt[:, (8 * g + h) * HEAD:(8 * g + h + 1) * HEAD], start=True, stop=True)
                pe.wait_ge(state_ready, 2 * c + 2)
                for g in range(GROUPS):
                    last = mm(bank[2 + g][:, :], c_c[:, g, :], state[:, g * 512:(g + 1) * 512], start=True, stop=True)
                last.then_inc(y_done, 1)
                pe.wait_ge(x_scaled, 2 * c + 2)
                for g in range(GROUPS):
                    last = mm(bank[g][:, :], bt_c[:, g * P:(g + 1) * P], x_out[:, g * 512:(g + 1) * 512], start=True, stop=True)
                last.then_inc(state_done, 1)
                pe.wait_ge(state_ready, 2 * c + 4)
                pe.wait_ge(y_step, 6 * c + 6)
            for m in range(KT):
                if m == 0:
                    pe.wait_ge(y_norm, 8)
                if m >= 2:
                    pe.wait_ge(ssd_lo, m - 1)
                for t in range(TT):
                    last = tr(bank[4 + m % 2][:, t * P:(t + 1) * P], z_tok[:, t * D + m * P:t * D + (m + 1) * P], ident)
                last.then_inc(y_turned, 1)

            pe.wait_ge(att_lo, 4)
            for s in range(2):
                pe.wait_ge(strip_split, FIRST["wo_att"] + s + 1)
                hi4 = w_hi[s].rearrange("p k n -> p (k n)").rearrange("p (k n) -> p k n", k=4)
                lo4 = w_lo[s].rearrange("p k n -> p (k n)").rearrange("p (k n) -> p k n", k=4)
                for j in range(4):
                    bank_free("wo_att", 4 * s + j)
                    cols = slice(j * P, (j + 1) * P)
                    for k in range(4):
                        mm(bank[j][:, :], hi4[:, k, cols], b_hi[:, k, :], start=(k == 0), stop=False)
                        mm(bank[j][:, :], hi4[:, k, cols], b_lo[:, k, :], start=False, stop=False)
                        last = mm(bank[j][:, :], lo4[:, k, cols], b_hi[:, k, :], start=False, stop=(k == 3))
                    if j % 2:
                        last.then_inc(unit_done, 1)
            stream("wo_ssd", feature_unit, A, ready=wait_tiles(ssd_lo),
                   after=lambda j: stat("mlp", j - 1) if j else None)
            stat("mlp", KT - 1)

            for g in range(FF_GROUPS):
                stream(f"ff1_{g}", feature_unit, B, ready=wait_tiles(NORMS["mlp"]["lo"]) if g == 0 else None)
                stream(f"ff2_{g}", feature_unit, A, ready=lambda k: pe.wait_ge(ff_lo, KT * g + k + 1),
                       after=(lambda j: stat("end1", j - 1) if j else None) if g == FF_GROUPS - 1 else None)
            stat("end1", KT - 1)

            for m in range(KT):
                stat("mix2", m)
            pe.wait_ge(NORMS["mix2"]["lo"], KT)
            small_columns(1, A)
            turn_rstd("mix2")
            for half in "ab":
                stream("qk2" + half, feature_unit, A)
                if half == "a":
                    pe.wait_ge(sp_step, SP_END)
                    for t in range(TT):
                        last = mm(bank[7][0:16, :], sp["val"][:, t * 16:(t + 1) * 16],
                                  steps01[:, (3 - t) * P:(3 - t) * P + T], start=(t == 0), stop=(t == TT - 1))
                    last.then_inc(cum_done, 1)
                stream("v2" + half, token_unit, A)
                pe.wait_ge(cum_act, 4)
                for h in range(8):
                    n = 8 * (half == "b") + h
                    if h >= 2:
                        pe.wait_ge(cum_bias, n - 1)
                    mm(bank[6 + h % 2][:, :], ident[0:16, n:n + 1].to_broadcast([16, P]), cum_t, start=True,
                       stop=True).then_inc(cum_spread, 1)
                pe.wait_ge(cum_bias, 8 * (half == "b") + 8)
                attention("2" + half, causal=True)
            turn_attention("2", 8, 96)

            looped("gate_b", feature_unit, A)
            stream("branch_b", feature_unit, B, ready=lambda k: pe.wait_ge(att_lo, 4 + k + 1))
            looped("zv", token_unit, A)
            looped("u", feature_unit, A)

            def spatial(g):
                if g == 0:
                    pe.wait_ge(ws_masked, 1)
                    pe.wait_ge(ln_ready, TT)
                if g >= 2:
                    pe.wait_ge(mix_read, g - 1)
                for t in range(TT):
                    last = mm(bank[6 + g % 2][:, t * P:(t + 1) * P], zv_tok[:, t * D + g * P:t * D + (g + 1) * P],
                              ws_t[:, g, :], start=True, stop=True)
                last.then_inc(mixed_done, 1)

            for g in range(KT):
                spatial(g)
            stream("gate_a", feature_unit, A)
            stream("branch_a", feature_unit, B, ready=wait_tiles(amix_lo))
            stream("out2", feature_unit, A, ready=wait_tiles(m_lo),
                   after=lambda j: stat("ffn2", j - 1) if j else None)
            stat("ffn2", KT - 1)

            done = 0
            for g in range(3):
                tiles = min(KT, UP_TILES - done)
                stream(f"up{g}", feature_unit, B, ready=wait_tiles(NORMS["ffn2"]["lo"]) if g == 0 else None)
                for s in range(4):
                    phase = f"down{g}"
                    pe.wait_ge(strip_split, FIRST[phase] + s + 1)
                    for u in range(2):
                        j = 2 * s + u
                        bank_free(phase, j)
                        feature_unit(bank[j % 4], s % 2, u, A, kt=tiles,
                                     ready=(lambda k: pe.wait_ge(up_lo, done + k + 1)) if j == 0 else None).then_inc(unit_done, 1)
                        if g == 2 and j:
                            stat("ple", j - 1)
                done += tiles
            stat("ple", KT - 1)

            pe.wait_ge(strip_split, FIRST["ple"] + 1)
            pe.wait_ge(p_lo_ready, 2)
            slot = FIRST["ple"] % 2
            hi2 = w_hi[slot].rearrange("p k n -> p (k n)").rearrange("p (k n) -> p k n", k=2)
            lo2 = w_lo[slot].rearrange("p k n -> p (k n)").rearrange("p (k n) -> p k n", k=2)
            for m in range(KT):
                bank_free("ple", m)
                cols = slice(m * P, (m + 1) * P)
                for k in range(2):
                    mm(bank[m % 4][:, :], hi2[:, k, cols], p_hi[:, k, :], start=(k == 0), stop=False)
                    mm(bank[m % 4][:, :], hi2[:, k, cols], p_lo[:, k, :], start=False, stop=False)
                    last = mm(bank[m % 4][:, :], lo2[:, k, cols], p_hi[:, k, :], start=False, stop=(k == 1))
                if m % 4 == 3:
                    last.then_inc(unit_done, 1)
            for s in range(4):
                pe.wait_ge(strip_split, FIRST["gate"] + s + 1)
                for u in range(2):
                    j = 2 * s + u
                    bank_free("gate", j)
                    feature_unit(bank[j % 4], (FIRST["gate"] + s) % 2, u, B,
                                 ready=wait_tiles(NORMS["ple"]["lo"]) if j == 0 else None).then_inc(unit_done, 1)
                    if j:
                        stat("end2", j - 1)
            stat("end2", KT - 1)

        @block.scalar
        def _(act):
            run = nc.scalar.activation
            act.dma_start(gains, d["gains"]).then_inc(consts_loaded, 16)
            act.dma_start(conv1_w, d["conv1"]).then_inc(consts_loaded, 16)
            act.dma_start(conv2_w, d["conv2"]).then_inc(consts_loaded, 16)
            act.dma_start(heads1[:, 0, :], d["dt_bias"].partition_broadcast(P)).then_inc(consts_loaded, 16)
            act.dma_start(heads1[:, 1, :], d["a_log"].partition_broadcast(P)).then_inc(consts_loaded, 16)
            act.dma_start(heads1[:, 2, :], d["d_skip"].partition_broadcast(P)).then_inc(consts_loaded, 16)
            act.dma_start(bf2, d["b_f"].partition_broadcast(P)).then_inc(consts_loaded, 16)
            for j in range(2):
                act.dma_start(w16_raw[j], d["w16"][j]).then_inc(consts_loaded, 16)
            act.dma_start(ln_gb[:, 0, :], d["ln_g"].partition_broadcast(P)).then_inc(consts_loaded, 16)
            act.dma_start(ln_gb[:, 1, :], d["ln_b"].partition_broadcast(P)).then_inc(consts_loaded, 16)
            act.dma_start(ws_t, d["ws_t"]).then_inc(consts_loaded, 16)
            act.dma_start(bs_bc.rearrange("p g t -> p (g t)"), d["bs"].partition_broadcast(P)).then_inc(consts_loaded, 16)
            act.dma_start(head_bias.rearrange("p (h m) -> p h m", h=H1), d["rel"].rearrange("h p m -> p h m")).then_inc(bias_loaded, 16)

            def prepare(norm, m, gain, dst, ready):
                n = NORMS[norm]
                ready()
                if m >= 2:
                    act.wait_ge(n["stat"], m - 1)
                run(sq[m % 2], x[:, m, :], ACT.Square).then_inc(n["sq"], 1)
                if dst is not None:
                    run(dst[:, m, :], x[:, m, :], ACT.Copy, scale=gains[:, gain, m:m + 1]).then_inc(n["hi"], 1)

            def root(norm, e):
                n = NORMS[norm]
                act.wait_ge(n["var"], 1)
                run(rstd, rstd, ACT.Sqrt).then_inc(n["std"], 1)

            def attention(call):
                def exps(n, q0):
                    w = P * (n % TT + 1)
                    act.wait_ge(maxed, STEPS * q0 + n + 1)
                    run(score[:, n % 4, 0:w], score[:, n % 4, 0:w], ACT.Exp, bias=row_max[:, n:n + 1],
                        accum_out=row_sum[:, n:n + 1]).then_inc(exped, 1)

                def keep(n, q0):
                    w = P * (n % TT + 1)
                    act.wait_ge(turned, STEPS * q0 + n + 1)
                    if n >= 2:
                        act.wait_ge(pv_done, STEPS * q0 + n - 1)
                    run(prob_t[:, n % 2, 0:w], bank[4 + n % 2][:, 0:w], ACT.Copy).then_inc(prob_ready, 1)

                with act.Fori(0, 2) as it:
                    q0 = QUAD0[call] + it
                    for n in range(STEPS + 2):
                        if n < STEPS:
                            exps(n, q0)
                        if n >= 2:
                            keep(n - 2, q0)
                    act.wait_ge(att_out, STEPS * q0 + STEPS)

            def split_attention(blk, tiles):
                for m in range(tiles):
                    act.wait_ge(att_turned, ATT_T0[blk] + m + 1)
                    run(b_hi[:, m, :], bank[4 + m % 2][:, :], ACT.Copy).then_inc(att_hi, 1)

            act.wait_ge(consts_loaded, 16 * N_CONST)
            for j in range(2):
                run(w16_hi[j], w16_raw[j], ACT.Copy).then_inc(w16_hi_ready, 1)
            run(exp_a, heads1[:, 1, :], ACT.Exp).then_inc(cum_act, 1)
            for m in range(KT):
                prepare("mix1", m, 0, a_hi, lambda: act.wait_ge(x_loaded[m // 4], 16))
            root("mix1", 0)
            act.wait_ge(NORMS["mix1"]["tok"], 1)

            def value_evac(phase):
                for j in range(FILLS[phase]):
                    act.wait_ge(unit_done, 2 * FIRST[phase] + j + 1)
                    for t in range(2):
                        tt = 2 * (j % 2) + t
                        ins = run(v_tok[:, tt * 512 + (j // 2) * STRIP:tt * 512 + (j // 2 + 1) * STRIP],
                                  bank[j % 4][:, t * STRIP:(t + 1) * STRIP], ACT.Copy, scale=rstd_tok[:, tt:tt + 1])
                    ins.then_inc(act_evac, 1)

            value_evac("v")
            attention("1")
            split_attention("1", 4)

            def keep_xs(m):
                act.wait_ge(xs_turned, m + 1)
                src = bank[4 + m % 2][:, :].rearrange("p (t f) -> p t f", t=TT)
                if m < 8:
                    dst = xs_tok.rearrange("p (t f) -> p t f", t=TT)[:, :, m * P:(m + 1) * P]
                else:
                    dst = b_tok[:, :, (m - 8) * P:(m - 7) * P]
                run(dst, src, ACT.Copy).then_inc(xs_ready, 1)

            for m in range(NXBC):
                act.wait_ge(dve_evac, EVAC0["xbc"] + m + 1)
                if m >= 2:
                    act.wait_ge(conv_silu, m - 1)
                run(conv[m % 2], u_pad[m % 2][:, 0:T], ACT.Identity, bias=conv1_w[:, m, CONV1:CONV1 + 1],
                    scale=conv1_w[:, m, 0:1]).then_inc(tap0, 1)
                act.wait_ge(taps, 3 * m + 3)
                if m >= 2 and m < 8:
                    act.wait_ge(xs_turned, m - 1)
                run(xs_t[m % 2] if m < 8 else bc_t[:, m - 8, :], conv[m % 2], ACT.Silu).then_inc(conv_silu, 1)
                if 1 <= m <= 10:
                    keep_xs(m - 1)
            with act.Fori(0, 2) as i:
                for j in range(4):
                    act.wait_ge(unit_done, 4 * i + 2 * FIRST["z"] + j + 1)
                    for t in range(2):
                        tt = 2 * (j % 2) + t
                        ins = run(z_tok[:, bass.ds(i * 512 + tt * D + (j // 2) * STRIP, STRIP)],
                                  bank[j][:, t * STRIP:(t + 1) * STRIP], ACT.Silu, scale=rstd_tok[:, tt:tt + 1])
                    ins.then_inc(act_evac, 1)

            def log_exp(k):
                act.wait_ge(sp_step, SP_A * k + 3)
                run(sp["e"], sp["na"], ACT.Exp).then_inc(sp_exp, 1)

            log_exp(0)
            act.wait_ge(cum_dve, 1)
            run(sp["eac"], bank[6][:, 0:64], ACT.Exp).then_inc(cum_act, 1)
            run(sp["cdec"], bank[6][:, 64:128], ACT.Exp).then_inc(cum_act, 1)
            act.wait_ge(cum_dve, 2)
            run(sp["dout"], sp["diff"], ACT.Exp).then_inc(sp_exp, 1)
            act.wait_ge(cum_dve, 3)
            with act.Fori(0, TT) as c:
                for q in range(4):
                    act.wait_ge(seg_done, 4 * c + q + 1)
                    for h in range(4):
                        ins = run(decay[:, 4 * q + h, :], bank[q][:, h * P:(h + 1) * P], ACT.Exp,
                                  bias=sp["nacum"][:, bass.ds(c * 16 + 4 * q + h, 1)])
                    ins.then_inc(decayed, 1)
                act.wait_ge(y_done, c + 1)
            for n in range(8):
                act.wait_ge(y_step, 6 * TT)
                run(y_tmp[:, 0:512] if n % 2 else y_tmp[:, 512:1024], z_tok[:, n * 512:(n + 1) * 512], ACT.Square,
                    accum_out=stats[:, 0, n:n + 1]).then_inc(y_sq, 1)
                act.wait_ge(y_sq, n + 1)
            act.wait_ge(y_stat, 1)
            run(stats[:, 2, :], stats[:, 1, :], ACT.Sqrt).then_inc(y_std, 1)
            for m in range(KT):
                act.wait_ge(y_turned, m + 1)
                run(a_hi[:, m, :], bank[4 + m % 2][:, :], ACT.Copy, scale=gains[:, 1, m:m + 1]).then_inc(ssd_hi, 1)
            for m in range(KT):
                prepare("mlp", m, 2, b_hi, lambda: act.wait_ge(dve_evac, EVAC0["wo_ssd"] + m + 1))
            root("mlp", 0)
            for g in range(FF_GROUPS):
                for j in range(KT):
                    n = KT * g + j
                    act.wait_ge(dve_evac, EVAC0[f"ff1_{g}"] + j + 1)
                    if n >= 2:
                        act.wait_ge(ff_lo, n - 1)
                    run(relu2[j % 2], relu[j % 2], ACT.Square).then_inc(ff_sq, 1)
                    if j == 0:
                        act.wait_ge(unit_done, 2 * FIRST[f"ff1_{g}"])
                    run(a_hi[:, j, :], relu[j % 2], ACT.Square).then_inc(ff_hi, 1)
            for m in range(KT):
                prepare("end1", m, 0, None, lambda: act.wait_ge(dve_evac, EVAC0[f"ff2_{FF_GROUPS - 1}"] + m + 1))
            root("end1", 0)
            for m in range(KT):
                if m < 2:
                    act.wait_ge(NORMS["end1"]["stat"], KT)
                prepare("mix2", m, 4, a_hi, lambda: act.wait_ge(NORMS["end1"]["x"], m + 1))
            root("mix2", 1)

            log_exp(1)
            act.wait_ge(NORMS["mix2"]["tok"], 1)
            for half in "ab":
                if half == "a":
                    act.wait_ge(cum_done, 2)
                    run(cum_t, bank[7][0:16, :], ACT.Copy, scale=-1.0).then_inc(cum_act, 1)
                value_evac("v2" + half)
                for h in range(8):
                    act.wait_ge(cum_spread, 8 * (half == "b") + h + 1)
                    run(head_bias[:, h * T:(h + 1) * T], bank[6 + h % 2][:, :], ACT.Copy).then_inc(cum_bias, 1)
                attention("2" + half)
            split_attention("2", 8)

            def sigmoids(phase, k0):
                for j in range(KT):
                    act.wait_ge(dve_evac, EVAC0[phase] + j + 1)
                    run(gate_t[:, j * T:(j + 1) * T] if phase == "gate_a" else merged[:, j * T:(j + 1) * T],
                        gate_t[:, j * T:(j + 1) * T] if phase == "gate_a" else merged[:, j * T:(j + 1) * T],
                        ACT.Sigmoid).then_inc(gated, 1)

            sigmoids("gate_b", 0)
            with act.Fori(0, 2) as i:
                for j in range(4):
                    act.wait_ge(unit_done, 4 * i + 2 * FIRST["zv"] + j + 1)
                    for t in range(2):
                        tt = 2 * (j % 2) + t
                        ins = run(zv_tok[:, bass.ds(i * 512 + tt * D + (j // 2) * STRIP, STRIP)],
                                  bank[j][:, t * STRIP:(t + 1) * STRIP], ACT.Gelu_apprx_tanh, scale=rstd_tok[:, tt:tt + 1])
                    ins.then_inc(act_evac, 1)
            for m in range(KT):
                act.wait_ge(dve_evac, EVAC0["u"] + m + 1)
                run(u_t[:, m * T:(m + 1) * T], lin[m % 2], ACT.Gelu_apprx_tanh).then_inc(ug, 1)
            for t in range(TT):
                act.wait_ge(ln_step, TT + t + 1)
                run(sq_wide, zv_tok[:, t * D:(t + 1) * D], ACT.Square, accum_out=stats[:, 0, 4 + t:5 + t]).then_inc(ln_sq, 1)
                act.wait_ge(ln_sq, t + 1)
            act.wait_ge(ln_step, 2 * TT + 1)
            run(stats[:, 2, 0:4], stats[:, 1, 0:4], ACT.Sqrt).then_inc(ln_std, 1)
            for g in range(KT):
                act.wait_ge(a_ready, g + 1)
                run(b_hi[:, g, :], u_t[:, g * T:(g + 1) * T], ACT.Copy).then_inc(amix_hi, 1)
            sigmoids("gate_a", 8)
            for m in range(KT):
                act.wait_ge(merged_ready, m + 1)
                if m == 0:
                    act.wait_ge(unit_done, 2 * FIRST["branch_a"])
                run(a_hi[:, m, :], merged[:, m * T:(m + 1) * T], ACT.Copy).then_inc(m_hi, 1)
            for m in range(KT):
                prepare("ffn2", m, 5, b_hi, lambda: act.wait_ge(dve_evac, EVAC0["out2"] + m + 1))
            root("ffn2", 1)
            act.dma_start(p_raw, d["p_t"]).then_inc(p_loaded, 16)

            n = 0
            for g in range(3):
                tiles = min(KT, UP_TILES - n)
                for i in range(tiles // 2):
                    for q in range(4):
                        half, tile = q // 2, n + 2 * i + q % 2
                        fill = 2 * n + 4 * i + q
                        act.wait_ge(dve_evac, EVAC0[f"up{g}"] + 4 * i + q + 1)
                        if fill >= 4:
                            act.wait_ge(up_gelu if half == 0 else up_act, tile - 1)
                        w = half * UP_TILES + tile
                        run(up_c[q], up_pad[q][:, 0:T], ACT.Identity, bias=conv2_w[:, w, CONV2:CONV2 + 1],
                            scale=conv2_w[:, w, 0:1]).then_inc(up_tap0, 1)
                        if half == 0:
                            act.wait_ge(up_taps, 2 * fill + 2)
                            if tile >= 2:
                                act.wait_ge(up_act, tile - 1)
                                act.wait_ge(up_lo, tile - 1)
                            run(up_g[q], up_c[q], ACT.Gelu_apprx_tanh).then_inc(up_gelu, 1)
                        else:
                            act.wait_ge(up_act, tile + 1)
                            if i == 0 and q == 2:
                                act.wait_ge(unit_done, 2 * FIRST[f"up{g}"])
                            run(a_hi[:, tile - n, :], up_g[q - 2], ACT.Copy).then_inc(up_hi, 1)
                n += tiles
            act.wait_ge(p_loaded, 16)
            for k in range(2):
                run(p_hi[:, k, :], p_raw[:, k, :], ACT.Copy).then_inc(p_hi_ready, 1)
            for m in range(KT):
                prepare("ple", m, 6, b_hi, lambda: act.wait_ge(dve_evac, EVAC0["down2"] + m + 1))
            root("ple", 1)
            for m in range(KT):
                act.wait_ge(unit_done, 2 * FIRST["ple"] + m // 4 + 1)
                run(ple_t[:, m * T:(m + 1) * T], bank[m % 4][:, :], ACT.Copy).then_inc(act_evac, 1)
            for m in range(KT):
                act.wait_ge(dve_evac, EVAC0["gate"] + m + 1)
                run(sig[m % 2], sig[m % 2], ACT.Sigmoid).then_inc(ple_sig, 1)
                prepare("end2", m, 0, None, lambda: act.wait_ge(ple_mul, 2 * m + 2))
            root("end2", 1)

        @block.vector
        def _(dve):
            v = nc.vector

            def low(norm, m, gain, dst):
                hi, lo = dst
                n = NORMS[norm]
                dve.wait_ge(n["hi"], m + 1)
                v.scalar_tensor_tensor(lo[:, m, :], x[:, m, :], gains[:, gain, m:m + 1], hi[:, m, :].bitcast(F32),
                                       ALU.mult, ALU.subtract).then_inc(n["lo"], 1)

            def inverse_rms(norm, e, tok=False):
                n = NORMS[norm]
                dve.wait_ge(n["stat"], KT)
                v.tensor_scalar(rstd, STAT[:, :], 1.0 / D, e, ALU.mult, ALU.add).then_inc(n["var"], 1)
                dve.wait_ge(n["std"], 1)
                v.reciprocal(rstd, rstd).then_inc(n["rstd"], 1)
                if tok:
                    dve.wait_ge(n["turned"], 1)
                    v.tensor_copy(rstd_tok, bank[5][:, :].rearrange("p (t c) -> p t c", t=TT)[:, :, 0]).then_inc(n["tok"], 1)
                dve.wait_ge(n["rstd"], 1)

            def scaled_evac(phase, j, dst, scale=None):
                dve.wait_ge(unit_done, 2 * FIRST[phase] + j + 1)
                if scale is None:
                    ins = v.tensor_tensor(dst, bank[j % 4][:, :], rstd, ALU.mult)
                else:
                    ins = v.scalar_tensor_tensor(dst, bank[j % 4][:, :], scale, rstd, ALU.mult, ALU.mult)
                ins.then_inc(dve_evac, 1)

            def add_x(phase, j, m, unit=None):
                dve.wait_ge(unit_done, 2 * FIRST[phase] + (j if unit is None else unit) + 1)
                v.tensor_tensor(x[:, m, :], x[:, m, :], bank[j % 4][:, :], ALU.add).then_inc(dve_evac, 1)

            sp_n = [0]

            def sp_do(ins):
                sp_n[0] += 1
                ins.then_inc(sp_step, 1)
                dve.wait_ge(sp_step, sp_n[0])

            def small_logs(k, bias, forget):
                b3 = lambda a: a.unsqueeze(1).to_broadcast([P, TT, 16])
                t3 = lambda a: a.rearrange("p (t h) -> p t h", t=TT)
                dve.wait_ge(small_done, k + 1)
                sp_do(v.tensor_tensor(t3(sp["x"]), t3(bank[6][:, 0:64]), rstd_tok.unsqueeze(2).to_broadcast([P, TT, 16]), ALU.mult))
                sp_do(v.tensor_tensor(t3(sp["x"]), t3(sp["x"]), b3(bias), ALU.add))
                sp_do(v.scalar_tensor_tensor(sp["na"], sp["x"], -1.0, sp["x"], ALU.mult, ALU.min))
                dve.wait_ge(sp_exp, 2 * k + 1)
                sp_do(v.tensor_scalar(sp["d"], sp["e"], 2.0, None, ALU.add))
                sp_do(v.reciprocal(sp["r"], sp["d"]))
                sp_do(v.tensor_tensor(sp["s"], sp["e"], sp["r"], ALU.mult))
                sp_do(v.tensor_tensor(sp["q"], sp["s"], sp["s"], ALU.mult))
                sp_do(v.tensor_scalar(sp["p"], sp["q"], 1.0 / 15, 1.0 / 13, ALU.mult, ALU.add))
                sp_do(v.tensor_tensor(sp["p"], sp["p"], sp["q"], ALU.mult))
                for c in (11, 9, 7, 5, 3):
                    sp_do(v.scalar_tensor_tensor(sp["p"], sp["p"], 1.0 / c, sp["q"], ALU.add, ALU.mult))
                sp_do(v.scalar_tensor_tensor(sp["p"], sp["p"], 1.0, sp["s"], ALU.add, ALU.mult))
                sp_do(v.tensor_scalar(sp["m"], sp["x"], 0.0, None, ALU.min if forget else ALU.max))
                sp_do(v.scalar_tensor_tensor(sp["val"], sp["p"], -2.0 if forget else 2.0, sp["m"], ALU.mult, ALU.add))

            def attention(call, causal):
                def bias(n, q0, it):
                    head, w = n // TT, P * (n % TT + 1)
                    dve.wait_ge(scored, STEPS * q0 + n + 1)
                    if n >= 4:
                        dve.wait_ge(turned, STEPS * q0 + n - 3)
                    off = head * T + (0 if causal else T - w)
                    v.tensor_tensor(score[:, n % 4, 0:w], bank[n % 3][:, 0:w],
                                    head_bias[:, bass.ds(it * (QUAD * T) + off, w)], ALU.add).then_inc(biased, 1)
                    dve.wait_ge(biased, STEPS * q0 + n + 1)
                    v.tensor_reduce(row_max[:, n:n + 1], score[:, n % 4, 0:w], AX_X, ALU.max, negate=True).then_inc(maxed, 1)

                def keep(n, q0, it):
                    head, i = n // TT, n % TT
                    dve.wait_ge(exped, STEPS * q0 + n + 1)
                    v.reciprocal(row_inv[:, n:n + 1], row_sum[:, n:n + 1]).then_inc(inverted, 1)
                    dve.wait_ge(pv_done, STEPS * q0 + n + 1)
                    dve.wait_ge(inverted, STEPS * q0 + n + 1)
                    first = (QUAD0[call] - (0 if call == "1" else 2)) * QUAD * HEAD
                    flat = att_tok.rearrange("p t f -> p (t f)")
                    v.tensor_scalar(flat[:, bass.ds(it * (QUAD * HEAD) + i * D + first + head * HEAD, HEAD)],
                                    bank[6 + n % 2][:, 0:HEAD], row_inv[:, n:n + 1], None, ALU.mult).then_inc(att_out, 1)

                with dve.Fori(0, 2) as it:
                    q0 = QUAD0[call] + it
                    for pair in range(2):
                        v.tensor_copy(q_pair[:, pair, :], qk[:, bass.ds(it * (2 * T) + pair * T, T)]).then_inc(qk_staged, 1)
                        v.tensor_copy(k_pair[:, pair, :], qk[:, bass.ds(it * (2 * T) + (4 + pair) * T, T)]).then_inc(qk_staged, 1)
                    for n in range(STEPS + 3):
                        if n < STEPS:
                            bias(n, q0, it)
                        if n >= 3:
                            keep(n - 3, q0, it)

            def split_attention(blk, tiles):
                for m in range(tiles):
                    n = ATT_T0[blk] + m
                    dve.wait_ge(att_hi, n + 1)
                    v.tensor_tensor(b_lo[:, m, :], bank[4 + m % 2][:, :], b_hi[:, m, :].bitcast(F32), ALU.subtract).then_inc(att_lo, 1)

            for j in range(2):
                dve.wait_ge(w16_hi_ready, j + 1)
                v.tensor_tensor(w16_lo[j], w16_raw[j], w16_hi[j].bitcast(F32), ALU.subtract).then_inc(w16_ready, 1)
            dve.wait_ge(consts_loaded, 16 * N_CONST)
            v.memset(ws_t[HEAD:P, :, 0:HEAD], 0.0).then_inc(ws_masked, 1)
            dve.wait_ge(bias_loaded, 16)
            v.memset(head_bias.rearrange("p (h m) -> p h m", h=H1)[0:HEAD, :, T - HEAD:T], -BIG).then_inc(bias_masked, 1)
            for m in range(KT):
                low("mix1", m, 0, (a_hi, a_lo))
            inverse_rms("mix1", EPS1)
            for j in range(8):
                scaled_evac("qk", j, qk[:, j * T:(j + 1) * T], HEAD ** -0.5 if j < 4 else None)
            n1 = NORMS["mix1"]
            dve.wait_ge(n1["turned"], 1)
            v.tensor_copy(rstd_tok, bank[5][:, :].rearrange("p (t c) -> p t c", t=TT)[:, :, 0]).then_inc(n1["tok"], 1)
            dve.wait_ge(dve_evac, EVAC0["qk"] + 8)
            dve.wait_ge(bias_masked, 1)
            attention("1", causal=False)
            split_attention("1", 4)

            for j in range(2):
                v.memset(u_pad[j][:, 0:CONV1 - 1], 0.0)
            for m in range(NXBC):
                if m >= 2:
                    dve.wait_ge(taps, 3 * m - 3)
                scaled_evac("xbc", m, u_pad[m % 2][:, CONV1 - 1:CONV1 - 1 + T])
                dve.wait_ge(tap0, m + 1)
                for j in range(1, CONV1):
                    if j > 1:
                        dve.wait_ge(taps, 3 * m + j - 1)
                    v.scalar_tensor_tensor(conv[m % 2], u_pad[m % 2][:, j:j + T], conv1_w[:, m, j:j + 1], conv[m % 2],
                                           ALU.mult, ALU.add).then_inc(taps, 1)
            dve.wait_ge(n1["tok"], 1)
            small_logs(0, heads1[:, 0, :], forget=False)
            dve.wait_ge(cum_act, 1)
            t3 = lambda a: a.rearrange("p (t h) -> p t h", t=TT)
            sp_n[0] += 1
            v.scalar_tensor_tensor(t3(sp["a"]), t3(sp["val"]), -1.0, exp_a.unsqueeze(1).to_broadcast([P, TT, 16]),
                                   ALU.mult, ALU.mult).then_inc(sp_step, 1)
            dve.wait_ge(cum_done, 1)
            v.tensor_scalar(sp["nacum"], bank[6][:, 0:64], -1.0, None, ALU.mult).then_inc(cum_dve, 1)
            dve.wait_ge(cum_dve, 1)
            dve.wait_ge(cum_act, 3)
            v.tensor_tensor(sp["diff"], bank[6][:, 64:128], sp["nacum"], ALU.add).then_inc(cum_dve, 1)
            v.tensor_copy(acum_t, bank[7][0:16, :]).then_inc(cum_dve, 1)
            dve.wait_ge(sp_exp, 2)
            h3 = lambda a, g=None: (a if g is None else a[:, g * 512:(g + 1) * 512]).rearrange("p (h f) -> p h f", f=HEAD)
            for g in range(GROUPS):
                v.memset(state[:, g * 512:(g + 1) * 512], 0.0).then_inc(state_ready, 1)
            dve.wait_ge(state_ready, 2)

            def by_head(a, c, h0, n):
                return a[:, bass.ds(c * 16 + h0, n)].unsqueeze(2).to_broadcast([P, n, HEAD])

            with dve.Fori(0, TT) as c:
                bc_flat = bc_t.rearrange("p m t -> p (m t)")
                for g in range(GROUPS):
                    ins = v.tensor_copy(b_c[:, g, :], bc_flat[:, bass.ds(c * P + g * T, P)])
                ins.then_inc(chunk_staged, 1)
                for g in range(GROUPS):
                    ins = v.tensor_copy(c_c[:, g, :], bc_flat[:, bass.ds(c * P + (2 + g) * T, P)])
                ins.then_inc(chunk_staged, 1)
                v.tensor_copy(bt_c, b_tok.rearrange("p t f -> p (t f)")[:, bass.ds(c * 256, 256)]).then_inc(chunk_staged, 1)
                xs_c = xs_tok[:, bass.ds(c * D, D)]
                z_c = z_tok[:, bass.ds(c * D, D)]
                v.tensor_tensor(h3(x_dt), h3(xs_c), by_head(sp["val"], c, 0, 16), ALU.mult).then_inc(x_scaled, 1)
                dve.wait_ge(x_scaled, 2 * c + 1)
                v.tensor_tensor(h3(x_out), h3(x_dt), by_head(sp["dout"], c, 0, 16), ALU.mult).then_inc(x_scaled, 1)
                v.tensor_tensor(h3(x_skip), h3(xs_c), heads1[:, 2, :].unsqueeze(2).to_broadcast([P, 16, HEAD]), ALU.mult).then_inc(y_step, 1)
                dve.wait_ge(cb_done, c + 1)
                for g in range(GROUPS):
                    dve.wait_ge(decayed, 4 * c + 2 * g + 2)
                    v.tensor_tensor(decay[:, 8 * g:8 * g + 8, :], decay[:, 8 * g:8 * g + 8, :],
                                    bank[4][:, g * P:(g + 1) * P].unsqueeze(1).to_broadcast([P, 8, P]), ALU.mult).then_inc(mixed_ready, 1)
                dve.wait_ge(y_done, c + 1)
                for g in range(GROUPS):
                    ins = v.tensor_tensor(h3(y_tmp, g), h3(bank[2 + g][:, :]), by_head(sp["eac"], c, 8 * g, 8), ALU.mult)
                ins.then_inc(y_step, 1)
                dve.wait_ge(y_step, 6 * c + 2)
                for g in range(GROUPS):
                    ins = v.tensor_tensor(y_tmp[:, g * 512:(g + 1) * 512], y_tmp[:, g * 512:(g + 1) * 512], bank[5 + g][:, :], ALU.add)
                ins.then_inc(y_step, 1)
                dve.wait_ge(state_done, c + 1)
                v.tensor_tensor(h3(state), h3(state), by_head(sp["cdec"], c, 0, 16), ALU.mult).then_inc(state_step, 1)
                dve.wait_ge(y_step, 6 * c + 3)
                v.tensor_tensor(y_tmp, y_tmp, x_skip, ALU.add).then_inc(y_step, 1)
                dve.wait_ge(state_step, c + 1)
                for g in range(GROUPS):
                    v.tensor_tensor(state[:, g * 512:(g + 1) * 512], state[:, g * 512:(g + 1) * 512], bank[g][:, :], ALU.add).then_inc(state_ready, 1)
                dve.wait_ge(y_step, 6 * c + 4)
                for g in range(GROUPS):
                    v.tensor_tensor(z_c[:, g * 512:(g + 1) * 512], z_c[:, g * 512:(g + 1) * 512], y_tmp[:, g * 512:(g + 1) * 512], ALU.mult).then_inc(y_step, 1)
                dve.wait_ge(state_ready, 2 * c + 4)
            dve.wait_ge(y_sq, 8)
            v.tensor_scalar(stats[:, 1, :], stats[:, 0, :], 1.0 / 512, EPS1, ALU.mult, ALU.add).then_inc(y_stat, 1)
            dve.wait_ge(y_std, 1)
            v.reciprocal(stats[:, 0, :], stats[:, 2, :]).then_inc(y_stat, 1)
            dve.wait_ge(y_stat, 2)
            for n in range(8):
                v.tensor_scalar(z_tok[:, n * 512:(n + 1) * 512], z_tok[:, n * 512:(n + 1) * 512], stats[:, 0, n:n + 1], None,
                                ALU.mult).then_inc(y_norm, 1)
            for m in range(KT):
                dve.wait_ge(ssd_hi, m + 1)
                v.scalar_tensor_tensor(a_lo[:, m, :], bank[4 + m % 2][:, :], gains[:, 1, m:m + 1], a_hi[:, m, :].bitcast(F32),
                                       ALU.mult, ALU.subtract).then_inc(ssd_lo, 1)
            for j in range(8):
                add_x("wo_att", j, j, unit=j // 2)
            for m in range(KT):
                dve.wait_ge(dve_evac, EVAC0["wo_att"] + m + 1)
                add_x("wo_ssd", m, m)
                low("mlp", m, 2, (b_hi, b_lo))
            inverse_rms("mlp", EPS1)
            for g in range(FF_GROUPS):
                for j in range(KT):
                    n = KT * g + j
                    dve.wait_ge(unit_done, 2 * FIRST[f"ff1_{g}"] + j + 1)
                    if n >= 2:
                        dve.wait_ge(ff_hi, n - 1)
                    v.scalar_tensor_tensor(relu[j % 2], bank[j % 4][:, :], 0.0, rstd, ALU.max, ALU.mult).then_inc(dve_evac, 1)
                    dve.wait_ge(ff_hi, n + 1)
                    v.tensor_tensor(a_lo[:, j, :], relu2[j % 2], a_hi[:, j, :].bitcast(F32), ALU.subtract).then_inc(ff_lo, 1)
                for m in range(KT):
                    before = EVAC0["wo_ssd"] if g == 0 else EVAC0[f"ff2_{g - 1}"]
                    dve.wait_ge(dve_evac, before + m + 1)
                    add_x(f"ff2_{g}", m, m)
            n3 = NORMS["end1"]
            inverse_rms("end1", EPS1)
            for m in range(KT):
                v.scalar_tensor_tensor(x[:, m, :], x[:, m, :], gains[:, 3, m:m + 1], rstd, ALU.mult, ALU.mult).then_inc(n3["x"], 1)
                if m:
                    low("mix2", m - 1, 4, (a_hi, a_lo))
            low("mix2", KT - 1, 4, (a_hi, a_lo))
            inverse_rms("mix2", EPS2, tok=True)

            dve.wait_ge(NORMS["mix2"]["tok"], 1)
            small_logs(1, bf2, forget=True)
            for half in "ab":
                for j in range(8):
                    scaled_evac("qk2" + half, j, qk[:, j * T:(j + 1) * T], HEAD ** -0.5 if j < 4 else None)
                dve.wait_ge(dve_evac, EVAC0["qk2" + half] + 8)
                dve.wait_ge(cum_bias, 8 * (half == "b") + 8)
                attention("2" + half, causal=True)
            split_attention("2", 8)
            for j in range(KT):
                scaled_evac("gate_b", j, merged[:, j * T:(j + 1) * T])
            for j in range(KT):
                dve.wait_ge(unit_done, 2 * FIRST["branch_b"] + j + 1)
                dve.wait_ge(gated, j + 1)
                v.tensor_tensor(merged[:, j * T:(j + 1) * T], merged[:, j * T:(j + 1) * T], bank[j % 4][:, :], ALU.mult).then_inc(dve_evac, 1)
            dve.wait_ge(act_evac, EVAC0["zv"] + FILLS["zv"])
            for t in range(TT):
                v.tensor_reduce(stats[:, 0, t:t + 1], zv_tok[:, t * D:(t + 1) * D], AX_X, ALU.add).then_inc(ln_step, 1)
            for m in range(2):
                if m >= 2:
                    dve.wait_ge(ug, m - 1)
                scaled_evac("u", m, lin[m % 2])
            dve.wait_ge(ln_step, TT)
            v.tensor_scalar(stats[:, 1, 4:8], stats[:, 0, 0:4], 1.0 / D, None, ALU.mult).then_inc(ln_mean, 1)
            dve.wait_ge(ln_mean, 1)
            for t in range(TT):
                v.tensor_scalar(zv_tok[:, t * D:(t + 1) * D], zv_tok[:, t * D:(t + 1) * D], stats[:, 1, 4 + t:5 + t], None,
                                ALU.subtract).then_inc(ln_step, 1)
            for m in range(2, KT):
                dve.wait_ge(ug, m - 1)
                scaled_evac("u", m, lin[m % 2])
            dve.wait_ge(ln_sq, TT)
            v.tensor_scalar(stats[:, 1, 0:4], stats[:, 0, 4:8], 1.0 / D, EPS2, ALU.mult, ALU.add).then_inc(ln_step, 1)
            dve.wait_ge(ln_std, 1)
            v.reciprocal(stats[:, 0, 0:4], stats[:, 2, 0:4]).then_inc(ln_mean, 1)
            dve.wait_ge(ln_mean, 2)
            for t in range(TT):
                zt = zv_tok[:, t * D:(t + 1) * D]
                v.scalar_tensor_tensor(zt, zt, stats[:, 0, t:t + 1], ln_gb[:, 0, :], ALU.mult, ALU.mult).then_inc(ln_mean, 1)
            for t in range(TT):
                zt = zv_tok[:, t * D:(t + 1) * D]
                dve.wait_ge(ln_mean, 3 + t)
                v.tensor_tensor(zt, zt, ln_gb[:, 1, :], ALU.add).then_inc(ln_ready, 1)
            dve.wait_ge(ug, KT)
            t4 = lambda a: a.rearrange("p (t c) -> p t c", t=TT)
            for g in range(KT):
                dve.wait_ge(mixed_done, g + 1)
                v.tensor_tensor(t4(lin2[g % 2]), t4(bank[6 + g % 2][:, :]), bs_bc[:, g, :].unsqueeze(1).to_broadcast([P, TT, P]),
                                ALU.add).then_inc(mix_read, 1)
                dve.wait_ge(mix_read, g + 1)
                ut = u_t[:, g * T:(g + 1) * T]
                v.tensor_tensor(ut, ut, lin2[g % 2], ALU.mult).then_inc(a_ready, 1)
                dve.wait_ge(amix_hi, g + 1)
                v.tensor_tensor(b_lo[:, g, :], ut, b_hi[:, g, :].bitcast(F32), ALU.subtract).then_inc(amix_lo, 1)
            for j in range(KT):
                scaled_evac("gate_a", j, gate_t[:, j * T:(j + 1) * T])
            for j in range(KT):
                gt, mt = gate_t[:, j * T:(j + 1) * T], merged[:, j * T:(j + 1) * T]
                dve.wait_ge(unit_done, 2 * FIRST["branch_a"] + j + 1)
                dve.wait_ge(gated, KT + j + 1)
                v.tensor_tensor(gt, gt, bank[j % 4][:, :], ALU.mult).then_inc(dve_evac, 1)
                dve.wait_ge(dve_evac, EVAC0["branch_a"] + j + 1)
                v.tensor_tensor(mt, mt, gt, ALU.add).then_inc(merged_ready, 1)
                dve.wait_ge(m_hi, j + 1)
                v.tensor_tensor(a_lo[:, j, :], mt, a_hi[:, j, :].bitcast(F32), ALU.subtract).then_inc(m_lo, 1)
            for m in range(KT):
                add_x("out2", m, m)
                low("ffn2", m, 5, (b_hi, b_lo))
            inverse_rms("ffn2", EPS2)
            for q in range(4):
                v.memset(up_pad[q][:, 0:CONV2 - 1], 0.0)
            n = 0
            for g in range(3):
                tiles = min(KT, UP_TILES - n)
                for i in range(tiles // 2):
                    for q in range(4):
                        half, tile = q // 2, n + 2 * i + q % 2
                        fill = 2 * n + 4 * i + q
                        w = half * UP_TILES + tile
                        scaled_evac(f"up{g}", 4 * i + q, up_pad[q][:, CONV2 - 1:CONV2 - 1 + T])
                        dve.wait_ge(up_tap0, fill + 1)
                        for j in range(1, CONV2):
                            if j > 1:
                                dve.wait_ge(up_taps, 2 * fill + j - 1)
                            v.scalar_tensor_tensor(up_c[q], up_pad[q][:, j:j + T], conv2_w[:, w, j:j + 1], up_c[q],
                                                   ALU.mult, ALU.add).then_inc(up_taps, 1)
                        if half == 1:
                            dve.wait_ge(up_gelu, tile + 1)
                            dve.wait_ge(up_taps, 2 * fill + 2)
                            v.tensor_tensor(up_g[q - 2], up_g[q - 2], up_c[q], ALU.mult).then_inc(up_act, 1)
                            dve.wait_ge(up_hi, tile + 1)
                            v.tensor_tensor(a_lo[:, tile - n, :], up_g[q - 2], a_hi[:, tile - n, :].bitcast(F32),
                                            ALU.subtract).then_inc(up_lo, 1)
                n += tiles
                if g == 2:
                    for k in range(2):
                        dve.wait_ge(p_hi_ready, k + 1)
                        v.tensor_tensor(p_lo[:, k, :], p_raw[:, k, :], p_hi[:, k, :].bitcast(F32), ALU.subtract).then_inc(p_lo_ready, 1)
                for m in range(KT):
                    dve.wait_ge(dve_evac, EVAC0["out2" if g == 0 else f"down{g - 1}"] + m + 1)
                    add_x(f"down{g}", m, m)
                    if g == 2:
                        low("ple", m, 6, (b_hi, b_lo))
            inverse_rms("ple", EPS2)
            for m in range(KT):
                s_m = sig[m % 2]
                scaled_evac("gate", m, s_m)
                dve.wait_ge(ple_sig, m + 1)
                dve.wait_ge(act_evac, EVAC0["ple"] + m + 1)
                v.tensor_tensor(s_m, s_m, ple_t[:, m * T:(m + 1) * T], ALU.mult).then_inc(ple_mul, 1)
                dve.wait_ge(ple_mul, 2 * m + 1)
                v.tensor_tensor(x[:, m, :], x[:, m, :], s_m, ALU.add).then_inc(ple_mul, 1)
            dve.wait_ge(ple_mul, 2 * KT)
            inverse_rms("end2", EPS2)
            for m in range(KT):
                v.scalar_tensor_tensor(out_t[m], x[:, m, :], gains[:, 7, m:m + 1], rstd, ALU.mult, ALU.mult).then_inc(out_ready, 1)


def by_k(w):
    kt, n = w.shape[0] // P, w.shape[1] // STRIP
    return w.reshape(kt, P, n, STRIP).transpose(2, 1, 0, 3).reshape(n, P, kt * STRIP)


def kernel(**inputs):
    import concourse.bacc as bacc
    from concourse import mybir as _mybir
    from concourse.bass_utils import run_bass_kernel_spmd

    g = {k: np.asarray(v) for k, v in inputs.items()}
    w_in, w_out, ff1, ff2 = g["w_in"][0], g["w_out"][0], g["w_ff1"][0], g["w_ff2"][0]
    w_in2, up, down = g["w_in_2"][0], g["w_up_2"][0], g["w_down_2"][0]
    strips = [by_k(w_in[:, 0:1024]), by_k(w_in[:, 1024:1536]), by_k(w_in[:, 2560:4096]), by_k(w_in[:, 1536:2560])]
    strips += [w_out[0:512].reshape(4, P, 2, 512).transpose(2, 1, 0, 3).reshape(2, P, SW), by_k(w_out[512:])]
    for j in range(FF_GROUPS):
        strips += [by_k(ff1[:, j * D:(j + 1) * D]), by_k(ff2[j * D:(j + 1) * D])]
    for j in range(2):
        for first in (2048, 3072, 4096):
            strips.append(by_k(w_in2[:, first + j * 512:first + (j + 1) * 512]))
    strips += [by_k(w_in2[:, 6160:7184]), by_k(g["w_branch_b_2"][0]), by_k(w_in2[:, 1024:2048]), by_k(w_in2[:, 0:1024])]
    strips += [by_k(w_in2[:, 5136:6160]), by_k(g["w_branch_a_2"][0]), by_k(g["w_out_2"][0])]
    half = UP_TILES * P
    ups = np.stack([by_k(up[:, 0:half]), by_k(up[:, half:])], axis=1).reshape(-1, P, SW)
    padded = np.concatenate([down, np.zeros((3 * D - half, D), down.dtype)])
    for j in range(3):
        strips += [ups[8 * j:8 * j + 8], by_k(padded[j * D:(j + 1) * D])]
    strips += [g["w_ple_2"][0].reshape(2, P, D).transpose(1, 0, 2).reshape(1, P, SW), by_k(g["w_ple_gate_2"][0])]

    def by_tile(v):
        return v.reshape(-1, P).T

    def sixteen(w):
        return w.reshape(KT, P, 16).transpose(1, 0, 2)

    gains = [g["norm_mix_w"], g["ssd_norm_w"], g["norm_mlp_w"], g["norm_final_w"], g["norm_mix_g_2"], g["norm_ffn_g_2"],
             g["norm_ple_g_2"], g["norm_final_g_2"], g["norm_final_g_2"]]
    taps1 = np.concatenate([g["conv_w"][0], g["conv_b"]])
    taps2 = np.concatenate([g["conv_w_2"][0], g["conv_b_2"]])
    dist = np.clip(T - P + np.arange(P)[:, None] - np.arange(T)[None, :], -REL, REL) + REL
    arrays = {
        "x_t": g["x"][0].T.reshape(KT, P, T).transpose(1, 0, 2),
        "strips": np.concatenate(strips),
        "gains": np.stack([by_tile(v) for v in gains], axis=1),
        "conv1": taps1.reshape(CONV1 + 1, NXBC, P).transpose(2, 1, 0),
        "conv2": taps2.reshape(CONV2 + 1, 2 * UP_TILES, P).transpose(2, 1, 0),
        "dt_bias": g["dt_bias"][0], "a_log": g["a_log"][0], "d_skip": g["d_skip"][0], "b_f": g["b_f_2"][0],
        "w16": np.stack([sixteen(w_in[:, 4096:4112]), sixteen(w_in2[:, 5120:5136])]),
        "ln_g": g["gmlp_ln_g_2"][0], "ln_b": g["gmlp_ln_b_2"][0],
        "ws_t": g["gmlp_w_s_2"][0].transpose(2, 0, 1), "bs": g["gmlp_b_s_2"][0].reshape(-1),
        "rel": g["rel_bias"][0].T[:, dist],
        "p_t": g["p_2"][0, 0].T.reshape(2, P, T).transpose(1, 0, 2),
    }
    nc = bacc.Bacc("TRN2", target_bir_lowering=False, num_devices=1)
    feed, aps = {}, {}
    for name, a in arrays.items():
        feed[f"in_{name}"] = np.ascontiguousarray(a)
        aps[name] = nc.dram_tensor(f"in_{name}", a.shape, _mybir.dt.from_np(a.dtype), kind="ExternalInput").ap()
    out = nc.dram_tensor("out", (KT, P, T), F32, kind="ExternalOutput").ap()
    build(nc, aps, out)
    r = run_bass_kernel_spmd(nc, [feed], core_ids=[0])
    return r.results[0]["out"].reshape(D, T).T.reshape(1, T, D)
```

```python
from contextlib import ExitStack

import numpy as np

import concourse.bass as bass
from concourse import mybir

F32 = mybir.dt.float32
F32R = mybir.dt.float32r
BF16 = mybir.dt.bfloat16
ALU = mybir.AluOpType
ACT = mybir.ActivationFunctionType
AX_X = mybir.AxisListType.X

P = 128
D = 1024
T = 512
KT = D // P
TT = T // P
STRIP = 256
SW = KT * STRIP
EPS1 = 1e-5
EPS2 = 1e-6
HEAD = 64
H1 = 8
H2 = 16
H_SSD = 16
GROUPS = 2
CONV1 = 4
CONV2 = 3
NXBC = 12
D_FF = 4096
FF_GROUPS = D_FF // D
UP_TILES = 2816 // P
BIG = 1e30
QUAD = 4
STEPS = QUAD * TT
REL = 256
SPLIT_ROWS = P
N_GAINS = 10

PHASES = [("xbc", 6), ("qk", 4), ("z", 4), ("v", 2), ("wo_ssd", 4), ("wo_att", 2)]
PHASES += [(f"{w}{g}", 4) for g in range(FF_GROUPS) for w in ("ff1_", "ff2_")]
PHASES += [("qk2a", 4), ("v2a", 2), ("zv", 4), ("u", 4), ("qk2b", 4), ("v2b", 2), ("gate_b", 4), ("gate_a", 4)]
PHASES += [("branch_b", 4), ("branch_a", 4), ("out2", 4)]
PHASES += [("up0", 8), ("down0", 4), ("up1", 8), ("down1", 4), ("up2", 6), ("down2", 4), ("ple", 1), ("gate", 4)]
FIRST = {}
for _name, _n in PHASES:
    FIRST[_name] = sum(n for _, n in PHASES[:len(FIRST)])
N_STRIPS = sum(n for _, n in PHASES)

ON_ACT = {"v", "z", "v2a", "v2b", "zv", "ple"}
FILLS = {name: 2 * n for name, n in PHASES} | {"wo_att": 8, "ple": 8}
WOVEN = {"z", "wo_ssd", "zv", "gate_b"}
BANKS = {name: 2 if name in WOVEN else 4 for name, _ in PHASES}
PIECES = 4 * KT
SLOTS = STEPS + 3
SLOT_PIECES = [5] + [1, 1, 2] * 5 + [2, 2, 3]


def evac_base():
    seen, base = {True: 2, False: 0}, {}
    for name, _ in PHASES:
        on_act = name in ON_ACT
        base[name] = seen[on_act]
        seen[on_act] += FILLS[name]
    return base


EVAC0 = evac_base()
BEFORE = {name: PHASES[n - 1][0] for n, (name, _) in enumerate(PHASES) if n}


def slot_pieces(n):
    return range(sum(SLOT_PIECES[:n]), sum(SLOT_PIECES[:n + 1]))


def slot_units(n):
    return [p // KT for p in slot_pieces(n) if p % KT == KT - 1]


def build(nc, d, out):
    ctx = ExitStack()
    with ctx:
        base = (nc.sbuf_base + 63) // 64 * 64
        place = {}
        cursor = [0]

        def sb(name, shape, dt=F32, at=None):
            size = 2 if dt == BF16 else 4
            cols = -(-int(np.prod(shape[1:])) * size // 32) * 8
            off = cursor[0] if at is None else at
            if at is None:
                cursor[0] += cols
            place[name] = off
            assert base + 4 * (off + cols) <= nc.sbuf_usable_end, (name, off, cols)
            return nc.alloc_sbuf_tensor_at(name, list(shape), dt, offset=base + 4 * off).ap()

        def sem(name):
            return ctx.enter_context(nc.semaphore(name))

        x = sb("x", [P, KT, T])
        a_hi = sb("a_hi", [P, KT, T], F32R)
        a_lo = sb("a_lo", [P, KT, T], F32R)
        b_hi = sb("b_hi", [P, KT, T], F32R)
        b_lo = sb("b_lo", [P, KT, T], F32R)
        w_raw = [sb(f"w_raw{j}", [P, KT, STRIP]) for j in range(2)]
        w_hi = [sb(f"w_hi{j}", [P, KT, STRIP], F32R) for j in range(2)]
        w_lo = [sb(f"w_lo{j}", [P, KT, STRIP], F32R) for j in range(2)]
        ident = sb("ident", [P, P])
        steps01 = sb("steps01", [P, 7 * P])
        tri, ones = steps01[:, 3 * P:4 * P], steps01[:, 4 * P:5 * P]
        ident16 = sb("ident16", [P, P], BF16)
        future16 = sb("future16", [P, P], BF16)
        past16 = sb("past16", [P, P], BF16)
        gains = sb("gains", [P, N_GAINS, KT])
        gain12 = sb("gain12", [P, KT])
        conv1_w = sb("conv1_w", [P, NXBC, CONV1 + 1])
        conv2_w = sb("conv2_w", [P, 2 * UP_TILES, CONV2 + 1])
        heads1 = sb("heads1", [P, 3, H_SSD])
        bf2 = sb("bf2", [P, H2])
        w16 = sb("w16", [P, 2, KT, 48], F32R)
        rstd = sb("rstd", [P, T])
        rstd_tok = sb("rstd_tok", [P, TT])
        exp_a = sb("exp_a", [P, H_SSD])
        row_max = sb("row_max", [P, STEPS])
        row_sum = sb("row_sum", [P, STEPS])
        row_inv = sb("row_inv", [P, STEPS])
        stats = sb("stats", [P, 3, 8])
        wait_note = sb("wait_note", [P, 1])
        sel = sb("sel", [SPLIT_ROWS, 16], F32R)
        sel_quad = sb("sel_quad", [SPLIT_ROWS, QUAD], F32R)
        work = cursor[0]

        B_HI, B_LO = place["b_hi"], place["b_lo"]
        sq = [sb(f"sq{j}", [P, T], at=work + j * T) for j in range(2)]
        sq_sum = sb("sq_sum", [P, T], at=work + 2 * T)
        sq_g = [sb(f"sq_g{j}", [P, T], at=work + 4096 + j * T) for j in range(2)]
        sq_g_sum = sb("sq_g_sum", [P, T], at=work + 4096 + 2 * T)
        rstd1 = sb("rstd1", [P, T], at=work + 4096 + 3 * T)
        ratio = sb("ratio", [P, T], at=work + 4096 + 4 * T)

        qk = sb("qk", [P, 8 * T], at=B_LO)
        head_bias = sb("head_bias", [P, H1 * T], at=B_HI)
        u_pad = [sb(f"u_pad{j}", [P, CONV1 - 1 + T], at=B_HI + 520 * j) for j in range(2)]
        conv = [sb(f"conv{j}", [P, T], at=B_HI + 1040 + T * j) for j in range(2)]
        xs_t = [sb(f"xs_t{j}", [P, T], at=B_HI + 2064 + T * j) for j in range(2)]
        decay = sb("decay", [P, H_SSD, P], at=B_HI)
        x_dt = sb("x_dt", [P, D], at=B_HI + 2048)
        x_out = sb("x_out", [P, D], at=B_HI + 3072)
        xs_tok = sb("xs_tok", [P, TT * D], at=work)
        bc_t = sb("bc_t", [P, 4, T], at=work + 4096)
        b_tok = sb("b_tok", [P, TT, 256], at=work + 6144)
        y_hi = sb("y_hi", [P, KT, T], F32R, at=work)
        y_lo = sb("y_lo", [P, KT, T], F32R, at=work + 4096)
        sp = {n: sb(f"sp_{n}", [P, TT * 16], at=work + 7168 + 64 * j) for j, n in enumerate(
            ("x", "na", "e", "d", "r", "s", "q", "p", "m", "val", "a", "nacum", "diff", "eac", "cdec", "dout"))}
        cum = sb("cum", [SPLIT_ROWS, T], F32R, at=work + 8192)
        small_t = sb("small_t", [48, T], at=work + 8704)
        w16_raw = sb("w16_raw", [P, 2, KT, 16], at=work + 16640)
        z_tok = sb("z_tok", [P, TT * D], at=work + 8704)
        state = sb("state", [P, D], at=work + 12800)
        y_tmp = sb("y_tmp", [P, D], at=work + 13824)
        x_skip = sb("x_skip", [P, D], at=work + 14848)
        b_c = sb("b_c", [P, 2, P], at=work + 15872)
        c_c = sb("c_c", [P, 2, P], at=work + 16128)
        bt_c = sb("bt_c", [P, 256], at=work + 16384)
        unused = [sb(f"unused{j}", [P, 512], at=work + 14848 + 512 * j) for j in range(4)]
        att_tok1 = sb("att_tok1", [P, TT * 512], at=work + 8704)
        pair1 = [sb(f"{n}_pair1", [P, 2, T], at=work + 10752 + 1024 * j) for j, n in enumerate("qk")]
        att_tok2 = sb("att_tok2", [P, TT * D], at=work + 8704)
        pair2 = [sb(f"{n}_pair2", [P, 2, T], at=B_HI + 1024 * j) for j, n in enumerate("qk")]
        v_tok = sb("v_tok", [P, TT * 8 * HEAD], at=work + 12800)
        score = sb("score", [P, 3, T], at=work + 14848)
        prob_t = sb("prob_t", [P, 2, T], at=work + 16384)
        relu = [sb(f"relu{j}", [P, T], at=work + 2048 + T * j) for j in range(2)]
        relu2 = [sb(f"relu2_{j}", [P, T], at=work + 3072 + T * j) for j in range(2)]
        ws_t = sb("ws_t", [P, KT, P], at=B_HI + 2048)
        shift = sb("shift", [P, KT, P], at=B_HI + 3072)
        u_t = sb("u_t", [P, KT * T], at=work)
        zv_tok = sb("zv_tok", [P, TT * D], at=work + 4096)
        merged = sb("merged", [P, KT * T], at=work + 4096)
        sq_wide = [sb(f"sq_wide{j}", [P, D], at=work + 14848 + D * j) for j in range(2)]
        lin = [sb(f"lin{j}", [P, T], at=work + 14848 + T * j) for j in range(2)]
        gate_t = sb("gate_t", [P, KT * T], at=work + 12800)
        up_pad = [sb(f"up_pad{j}", [P, CONV2 - 1 + T], at=work + 2048 + 520 * j) for j in range(4)]
        up_c = [sb(f"up_c{j}", [P, T], at=work + 4608 + T * j) for j in range(4)]
        up_g = [sb(f"up_g{j}", [P, T], at=work + 6656 + T * j) for j in range(2)]
        ple_t = sb("ple_t", [P, KT * T], at=work + 8192)
        p_raw = sb("p_raw", [P, 2, T], at=work + 12288)
        p_hi = sb("p_hi", [P, 2, T], F32R, at=work + 13312)
        p_lo = sb("p_lo", [P, 2, T], F32R, at=work + 14336)
        sig = [sb(f"sig{j}", [P, T], at=work + 2048 + T * j) for j in range(2)]
        out_t = [sb(f"out_t{j}", [P, T], at=work + 3072 + T * j) for j in range(8)]

        bank = [ctx.enter_context(nc.psum_tensor(f"bank{j}", [P, T], F32)) for j in range(8)]
        STAT = [bank[4], bank[5]]

        x_loaded = [sem(f"x_loaded{j}") for j in range(4)]
        gains_loaded = sem("gains_loaded")
        consts_loaded = sem("consts_loaded")
        late_loaded = sem("late_loaded")
        raw_loaded = [sem(f"raw_loaded{j}") for j in range(2)]
        half_loaded = sem("half_loaded")
        masks_ready = sem("masks_ready")
        mask_step = sem("mask_step")
        hi_split = sem("hi_split")
        strip_split = sem("strip_split")
        unit_done = sem("unit_done")
        act_evac = sem("act_evac")
        dve_evac = sem("dve_evac")

        def norm_sems(n):
            keys = ["sq", "sum", "stat", "var", "std", "rstd"]
            keys += ["hi", "lo"] if not n.startswith("end") else []
            keys += ["turned", "tok"] if n.startswith("mix") else []
            keys += ["var2"] if n == "mix2" else []
            return {k: sem(f"{n}_{k}") for k in keys}

        NORMS = {n: norm_sems(n) for n in ("mix1", "mlp", "end1", "mix2", "ffn2", "ple", "end2")}
        small_ready = sem("small_ready")
        x_normed = sem("x_normed")
        w16_hi_ready = sem("w16_hi_ready")
        w16_ready = sem("w16_ready")
        key_masked = sem("key_masked")
        qk_staged = sem("qk_staged")
        sel_staged = sem("sel_staged")
        scored = sem("scored")
        biased = sem("biased")
        maxed = sem("maxed")
        exped = sem("exped")
        turned = sem("turned")
        prob_ready = sem("prob_ready")
        pv_done = sem("pv_done")
        inverted = sem("inverted")
        att_out = sem("att_out")
        att_turned = sem("att_turned")
        att_hi = sem("att_hi")
        att_lo = sem("att_lo")
        small_done = sem("small_done")
        sp_step = sem("sp_step")
        sp_exp = sem("sp_exp")
        cum_done = sem("cum_done")
        cum_act = sem("cum_act")
        cum_dve = sem("cum_dve")
        cum_ready = sem("cum_ready")
        tap0 = sem("tap0")
        taps = sem("taps")
        conv_silu = sem("conv_silu")
        xs_turned = sem("xs_turned")
        xs_ready = sem("xs_ready")
        chunk_staged = sem("chunk_staged")
        x_scaled = sem("x_scaled")
        seg_done = sem("seg_done")
        cb_done = sem("cb_done")
        decayed = sem("decayed")
        mixed_ready = sem("mixed_ready")
        y_done = sem("y_done")
        state_done = sem("state_done")
        y_step = sem("y_step")
        state_ready = sem("state_ready")
        state_step = sem("state_step")
        z_silu = sem("z_silu")
        y_gated = sem("y_gated")
        y_sq = sem("y_sq")
        y_std = sem("y_std")
        y_stat = sem("y_stat")
        y_norm = sem("y_norm")
        y_turned = sem("y_turned")
        ssd_hi = sem("ssd_hi")
        ssd_lo = sem("ssd_lo")
        ff_sq = sem("ff_sq")
        ff_hi = sem("ff_hi")
        ff_lo = sem("ff_lo")
        gated = sem("gated")
        merged_ready = sem("merged_ready")
        m_hi = sem("m_hi")
        m_lo = sem("m_lo")
        ug = sem("ug")
        row_sums = sem("row_sums")
        shift_ready = sem("shift_ready")
        zv_gelu = sem("zv_gelu")
        ln_step = sem("ln_step")
        ln_sq = sem("ln_sq")
        ln_std = sem("ln_std")
        ln_ready = sem("ln_ready")
        mixed_done = sem("mixed_done")
        mix_read = sem("mix_read")
        a_ready = sem("a_ready")
        amix_hi = sem("amix_hi")
        amix_lo = sem("amix_lo")
        up_tap0 = sem("up_tap0")
        up_taps = sem("up_taps")
        up_gelu = sem("up_gelu")
        up_act = sem("up_act")
        up_hi = sem("up_hi")
        up_lo = sem("up_lo")
        p_hi_ready = sem("p_hi_ready")
        p_lo_ready = sem("p_lo_ready")
        ple_sig = sem("ple_sig")
        ple_mul = sem("ple_mul")
        out_ready = sem("out_ready")
        stored = sem("stored")

        QUAD0 = {"1": 0, "2a": 2, "2b": 4}
        ATT_T0 = {"1": 0, "2": 4}
        N_CONST = 8
        SP_LOG = 17
        SP_A = SP_LOG + 1
        SP_END = SP_A + SP_LOG

        block = ctx.enter_context(nc.Block())

        def evac_sem(phase):
            return act_evac if phase in ON_ACT else dve_evac

        @block.sync
        def _(sp_eng):
            for h in range(2):
                sp_eng.dma_start(w_raw[0].rearrange("p k n -> p (k n)")[:, h * (SW // 2):(h + 1) * (SW // 2)],
                                 d["strips"][0][:, h * (SW // 2):(h + 1) * (SW // 2)]).then_inc(raw_loaded[0] if h == 0 else half_loaded, 16)
            sp_eng.wait_ge(x_loaded[3], 16)
            sp_eng.dma_start(w_raw[1].rearrange("p k n -> p (k n)"), d["strips"][1]).then_inc(raw_loaded[1], 16)
            with sp_eng.Fori(1, N_STRIPS // 2) as i:
                for j in range(2):
                    sp_eng.wait_ge(strip_split, 2 * i + j - 1)
                    sp_eng.dma_start(w_raw[j].rearrange("p k n -> p (k n)"),
                                     d["strips"][bass.ds(2 * i + j, 1)].rearrange("a p n -> (a p) n")).then_inc(raw_loaded[j], 16)
            sp_eng.wait_ge(strip_split, N_STRIPS - 2)
            sp_eng.dma_start(w_raw[0].rearrange("p k n -> p (k n)"), d["strips"][N_STRIPS - 1]).then_inc(raw_loaded[0], 16)
            for m in range(KT):
                sp_eng.wait_ge(out_ready, m + 1)
                sp_eng.dma_start(out[m], out_t[m]).then_inc(stored, 16)
            sp_eng.wait_ge(stored, 16 * KT)

        @block.gpsimd
        def _(pool):
            def split_strip(j, loads, strip, first):
                pool.wait_ge(raw_loaded[j], 16 * loads)
                if not first:
                    pool.wait_ge(unit_done, 2 * strip - 2)
                pool.tensor_tensor(wait_note, ident[:, 0:1], ident[:, 0:1], ALU.mult)
                pool.tensor_scalar(w_hi[j], w_raw[j], 1.0, 1.0, ALU.mult, ALU.mult).then_inc(hi_split, 1)
                pool.wait_ge(hi_split, strip)
                pool.tensor_tensor(w_lo[j], w_raw[j], w_hi[j].bitcast(F32), ALU.subtract).then_inc(strip_split, 1)

            for part, value in ((ident, 0.0), (steps01[:, 0:3 * P], 0.0), (steps01[:, 3 * P:7 * P], 1.0), (ident16, 0.0),
                                (future16, 0.0), (past16, 0.0)):
                pool.memset(part, value).then_inc(mask_step, 1)
            pool.wait_ge(mask_step, 6)
            for m in (ident, ident16):
                pool.affine_select(out=m, in_=m, compare_op=ALU.not_equal, fill=1.0, base=0,
                                   pattern=[[-1, P]], channel_multiplier=1).then_inc(masks_ready, 1)
            pool.affine_select(out=tri, in_=tri, compare_op=ALU.is_ge, fill=0.0, base=0,
                               pattern=[[1, P]], channel_multiplier=-1).then_inc(masks_ready, 1)
            pool.affine_select(out=future16, in_=future16, compare_op=ALU.is_ge, fill=-BIG, base=0,
                               pattern=[[-1, P]], channel_multiplier=1).then_inc(masks_ready, 1)
            pool.affine_select(out=past16, in_=past16, compare_op=ALU.is_ge, fill=-BIG, base=0,
                               pattern=[[1, P]], channel_multiplier=-1).then_inc(masks_ready, 1)
            pool.wait_ge(masks_ready, 5)
            for h in range(2):
                half = slice(h * (KT // 2), (h + 1) * (KT // 2))
                pool.wait_ge(raw_loaded[0] if h == 0 else half_loaded, 16)
                pool.tensor_scalar(w_hi[0][:, half], w_raw[0][:, half], 1.0, 1.0, ALU.mult, ALU.mult).then_inc(mask_step, 1)
                pool.wait_ge(mask_step, 7 + 2 * h)
                pool.tensor_tensor(w_lo[0][:, half], w_raw[0][:, half], w_hi[0][:, half].bitcast(F32),
                                   ALU.subtract).then_inc(mask_step if h == 0 else strip_split, 1)
            split_strip(1, 1, 1, True)
            with pool.Fori(1, N_STRIPS // 2) as i:
                for j in range(2):
                    split_strip(j, i + 1, 2 * i + j, False)
            split_strip(0, N_STRIPS // 2 + 1, N_STRIPS - 1, False)

        @block.tensor
        def _(pe):
            mm, tr = nc.tensor.matmul, nc.tensor.transpose

            def bank_free(phase, j, fills=0):
                n = BANKS[phase]
                if j >= n:
                    pe.wait_ge(evac_sem(phase), EVAC0[phase] + fills + j - n + 1)
                elif phase in BEFORE:
                    before = BEFORE[phase]
                    last = FILLS[before] - BANKS[before] + min(j, BANKS[before] - 1)
                    pe.wait_ge(evac_sem(before), EVAC0[before] + fills + last + 1)

            def feature_k(ps, slot, u, act, k, kt=KT):
                cols, (hi, lo) = slice(u * P, u * P + P), act
                mm(ps[:, :], w_hi[slot][:, k, cols], hi[:, k, :], start=(k == 0), stop=False)
                mm(ps[:, :], w_hi[slot][:, k, cols], lo[:, k, :], start=False, stop=False)
                return mm(ps[:, :], w_lo[slot][:, k, cols], hi[:, k, :], start=False, stop=(k == kt - 1))

            def token_k(ps, slot, u, act, k, kt=KT):
                t, (hi, lo) = k // 4, act
                dst = ps[:, t * STRIP:(t + 1) * STRIP]
                tok = slice((2 * u + t) * P, (2 * u + t + 1) * P)
                for q in (2 * k % KT, 2 * k % KT + 1):
                    mm(dst, hi[:, q, tok], w_hi[slot][:, q, :], start=(q == 0), stop=False)
                    mm(dst, hi[:, q, tok], w_lo[slot][:, q, :], start=False, stop=False)
                    last = mm(dst, lo[:, q, tok], w_hi[slot][:, q, :], start=False, stop=(q == KT - 1))
                return last

            def stream(phase, part, act, ready=None, after=None, strips=0, fills=0, kt=KT):
                for s in range(FILLS[phase] // 2):
                    slot = (FIRST[phase] + s) % 2
                    if FIRST[phase] + s:
                        pe.wait_ge(strip_split, FIRST[phase] + s + 1 + strips)
                    else:
                        pe.wait_ge(mask_step, 8)
                    pair = s == 0 and ready is not None
                    if pair:
                        for u in range(2):
                            bank_free(phase, u, fills)
                        for k in range(kt):
                            if FIRST[phase] == 0 and k == KT // 2:
                                pe.wait_ge(strip_split, 1)
                            ready(k)
                            for u in range(2):
                                last = part(bank[u], slot, u, act, k, kt)
                                if k == kt - 1:
                                    last.then_inc(unit_done, 1)
                    for u in range(2):
                        j = 2 * s + u
                        if not pair:
                            bank_free(phase, j, fills)
                            for k in range(kt):
                                last = part(bank[j % BANKS[phase]], slot, u, act, k, kt)
                            last.then_inc(unit_done, 1)
                        if after is not None:
                            after(j)

            def piece(phase, part, act, p, it, ready=None):
                j, k = p // KT, p % KT
                if k == 0:
                    if j % 2 == 0:
                        pe.wait_ge(strip_split, FIRST[phase] + 2 * it + j // 2 + 1)
                    pe.wait_ge(evac_sem(phase), EVAC0[phase] + 4 * it + j - 1)
                if j == 0 and ready is not None:
                    ready(k)
                last = part(bank[j % 2], j // 2, j % 2, act, k)
                if k == KT - 1:
                    last.then_inc(unit_done, 1)

            def woven_start(phase):
                for j in range(2):
                    bank_free(phase, j)

            def stat(norm, total, where):
                pe.wait_ge(NORMS[norm]["sum"], KT)
                mm(where[:, :], ones, total, start=True, stop=True).then_inc(NORMS[norm]["stat"], 1)

            def turn_rstd(norm):
                n = NORMS[norm]
                pe.wait_ge(n["rstd"], 1)
                for t in range(TT):
                    last = tr(bank[7][:, t * P:(t + 1) * P], rstd[:, t * P:(t + 1) * P], ident)
                last.then_inc(n["turned"], 1)

            def wait_tiles(s):
                return lambda k: pe.wait_ge(s, k + 1)

            def small_columns(which, act):
                pe.wait_ge(w16_ready, 2 + which)
                for k in range(KT):
                    for part in act:
                        last = mm(bank[6][0:48, :], w16[:, which, k, :], part[:, k, :], start=(k == 0 and part is act[0]),
                                  stop=(k == KT - 1 and part is act[1]))
                last.then_inc(small_done, 1)

            def turn_small(which, norm):
                pe.wait_ge(NORMS[norm]["tok"], 1)
                pe.wait_ge(small_ready, 4)
                pe.wait_ge(sp_exp, 3 * which + 1)
                for t in range(TT):
                    last = mm(bank[7][:, t * 16:(t + 1) * 16], small_t[:, t * P:(t + 1) * P], sel.bitcast(F32)[0:48, :],
                              start=True, stop=True)
                last.then_inc(small_done, 1)

            def attention(call, phase, part, act, ready=None):
                causal = call != "1"
                v_phase = {"1": "v", "2a": "v2a", "2b": "v2b"}[call]
                pe.wait_ge(act_evac, EVAC0[v_phase] + FILLS[v_phase])
                woven_start(phase)
                q_pair, k_pair = pair2 if causal else pair1

                def scores(n, q0):
                    head, i = n // TT, n % TT
                    rows, w = slice(HEAD * (head % 2), HEAD * (head % 2) + HEAD), P * (i + 1)
                    if n % (2 * TT) == 0:
                        pe.wait_ge(qk_staged, 4 * q0 + 2 * (head // 2) + 2)
                    if n == 0 and causal:
                        pe.wait_ge(sel_staged, q0 - 1)
                    if n >= 2:
                        pe.wait_ge(exped if causal else biased, STEPS * q0 + n - 1)
                    ps = bank[2 + n % 2]
                    q_rows, k_rows = q_pair[rows, head // 2, i * P:(i + 1) * P], k_pair[rows, head // 2, 0:w]
                    if not causal:
                        mm(ps[:, 0:w], q_rows, k_rows, start=True, stop=True).then_inc(scored, 1)
                        return
                    pick = sel_quad[:, head:head + 1].to_broadcast([SPLIT_ROWS, P])
                    for cols in ([slice(0, w - P)] if i else []) + [slice(w - P, w)]:
                        own = cols.stop == w
                        mm(ps[:, cols], q_rows, k_rows[:, cols], start=True, stop=False)
                        last = mm(ps[:, cols], pick, cum[:, cols], start=False, stop=not own)
                    last = mm(ps[:, w - P:w], ident16, future16, start=False, stop=True)
                    last.then_inc(scored, 1)

                def turn(n, q0):
                    i = n % TT
                    pe.wait_ge(exped, STEPS * q0 + n + 1)
                    if n == 0 and not causal:
                        pe.wait_ge(ssd_lo, KT)
                    if n >= 2:
                        pe.wait_ge(prob_ready, STEPS * q0 + n - 1)
                    for j in range(i + 1):
                        last = tr(bank[4 + n % 2][:, j * P:(j + 1) * P], score[:, n % 3, j * P:(j + 1) * P], ident)
                    last.then_inc(turned, 1)

                def values(n, q0, it):
                    head, i = n // TT, n % TT
                    pe.wait_ge(prob_ready, STEPS * q0 + n + 1)
                    if n >= 2:
                        pe.wait_ge(att_out, STEPS * q0 + n - 1)
                    for j in range(i + 1):
                        last = mm(bank[6 + n % 2][:, 0:HEAD], prob_t[:, n % 2, j * P:(j + 1) * P],
                                  v_tok[:, bass.ds(j * 8 * HEAD + head * HEAD + it * (QUAD * HEAD), HEAD)],
                                  start=(j == 0), stop=(j == i))
                    last.then_inc(pv_done, 1)

                with pe.Fori(0, 2) as it:
                    q0 = QUAD0[call] + it
                    for n in range(SLOTS):
                        if n < STEPS and n:
                            scores(n, q0)
                        if n < SLOTS - 1:
                            for p in slot_pieces(n):
                                piece(phase, part, act, p, it, ready)
                        if n == 0:
                            scores(n, q0)
                        if 2 <= n < STEPS + 2:
                            turn(n - 2, q0)
                        if n >= 3:
                            values(n - 3, q0, it)
                    for p in slot_pieces(SLOTS - 1):
                        piece(phase, part, act, p, it, ready)
                    pe.wait_ge(att_out, STEPS * q0 + STEPS)

            def turn_attention(blk, m):
                n = ATT_T0[blk] + m
                if m >= 2:
                    pe.wait_ge(att_lo, n - 1)
                src, width = (att_tok1, 512) if blk == "1" else (att_tok2, D)
                for t in range(TT):
                    last = tr(bank[4 + m % 2][:, t * P:(t + 1) * P], src[:, t * width + m * P:t * width + (m + 1) * P], ident)
                last.then_inc(att_turned, 1)

            A, B, Y = (a_hi, a_lo), (b_hi, b_lo), (y_hi, y_lo)
            pe.wait_ge(masks_ready, 5)

            def turn_xs(m):
                pe.wait_ge(conv_silu, m + 1)
                if m >= 2:
                    pe.wait_ge(xs_ready, m - 1)
                else:
                    pe.wait_ge(NORMS["mix1"]["var"], 1)
                src = xs_t[m % 2] if m < 8 else bc_t[:, m - 8, :]
                for t in range(TT):
                    last = tr(bank[4 + m % 2][:, t * P:(t + 1) * P], src[:, t * P:(t + 1) * P], ident)
                last.then_inc(xs_turned, 1)

            def after_xbc(j):
                if j == 1:
                    stat("mix1", sq_sum, STAT[0])
                if j == 3:
                    turn_rstd("mix1")
                if j >= 3:
                    turn_xs(j - 3)

            stream("xbc", feature_k, A, ready=wait_tiles(NORMS["mix1"]["lo"]), after=after_xbc)
            small_columns(0, A)
            turn_xs(9)

            def after_qk(j):
                if j == 0:
                    turn_small(0, "mix1")
                if j != 5:
                    return
                pe.wait_ge(sp_step, SP_A)
                mm(bank[6][:, 0:64], tri, sp["a"], start=True, stop=True)
                mm(bank[6][:, 64:128], ones, sp["a"], start=True, stop=True)
                for c in range(TT):
                    last = mm(bank[7][0:16, c * P:(c + 1) * P], sp["a"][:, c * 16:(c + 1) * 16], tri, start=True, stop=True)
                last.then_inc(cum_done, 1)

            stream("qk", feature_k, A, after=after_qk)

            woven_start("z")
            pe.wait_ge(cum_ready, 2)
            pe.wait_ge(small_ready, 4)
            with pe.Fori(0, TT // 2) as it:
                def fill(first, last):
                    for p in range(first, last):
                        piece("z", token_k, A, p, it)

                for half in range(2):
                    c, p0 = 2 * it + half, half * (PIECES // 2)

                    def seg(q):
                        for h in range(4):
                            part = bank[2 + q % 2][:, h * P:(h + 1) * P]
                            mm(part, ident16, past16, start=True, stop=False)
                            last = mm(part, sel[:, 4 * q + h:4 * q + h + 1].to_broadcast([SPLIT_ROWS, P]),
                                      cum[:, bass.ds(c * P, P)], start=False, stop=True)
                        last.then_inc(seg_done, 1)

                    fill(p0, p0 + 2)
                    pe.wait_ge(chunk_staged, 3 * c + 3)
                    for g in range(GROUPS):
                        last = mm(bank[4][:, g * P:(g + 1) * P], b_c[:, g, :], c_c[:, g, :], start=True, stop=True)
                    last.then_inc(cb_done, 1)
                    seg(0)
                    seg(1)
                    fill(p0 + 2, p0 + 5)
                    for q in (2, 3):
                        pe.wait_ge(decayed, 4 * c + q - 1)
                        seg(q)
                    fill(p0 + 5, p0 + 9)
                    for g in range(GROUPS):
                        pe.wait_ge(mixed_ready, 2 * c + g + 1)
                        for h in range(8):
                            last = mm(bank[5 + g][:, h * HEAD:(h + 1) * HEAD], decay[:, 8 * g + h, :],
                                      x_dt[:, (8 * g + h) * HEAD:(8 * g + h + 1) * HEAD], start=True, stop=True)
                        if g == 0:
                            fill(p0 + 9, p0 + 11)
                    pe.wait_ge(state_ready, 2 * c + 2)
                    for g in range(GROUPS):
                        last = mm(bank[2 + g][:, :], c_c[:, g, :], state[:, g * 512:(g + 1) * 512], start=True, stop=True)
                    last.then_inc(y_done, 1)
                    for g in range(GROUPS):
                        last = mm(bank[4 + 3 * g][:, :], bt_c[:, g * P:(g + 1) * P], x_out[:, g * 512:(g + 1) * 512],
                                  start=True, stop=True)
                    last.then_inc(state_done, 1)
                    fill(p0 + 11, p0 + 16)
                    pe.wait_ge(state_ready, 2 * c + 4)
                    pe.wait_ge(y_step, 4 * c + 3)

            stream("v", token_k, A)
            for m in range(KT):
                if m == 0:
                    pe.wait_ge(y_norm, 8)
                if m >= 2:
                    pe.wait_ge(ssd_lo, m - 1)
                for t in range(TT):
                    last = tr(bank[4 + m % 2][:, t * P:(t + 1) * P], z_tok[:, t * D + m * P:t * D + (m + 1) * P], ident)
                last.then_inc(y_turned, 1)

            attention("1", "wo_ssd", feature_k, Y, ready=wait_tiles(ssd_lo))
            for m in range(4):
                turn_attention("1", m)

            for s in range(2):
                pe.wait_ge(strip_split, FIRST["wo_att"] + s + 1)
                hi4 = w_hi[s].rearrange("p k n -> p (k n)").rearrange("p (k n) -> p k n", k=4)
                lo4 = w_lo[s].rearrange("p k n -> p (k n)").rearrange("p (k n) -> p k n", k=4)
                for j in range(4):
                    bank_free("wo_att", 4 * s + j)
                    cols = slice(j * P, (j + 1) * P)
                    for k in range(4):
                        if s == 0 and j == 0:
                            pe.wait_ge(att_lo, k + 1)
                        mm(bank[j][:, :], hi4[:, k, cols], b_hi[:, k, :], start=(k == 0), stop=False)
                        mm(bank[j][:, :], hi4[:, k, cols], b_lo[:, k, :], start=False, stop=False)
                        last = mm(bank[j][:, :], lo4[:, k, cols], b_hi[:, k, :], start=False, stop=(k == 3))
                    if j % 2:
                        last.then_inc(unit_done, 1)

            def ff_group(g, norm):
                stream("ff1_0", feature_k, A, ready=wait_tiles(NORMS["mlp"]["lo"]), strips=8 * g, fills=16 * g,
                       after=(lambda j: stat("mlp", sq_sum, STAT[0]) if j == 0 else None) if norm else None)
                stream("ff2_0", feature_k, B, ready=lambda k: pe.wait_ge(ff_lo, KT * g + k + 1), strips=8 * g, fills=16 * g)

            ff_group(0, True)
            with pe.Fori(1, FF_GROUPS) as g:
                ff_group(g, False)

            def after_qk2a(j):
                if j == 0:
                    stat("end1", sq_sum, STAT[0])
                    stat("mix2", sq_g_sum, STAT[1])
                if j == 2:
                    turn_rstd("mix2")
                    small_columns(1, A)
                if j == 3:
                    turn_small(1, "mix2")
                if j == 6:
                    pe.wait_ge(sp_step, SP_END)
                    for t in range(TT):
                        last = mm(bank[7][0:16, :], sp["val"][:, t * 16:(t + 1) * 16],
                                  steps01[:, (3 - t) * P:(3 - t) * P + T], start=(t == 0), stop=(t == TT - 1))
                    last.then_inc(cum_done, 1)

            stream("qk2a", feature_k, A, ready=wait_tiles(NORMS["mix2"]["lo"]), after=after_qk2a)
            stream("v2a", token_k, A)
            pe.wait_ge(cum_ready, 4)
            attention("2a", "zv", token_k, A)

            def after_u(j):
                if j == 0:
                    pe.wait_ge(key_masked, 2)
                    for h in range(2):
                        last = mm(bank[4 + h][:, :], ones, ws_t[:, 4 * h:4 * h + 4, :].rearrange("p g t -> p (g t)"),
                                  start=True, stop=True)
                    last.then_inc(row_sums, 1)

            stream("u", feature_k, A, after=after_u)

            def spatial(g):
                if g == 0:
                    pe.wait_ge(ln_ready, TT)
                if g >= 2:
                    pe.wait_ge(mix_read, g - 1)
                for t in range(TT):
                    last = mm(bank[6 + g % 2][:, t * P:(t + 1) * P], zv_tok[:, t * D + g * P:t * D + (g + 1) * P],
                              ws_t[:, g, :], start=True, stop=True)
                last.then_inc(mixed_done, 1)

            stream("qk2b", feature_k, A, after=spatial)
            stream("v2b", token_k, A)
            pe.wait_ge(mix_read, KT)
            attention("2b", "gate_b", feature_k, A)
            stream("gate_a", feature_k, A, after=lambda j: turn_attention("2", j))
            stream("branch_b", feature_k, B, ready=lambda k: pe.wait_ge(att_lo, 4 + k + 1))
            stream("branch_a", feature_k, A, ready=wait_tiles(amix_lo))
            stream("out2", feature_k, B, ready=wait_tiles(m_lo))

            def up_group(g, norm):
                stream("up0", feature_k, A, ready=wait_tiles(NORMS["ffn2"]["lo"]), strips=12 * g, fills=24 * g,
                       after=(lambda j: stat("ffn2", sq_sum, STAT[0]) if j == 0 else None) if norm else None)
                stream("down0", feature_k, B, ready=lambda k: pe.wait_ge(up_lo, KT * g + k + 1), strips=12 * g, fills=24 * g)

            up_group(0, True)
            with pe.Fori(1, UP_TILES // KT) as g:
                up_group(g, False)
            stream("up2", feature_k, A)
            stream("down2", feature_k, B, ready=lambda k: pe.wait_ge(up_lo, 2 * KT + k + 1), kt=UP_TILES % KT)

            pe.wait_ge(strip_split, FIRST["ple"] + 1)
            pe.wait_ge(p_lo_ready, 2)
            slot = FIRST["ple"] % 2
            hi2 = w_hi[slot].rearrange("p k n -> p (k n)").rearrange("p (k n) -> p k n", k=2)
            lo2 = w_lo[slot].rearrange("p k n -> p (k n)").rearrange("p (k n) -> p k n", k=2)
            for m in range(KT):
                bank_free("ple", m)
                cols = slice(m * P, (m + 1) * P)
                for k in range(2):
                    mm(bank[m % 4][:, :], hi2[:, k, cols], p_hi[:, k, :], start=(k == 0), stop=False)
                    mm(bank[m % 4][:, :], hi2[:, k, cols], p_lo[:, k, :], start=False, stop=False)
                    last = mm(bank[m % 4][:, :], lo2[:, k, cols], p_hi[:, k, :], start=False, stop=(k == 1))
                if m % 4 == 3:
                    last.then_inc(unit_done, 1)
            stream("gate", feature_k, A, ready=wait_tiles(NORMS["ple"]["lo"]),
                   after=lambda j: stat("ple", sq_sum, STAT[0]) if j == 0 else None)
            stat("end2", sq_sum, STAT[1])

        @block.scalar
        def _(act):
            run = nc.scalar.activation
            act.dma_start(gains, d["gains"]).then_inc(gains_loaded, 16)
            for j in range(4):
                act.dma_start(x[:, 2 * j:2 * j + 2, :], d["x_t"][:, 2 * j:2 * j + 2, :]).then_inc(x_loaded[j], 16)
            act.dma_start(conv1_w, d["conv1"]).then_inc(consts_loaded, 16)
            act.dma_start(conv2_w, d["conv2"]).then_inc(consts_loaded, 16)
            act.dma_start(heads1[:, 0, :], d["dt_bias"].partition_broadcast(P)).then_inc(consts_loaded, 16)
            act.dma_start(heads1[:, 1, :], d["a_log"].partition_broadcast(P)).then_inc(consts_loaded, 16)
            act.dma_start(heads1[:, 2, :], d["d_skip"].partition_broadcast(P)).then_inc(consts_loaded, 16)
            act.dma_start(bf2, d["b_f"].partition_broadcast(P)).then_inc(consts_loaded, 16)
            for j in range(2):
                act.dma_start(w16_raw[:, j], d["w16"][j]).then_inc(consts_loaded, 16)

            def square(norm, m, total=sq_sum, parts=sq, scale=1.0):
                n = NORMS[norm]
                if m >= 3:
                    act.wait_ge(n["sum"], m - 1)
                run(parts[m % 2] if m else total, x[:, m, :], ACT.Square, scale=scale).then_inc(n["sq"], 1)

            def high(norm, m, gain, dst):
                run(dst[:, m, :], x[:, m, :], ACT.Copy, scale=gain[:, m:m + 1]).then_inc(NORMS[norm]["hi"], 1)

            def root(norm, where):
                n = NORMS[norm]
                act.wait_ge(n["var"], 1)
                run(where, where, ACT.Sqrt).then_inc(n["std"], 1)

            def attention(call, evac):
                causal = call != "1"

                def exps(n, q0):
                    w = P * (n % TT + 1)
                    act.wait_ge(maxed, STEPS * q0 + n + 1)
                    src = bank[2 + n % 2][:, 0:w] if causal else score[:, n % 3, 0:w]
                    run(score[:, n % 3, 0:w], src, ACT.Exp, bias=row_max[:, n:n + 1],
                        accum_out=row_sum[:, n:n + 1]).then_inc(exped, 1)

                def keep(n, q0):
                    w = P * (n % TT + 1)
                    act.wait_ge(turned, STEPS * q0 + n + 1)
                    if n >= 2:
                        act.wait_ge(pv_done, STEPS * q0 + n - 1)
                    run(prob_t[:, n % 2, 0:w], bank[4 + n % 2][:, 0:w], ACT.Copy).then_inc(prob_ready, 1)

                with act.Fori(0, 2) as it:
                    q0 = QUAD0[call] + it
                    for n in range(SLOTS):
                        if n < STEPS:
                            exps(n, q0)
                        if 2 <= n < STEPS + 2:
                            keep(n - 2, q0)
                        if evac is not None:
                            for j in slot_units(n):
                                evac(j, it)
                    act.wait_ge(att_out, STEPS * q0 + STEPS)

            def split_attention(blk, m):
                act.wait_ge(att_turned, ATT_T0[blk] + m + 1)
                run(b_hi[:, m, :], bank[4 + m % 2][:, :], ACT.Copy).then_inc(att_hi, 1)

            def token_evac(phase, j, ps, dst, width, it=None):
                act.wait_ge(unit_done, 2 * FIRST[phase] + j + 1 if it is None else 4 * it + 2 * FIRST[phase] + j + 1)
                for t in range(2):
                    tt = 2 * (j % 2) + t
                    at = tt * width + (j // 2) * STRIP
                    ins = run(dst[:, at:at + STRIP] if it is None else dst[:, bass.ds(it * 512 + at, STRIP)],
                              ps[:, t * STRIP:(t + 1) * STRIP], ACT.Copy, scale=rstd_tok[:, tt:tt + 1])
                ins.then_inc(act_evac, 1)

            def value_evac(phase):
                for j in range(FILLS[phase]):
                    token_evac(phase, j, bank[j % 4], v_tok, 512)

            act.wait_ge(gains_loaded, 16)
            run(exp_a[:, 0:1], gains[:, 0, 0:1], ACT.Copy).then_inc(act_evac, 2)
            for m in range(KT):
                act.wait_ge(x_loaded[m // 2], 16)
                high("mix1", m, gains[:, 0, :], a_hi)
            for m in range(KT):
                square("mix1", m)
            root("mix1", rstd)
            act.wait_ge(consts_loaded, 16 * N_CONST)
            for j in range(2):
                if j == 0:
                    act.wait_ge(w16_ready, 1)
                run(w16[:, j, :, 0:16], w16_raw[:, j], ACT.Copy).then_inc(w16_hi_ready, 1)
            run(exp_a, heads1[:, 1, :], ACT.Exp).then_inc(cum_act, 1)

            def keep_xs(m):
                act.wait_ge(xs_turned, m + 1)
                src = bank[4 + m % 2][:, :].rearrange("p (t f) -> p t f", t=TT)
                if m < 8:
                    dst = xs_tok.rearrange("p (t f) -> p t f", t=TT)[:, :, m * P:(m + 1) * P]
                else:
                    dst = b_tok[:, :, (m - 8) * P:(m - 7) * P]
                run(dst, src, ACT.Copy).then_inc(xs_ready, 1)

            for m in range(NXBC):
                act.wait_ge(dve_evac, EVAC0["xbc"] + m + 1)
                if m >= 2:
                    act.wait_ge(conv_silu, m - 1)
                run(conv[m % 2], u_pad[m % 2][:, 0:T], ACT.Identity, bias=conv1_w[:, m, CONV1:CONV1 + 1],
                    scale=conv1_w[:, m, 0:1]).then_inc(tap0, 1)
                act.wait_ge(taps, 3 * m + 3)
                if 2 <= m < 8:
                    act.wait_ge(xs_turned, m - 1)
                run(xs_t[m % 2] if m < 8 else bc_t[:, m - 8, :], conv[m % 2], ACT.Silu).then_inc(conv_silu, 1)
                if m >= 3:
                    keep_xs(m - 3)
            keep_xs(9)

            def log_exp(k):
                act.wait_ge(small_done, 2 * k + 1)
                run(small_t, bank[6][0:48, :], ACT.Copy).then_inc(sp_exp, 1)
                act.wait_ge(sp_step, SP_A * k + 3)
                run(sp["e"], sp["na"], ACT.Exp).then_inc(sp_exp, 1)

            log_exp(0)
            act.wait_ge(cum_dve, 2)
            run(sp["eac"], bank[6][:, 0:64], ACT.Exp).then_inc(cum_act, 1)
            run(sp["cdec"], bank[6][:, 64:128], ACT.Exp).then_inc(cum_act, 1)
            act.wait_ge(cum_dve, 3)
            run(sp["dout"], sp["diff"], ACT.Exp).then_inc(sp_exp, 1)

            with act.Fori(0, TT // 2) as it:
                for half in range(2):
                    c = 2 * it + half
                    for q in range(4):
                        act.wait_ge(seg_done, 4 * c + q + 1)
                        for h in range(4):
                            ins = run(decay[:, 4 * q + h, :], bank[2 + q % 2][:, h * P:(h + 1) * P], ACT.Exp,
                                      bias=sp["nacum"][:, bass.ds(c * 16 + 4 * q + h, 1)])
                        ins.then_inc(decayed, 1)
                    token_evac("z", 2 * half, bank[0], z_tok, D, it)
                    act.wait_ge(y_done, c + 1)
                    token_evac("z", 2 * half + 1, bank[1], z_tok, D, it)
            act.wait_ge(y_step, 4 * TT)
            act.dma_start(head_bias.rearrange("p (h m) -> p h m", h=H1), d["rel"].rearrange("h p m -> p h m")).then_inc(late_loaded, 16)
            act.wait_ge(act_evac, EVAC0["z"] + FILLS["z"])
            for t in range(TT):
                run(z_tok[:, t * D:(t + 1) * D], z_tok[:, t * D:(t + 1) * D], ACT.Silu).then_inc(z_silu, 1)

            def group_squares(t):
                act.wait_ge(y_gated, t + 1)
                for n in (2 * t, 2 * t + 1):
                    if n >= 4:
                        act.wait_ge(y_sq, n - 3)
                    run(unused[n % 4], z_tok[:, n * 512:(n + 1) * 512], ACT.Square,
                        accum_out=stats[:, 0, n:n + 1]).then_inc(y_sq, 1)

            group_squares(0)
            group_squares(1)
            token_evac("v", 0, bank[0], v_tok, 512)
            group_squares(2)
            group_squares(3)
            act.wait_ge(y_stat, 1)
            run(stats[:, 2, :], stats[:, 1, :], ACT.Sqrt).then_inc(y_std, 1)
            for j in range(1, 4):
                token_evac("v", j, bank[j], v_tok, 512)
            for m in range(KT):
                act.wait_ge(y_turned, m + 1)
                run(y_hi[:, m, :], bank[4 + m % 2][:, :], ACT.Copy, scale=gains[:, 1, m:m + 1]).then_inc(ssd_hi, 1)
            attention("1", None)
            for m in range(4):
                split_attention("1", m)

            for m in range(KT):
                act.wait_ge(dve_evac, EVAC0["wo_att"] + m + 1)
                high("mlp", m, gains[:, 2, :], a_hi)
                square("mlp", m)
            root("mlp", rstd)

            def ff_group(g):
                for j in range(KT):
                    act.wait_ge(dve_evac, EVAC0["ff1_0"] + 16 * g + j + 1)
                    if j >= 2:
                        act.wait_ge(ff_lo, KT * g + j - 1)
                    run(relu2[j % 2], relu[j % 2], ACT.Square).then_inc(ff_sq, 1)
                    if j == 0:
                        act.wait_ge(unit_done, 2 * FIRST["ff1_0"] + 16 * g)
                    run(b_hi[:, j, :], relu[j % 2], ACT.Square).then_inc(ff_hi, 1)
                act.wait_ge(ff_lo, KT * g + KT)

            with act.Fori(0, FF_GROUPS) as g:
                ff_group(g)
            act.wait_ge(small_ready, 1)
            for m in range(KT):
                act.wait_ge(dve_evac, EVAC0[f"ff2_{FF_GROUPS - 1}"] + m + 1)
                high("mix2", m, gain12, a_hi)
                square("end1", m)
                square("mix2", m, sq_g_sum, sq_g, gains[:, 3, m:m + 1])
            act.wait_ge(unit_done, 2 * FIRST["qk2a"])
            act.dma_start(ws_t, d["ws_t"]).then_inc(late_loaded, 16)
            act.dma_start(shift.rearrange("p g t -> p (g t)"), d["bs"].partition_broadcast(P)).then_inc(late_loaded, 16)
            root("end1", rstd1)
            root("mix2", rstd)
            log_exp(1)

            value_evac("v2a")
            attention("2a", lambda j, it: token_evac("zv", j, bank[j % 2], zv_tok, D, it))
            act.wait_ge(act_evac, EVAC0["zv"] + FILLS["zv"])
            for t in range(TT):
                zt = zv_tok[:, t * D:(t + 1) * D]
                run(zt, zt, ACT.Gelu_apprx_tanh, accum_out=stats[:, 0, t:t + 1]).then_inc(zv_gelu, 1)
            act.wait_ge(ln_step, 1)
            for t in range(TT):
                if t >= 2:
                    act.wait_ge(ln_sq, t - 1)
                run(sq_wide[t % 2], zv_tok[:, t * D:(t + 1) * D], ACT.Square, bias=stats[:, 1, t:t + 1],
                    accum_out=stats[:, 0, 4 + t:5 + t]).then_inc(ln_sq, 1)
            act.wait_ge(ln_step, 2)
            run(stats[:, 2, 0:4], stats[:, 1, 4:8], ACT.Sqrt).then_inc(ln_std, 1)
            for m in range(KT):
                act.wait_ge(dve_evac, EVAC0["u"] + m + 1)
                ut = u_t[:, m * T:(m + 1) * T]
                run(ut, ut, ACT.Gelu_apprx_tanh).then_inc(ug, 1)
            value_evac("v2b")
            attention("2b", None)

            def sigmoids(phase, where):
                for j in range(KT):
                    act.wait_ge(dve_evac, EVAC0[phase] + j + 1)
                    part = where[:, j * T:(j + 1) * T]
                    run(part, part, ACT.Sigmoid).then_inc(gated, 1)

            sigmoids("gate_b", merged)
            for m in range(KT):
                split_attention("2", m)
            sigmoids("gate_a", gate_t)
            for g in range(KT):
                act.wait_ge(a_ready, g + 1)
                if g == 0:
                    act.wait_ge(unit_done, 2 * FIRST["branch_b"])
                run(a_hi[:, g, :], u_t[:, g * T:(g + 1) * T], ACT.Copy).then_inc(amix_hi, 1)
            for m in range(KT):
                act.wait_ge(merged_ready, m + 1)
                if m == 0:
                    act.wait_ge(unit_done, 2 * FIRST["branch_a"])
                run(b_hi[:, m, :], merged[:, m * T:(m + 1) * T], ACT.Copy).then_inc(m_hi, 1)
            for m in range(KT):
                act.wait_ge(dve_evac, EVAC0["out2"] + m + 1)
                high("ffn2", m, gains[:, 5, :], a_hi)
                square("ffn2", m)
            root("ffn2", rstd)
            act.dma_start(p_raw, d["p_t"]).then_inc(late_loaded, 16)

            def up_group(g, tiles):
                for i in range(tiles // 2):
                    for q in range(4):
                        half, tile = q // 2, 2 * i + q % 2
                        fill = 4 * i + q
                        act.wait_ge(dve_evac, EVAC0["up0"] + 24 * g + fill + 1)
                        if i:
                            act.wait_ge(up_gelu if half == 0 else up_act, KT * g + tile - 1)
                        at = KT * g + half * UP_TILES + tile
                        flat = conv2_w.rearrange("p w c -> p (w c)")
                        run(up_c[q], up_pad[q][:, 0:T], ACT.Identity, bias=flat[:, bass.ds(at * (CONV2 + 1) + CONV2, 1)],
                            scale=flat[:, bass.ds(at * (CONV2 + 1), 1)]).then_inc(up_tap0, 1)
                        if half == 0:
                            act.wait_ge(up_taps, 2 * (2 * KT * g + fill) + 2)
                            if i:
                                act.wait_ge(up_lo, KT * g + tile - 1)
                            run(up_g[q], up_c[q], ACT.Gelu_apprx_tanh).then_inc(up_gelu, 1)
                        else:
                            act.wait_ge(up_act, KT * g + tile + 1)
                            if i == 0 and q == 2:
                                act.wait_ge(unit_done, 2 * FIRST["up0"] + 24 * g)
                            run(b_hi[:, tile, :], up_g[q - 2], ACT.Copy).then_inc(up_hi, 1)
                act.wait_ge(up_lo, KT * g + tiles)

            with act.Fori(0, UP_TILES // KT) as g:
                up_group(g, KT)
            up_group(UP_TILES // KT, UP_TILES % KT)
            act.wait_ge(late_loaded, 64)
            for k in range(2):
                run(p_hi[:, k, :], p_raw[:, k, :], ACT.Copy).then_inc(p_hi_ready, 1)
            for m in range(KT):
                act.wait_ge(dve_evac, EVAC0["down2"] + m + 1)
                high("ple", m, gains[:, 6, :], a_hi)
                square("ple", m)
            for m in range(KT):
                act.wait_ge(unit_done, 2 * FIRST["ple"] + m // 4 + 1)
                run(ple_t[:, m * T:(m + 1) * T], bank[m % 4][:, :], ACT.Copy).then_inc(act_evac, 1)
            root("ple", rstd)
            for m in range(KT):
                act.wait_ge(dve_evac, EVAC0["gate"] + m + 1)
                run(sig[m % 2], sig[m % 2], ACT.Sigmoid).then_inc(ple_sig, 1)
                if m:
                    act.wait_ge(ple_mul, 2 * m)
                    square("end2", m - 1)
            act.wait_ge(ple_mul, 2 * KT)
            square("end2", KT - 1)
            root("end2", rstd)

        @block.vector
        def _(dve):
            v = nc.vector

            def add_square(norm, m, total=sq_sum, parts=sq):
                n = NORMS[norm]
                dve.wait_ge(n["sq"], m + 1)
                if m == 0:
                    v.tensor_copy(total[:, 0:1], total[:, 0:1]).then_inc(n["sum"], 1)
                else:
                    dve.wait_ge(n["sum"], m)
                    v.tensor_tensor(total, total, parts[m % 2], ALU.add).then_inc(n["sum"], 1)

            def low(norm, m, gain, dst):
                hi, lo = dst
                n = NORMS[norm]
                dve.wait_ge(n["hi"], m + 1)
                v.scalar_tensor_tensor(lo[:, m, :], x[:, m, :], gain[:, m:m + 1], hi[:, m, :].bitcast(F32),
                                       ALU.mult, ALU.subtract).then_inc(n["lo"], 1)

            def inverse_rms(norm, e, where=STAT[0], to=rstd):
                n = NORMS[norm]
                dve.wait_ge(n["stat"], 1)
                v.tensor_scalar(to, where[:, :], 1.0 / D, e, ALU.mult, ALU.add).then_inc(n["var"], 1)
                dve.wait_ge(n["std"], 1)
                v.reciprocal(to, to).then_inc(n["rstd"], 1)
                dve.wait_ge(n["rstd"], 1)

            def rstd_by_token(norm):
                n = NORMS[norm]
                dve.wait_ge(n["turned"], 1)
                v.tensor_copy(rstd_tok, bank[7][:, :].rearrange("p (t c) -> p t c", t=TT)[:, :, 0]).then_inc(n["tok"], 1)
                dve.wait_ge(n["tok"], 1)

            def scaled_evac(phase, j, dst, scale=None, ps=None, rounds=0):
                dve.wait_ge(unit_done, 2 * FIRST[phase] + j + 1 + rounds)
                src = (bank[j % 4] if ps is None else ps)[:, :]
                if scale is None:
                    ins = v.tensor_tensor(dst, src, rstd, ALU.mult)
                else:
                    ins = v.scalar_tensor_tensor(dst, src, scale, rstd, ALU.mult, ALU.mult)
                ins.then_inc(dve_evac, 1)

            def add_x(phase, j, m, unit=None, rounds=0):
                dve.wait_ge(unit_done, 2 * FIRST[phase] + (j if unit is None else unit) + 1 + rounds)
                v.tensor_tensor(x[:, m, :], x[:, m, :], bank[j % 4][:, :], ALU.add).then_inc(dve_evac, 1)

            sp_n = [0]

            def sp_do(ins):
                sp_n[0] += 1
                ins.then_inc(sp_step, 1)
                dve.wait_ge(sp_step, sp_n[0])

            def small_logs(k, bias, forget):
                b3 = lambda a: a.unsqueeze(1).to_broadcast([P, TT, 16])
                t3 = lambda a: a.rearrange("p (t h) -> p t h", t=TT)
                dve.wait_ge(small_done, 2 * k + 2)
                sp_do(v.tensor_tensor(t3(sp["x"]), t3(bank[7][:, 0:64]), rstd_tok.unsqueeze(2).to_broadcast([P, TT, 16]), ALU.mult))
                sp_do(v.tensor_tensor(t3(sp["x"]), t3(sp["x"]), b3(bias), ALU.add))
                sp_do(v.scalar_tensor_tensor(sp["na"], sp["x"], -1.0, sp["x"], ALU.mult, ALU.min))
                dve.wait_ge(sp_exp, 3 * k + 2)
                sp_do(v.tensor_scalar(sp["d"], sp["e"], 2.0, None, ALU.add))
                sp_do(v.reciprocal(sp["r"], sp["d"]))
                sp_do(v.tensor_tensor(sp["s"], sp["e"], sp["r"], ALU.mult))
                sp_do(v.tensor_tensor(sp["q"], sp["s"], sp["s"], ALU.mult))
                sp_do(v.tensor_scalar(sp["p"], sp["q"], 1.0 / 15, 1.0 / 13, ALU.mult, ALU.add))
                sp_do(v.tensor_tensor(sp["p"], sp["p"], sp["q"], ALU.mult))
                for c in (11, 9, 7, 5, 3):
                    sp_do(v.scalar_tensor_tensor(sp["p"], sp["p"], 1.0 / c, sp["q"], ALU.add, ALU.mult))
                sp_do(v.scalar_tensor_tensor(sp["p"], sp["p"], 1.0, sp["s"], ALU.add, ALU.mult))
                sp_do(v.tensor_scalar(sp["m"], sp["x"], 0.0, None, ALU.min if forget else ALU.max))
                sp_do(v.scalar_tensor_tensor(sp["val"], sp["p"], -2.0 if forget else 2.0, sp["m"], ALU.mult, ALU.add))

            def split_cum(k, sign):
                v.tensor_scalar(cum[0:16, :], bank[7][0:16, :], sign, None, ALU.mult).then_inc(cum_ready, 1)
                dve.wait_ge(cum_ready, 2 * k + 1)
                v.scalar_tensor_tensor(cum[32:48, :], bank[7][0:16, :], sign, cum[0:16, :].bitcast(F32),
                                       ALU.mult, ALU.subtract).then_inc(cum_ready, 1)

            def attention(call, evac):
                causal = call != "1"
                q_pair, k_pair = pair2 if causal else pair1
                att_tok, width = (att_tok2, D) if causal else (att_tok1, 512)

                def most(n, q0, it):
                    head, w = n // TT, P * (n % TT + 1)
                    dve.wait_ge(scored, STEPS * q0 + n + 1)
                    src = bank[2 + n % 2][:, 0:w]
                    if not causal:
                        if n >= 3:
                            dve.wait_ge(turned, STEPS * q0 + n - 2)
                        dst = score[:, n % 3, 0:w]
                        v.tensor_tensor(dst, src, head_bias[:, bass.ds(it * (QUAD * T) + head * T + T - w, w)],
                                        ALU.add).then_inc(biased, 1)
                        dve.wait_ge(biased, STEPS * q0 + n + 1)
                        src = dst
                    v.tensor_reduce(row_max[:, n:n + 1], src, AX_X, ALU.max, negate=True).then_inc(maxed, 1)

                def keep(n, q0, it):
                    head, i = n // TT, n % TT
                    dve.wait_ge(exped, STEPS * q0 + n + 1)
                    v.reciprocal(row_inv[:, n:n + 1], row_sum[:, n:n + 1]).then_inc(inverted, 1)
                    dve.wait_ge(pv_done, STEPS * q0 + n + 1)
                    dve.wait_ge(inverted, STEPS * q0 + n + 1)
                    first = 8 * HEAD if call == "2b" else 0
                    v.tensor_scalar(att_tok[:, bass.ds(it * (QUAD * HEAD) + i * width + first + head * HEAD, HEAD)],
                                    bank[6 + n % 2][:, 0:HEAD], row_inv[:, n:n + 1], None, ALU.mult).then_inc(att_out, 1)

                with dve.Fori(0, 2) as it:
                    q0 = QUAD0[call] + it
                    for pair in range(2):
                        v.tensor_copy(q_pair[:, pair, :], qk[:, bass.ds(it * (2 * T) + pair * T, T)]).then_inc(qk_staged, 1)
                        v.tensor_copy(k_pair[:, pair, :], qk[:, bass.ds(it * (2 * T) + (4 + pair) * T, T)]).then_inc(qk_staged, 1)
                        if causal and pair == 0:
                            first = 8 if call == "2b" else 0
                            v.tensor_copy(sel_quad, sel.bitcast(F32)[:, bass.ds(it * QUAD + first, QUAD)]).then_inc(sel_staged, 1)
                    for n in range(SLOTS):
                        if n < STEPS:
                            most(n, q0, it)
                        if n >= 3:
                            keep(n - 3, q0, it)
                        if evac is not None:
                            for j in slot_units(n):
                                evac(j, it)

            def split_attention(blk, m):
                n = ATT_T0[blk] + m
                dve.wait_ge(att_hi, n + 1)
                v.tensor_tensor(b_lo[:, m, :], bank[4 + m % 2][:, :], b_hi[:, m, :].bitcast(F32), ALU.subtract).then_inc(att_lo, 1)

            for m in range(KT):
                low("mix1", m, gains[:, 0, :], (a_hi, a_lo))
            for m in range(KT):
                add_square("mix1", m)
            inverse_rms("mix1", EPS1)
            v.memset(w16.bitcast(F32), 0.0).then_inc(w16_ready, 1)
            v.tensor_tensor(gain12, gains[:, 3, :], gains[:, 4, :], ALU.mult).then_inc(small_ready, 1)
            dve.wait_ge(masks_ready, 5)
            v.memset(sel.bitcast(F32), 0.0).then_inc(small_ready, 1)
            dve.wait_ge(small_ready, 2)
            for j in range(2):
                v.tensor_copy(sel[32 * j:32 * j + 16, :], ident[0:16, 0:16]).then_inc(small_ready, 1)

            for j in range(2):
                v.memset(u_pad[j][:, 0:CONV1 - 1], 0.0)
            for m in range(NXBC):
                if m >= 2:
                    dve.wait_ge(taps, 3 * m - 3)
                scaled_evac("xbc", m, u_pad[m % 2][:, CONV1 - 1:CONV1 - 1 + T])
                dve.wait_ge(tap0, m + 1)
                for j in range(1, CONV1):
                    if j > 1:
                        dve.wait_ge(taps, 3 * m + j - 1)
                    v.scalar_tensor_tensor(conv[m % 2], u_pad[m % 2][:, j:j + T], conv1_w[:, m, j:j + 1], conv[m % 2],
                                           ALU.mult, ALU.add).then_inc(taps, 1)
                if m == 3:
                    rstd_by_token("mix1")
                if m == 5:
                    for j in range(2):
                        dve.wait_ge(w16_hi_ready, j + 1)
                        v.tensor_tensor(w16[:, j, :, 32:48], w16_raw[:, j], w16[:, j, :, 0:16].bitcast(F32),
                                        ALU.subtract).then_inc(w16_ready, 1)

            def qk_evac(phase, first, last):
                for j in range(first, last):
                    scaled_evac(phase, j, qk[:, j * T:(j + 1) * T], HEAD ** -0.5 if j < 4 else None)

            qk_evac("qk", 0, 2)
            v.memset(cum.bitcast(F32), 0.0).then_inc(cum_dve, 1)
            small_logs(0, heads1[:, 0, :], forget=False)
            dve.wait_ge(cum_act, 1)
            t3 = lambda a: a.rearrange("p (t h) -> p t h", t=TT)
            sp_n[0] += 1
            v.scalar_tensor_tensor(t3(sp["a"]), t3(sp["val"]), -1.0, exp_a.unsqueeze(1).to_broadcast([P, TT, 16]),
                                   ALU.mult, ALU.mult).then_inc(sp_step, 1)
            qk_evac("qk", 2, 6)
            dve.wait_ge(cum_done, 1)
            v.tensor_scalar(sp["nacum"], bank[6][:, 0:64], -1.0, None, ALU.mult).then_inc(cum_dve, 1)
            split_cum(0, 1.0)
            dve.wait_ge(cum_dve, 2)
            dve.wait_ge(cum_act, 3)
            v.tensor_tensor(sp["diff"], bank[6][:, 64:128], sp["nacum"], ALU.add).then_inc(cum_dve, 1)
            qk_evac("qk", 6, 8)
            dve.wait_ge(sp_exp, 3)

            h3 = lambda a, g=None: (a if g is None else a[:, g * 512:(g + 1) * 512]).rearrange("p (h f) -> p h f", f=HEAD)
            for g in range(GROUPS):
                v.memset(state[:, g * 512:(g + 1) * 512], 0.0).then_inc(state_ready, 1)
            dve.wait_ge(state_ready, 2)
            dve.wait_ge(xs_ready, 10)
            dve.wait_ge(conv_silu, NXBC)

            def by_head(a, c, h0, n):
                return a[:, bass.ds(c * 16 + h0, n)].unsqueeze(2).to_broadcast([P, n, HEAD])

            with dve.Fori(0, TT) as c:
                bc_flat = bc_t.rearrange("p m t -> p (m t)")
                for g in range(GROUPS):
                    ins = v.tensor_copy(b_c[:, g, :], bc_flat[:, bass.ds(c * P + g * T, P)])
                ins.then_inc(chunk_staged, 1)
                for g in range(GROUPS):
                    ins = v.tensor_copy(c_c[:, g, :], bc_flat[:, bass.ds(c * P + (2 + g) * T, P)])
                ins.then_inc(chunk_staged, 1)
                v.tensor_copy(bt_c, b_tok.rearrange("p t f -> p (t f)")[:, bass.ds(c * 256, 256)]).then_inc(chunk_staged, 1)
                xs_c = xs_tok[:, bass.ds(c * D, D)]
                v.tensor_tensor(h3(x_dt), h3(xs_c), by_head(sp["val"], c, 0, 16), ALU.mult).then_inc(x_scaled, 1)
                dve.wait_ge(x_scaled, 2 * c + 1)
                v.tensor_tensor(h3(x_out), h3(x_dt), by_head(sp["dout"], c, 0, 16), ALU.mult).then_inc(x_scaled, 1)
                v.tensor_tensor(h3(x_skip), h3(xs_c), heads1[:, 2, :].unsqueeze(2).to_broadcast([P, 16, HEAD]), ALU.mult).then_inc(y_step, 1)
                dve.wait_ge(cb_done, c + 1)
                for g in range(GROUPS):
                    dve.wait_ge(decayed, 4 * c + 2 * g + 2)
                    v.tensor_tensor(decay[:, 8 * g:8 * g + 8, :], decay[:, 8 * g:8 * g + 8, :],
                                    bank[4][:, g * P:(g + 1) * P].unsqueeze(1).to_broadcast([P, 8, P]), ALU.mult).then_inc(mixed_ready, 1)
                dve.wait_ge(y_done, c + 1)
                for g in range(GROUPS):
                    ins = v.tensor_tensor(h3(y_tmp, g), h3(bank[2 + g][:, :]), by_head(sp["eac"], c, 8 * g, 8), ALU.mult)
                ins.then_inc(y_step, 1)
                dve.wait_ge(y_step, 4 * c + 2)
                for g in range(GROUPS):
                    ins = v.tensor_tensor(y_tmp[:, g * 512:(g + 1) * 512], y_tmp[:, g * 512:(g + 1) * 512], bank[5 + g][:, :], ALU.add)
                ins.then_inc(y_step, 1)
                dve.wait_ge(state_done, c + 1)
                v.tensor_tensor(h3(state), h3(state), by_head(sp["cdec"], c, 0, 16), ALU.mult).then_inc(state_step, 1)
                dve.wait_ge(state_step, c + 1)
                for g in range(GROUPS):
                    v.tensor_tensor(state[:, g * 512:(g + 1) * 512], state[:, g * 512:(g + 1) * 512], bank[4 + 3 * g][:, :],
                                    ALU.add).then_inc(state_ready, 1)
                dve.wait_ge(y_step, 4 * c + 3)
                v.tensor_tensor(xs_c, y_tmp, x_skip, ALU.add).then_inc(y_step, 1)
                dve.wait_ge(state_ready, 2 * c + 4)
            dve.wait_ge(y_step, 4 * TT)
            for t in range(TT):
                zt = z_tok[:, t * D:(t + 1) * D]
                dve.wait_ge(z_silu, t + 1)
                v.tensor_tensor(zt, zt, xs_tok[:, t * D:(t + 1) * D], ALU.mult).then_inc(y_gated, 1)
            dve.wait_ge(y_sq, 8)
            v.tensor_scalar(stats[:, 1, :], stats[:, 0, :], 1.0 / 512, EPS1, ALU.mult, ALU.add).then_inc(y_stat, 1)
            dve.wait_ge(y_std, 1)
            v.reciprocal(stats[:, 0, :], stats[:, 2, :]).then_inc(y_stat, 1)
            dve.wait_ge(y_stat, 2)
            dve.wait_ge(y_gated, TT)
            for n in range(8):
                v.tensor_scalar(z_tok[:, n * 512:(n + 1) * 512], z_tok[:, n * 512:(n + 1) * 512], stats[:, 0, n:n + 1], None,
                                ALU.mult).then_inc(y_norm, 1)
            dve.wait_ge(late_loaded, 16)
            v.memset(head_bias.rearrange("p (h m) -> p h m", h=H1)[0:HEAD, :, T - HEAD:T], -BIG).then_inc(key_masked, 1)
            for m in range(KT):
                dve.wait_ge(ssd_hi, m + 1)
                v.scalar_tensor_tensor(y_lo[:, m, :], bank[4 + m % 2][:, :], gains[:, 1, m:m + 1], y_hi[:, m, :].bitcast(F32),
                                       ALU.mult, ALU.subtract).then_inc(ssd_lo, 1)

            def add_ssd(j, it):
                dve.wait_ge(unit_done, 4 * it + 2 * FIRST["wo_ssd"] + j + 1)
                xt = x.rearrange("p m t -> p (m t)")[:, bass.ds(it * (4 * T) + j * T, T)]
                v.tensor_tensor(xt, xt, bank[j % 2][:, :], ALU.add).then_inc(dve_evac, 1)

            dve.wait_ge(key_masked, 1)
            dve.wait_ge(dve_evac, EVAC0["qk"] + 8)
            attention("1", add_ssd)
            for m in range(4):
                split_attention("1", m)
            for m in range(KT):
                dve.wait_ge(dve_evac, EVAC0["wo_ssd"] + m + 1)
                add_x("wo_att", m, m, unit=m // 2)
                low("mlp", m, gains[:, 2, :], (a_hi, a_lo))
                add_square("mlp", m)
            inverse_rms("mlp", EPS1)

            def ff_group(g, last=False):
                for j in range(KT):
                    n = KT * g + j
                    dve.wait_ge(unit_done, 2 * FIRST["ff1_0"] + 16 * g + j + 1)
                    v.scalar_tensor_tensor(relu[j % 2], bank[j % 4][:, :], 0.0, rstd, ALU.max, ALU.mult).then_inc(dve_evac, 1)
                    dve.wait_ge(ff_hi, n + 1)
                    v.tensor_tensor(b_lo[:, j, :], relu2[j % 2], b_hi[:, j, :].bitcast(F32), ALU.subtract).then_inc(ff_lo, 1)
                for m in range(KT):
                    dve.wait_ge(dve_evac, EVAC0["ff1_0"] + 16 * g - 8 + m + 1)
                    add_x("ff2_0", m, m, rounds=16 * g)
                    if last:
                        low("mix2", m, gain12, (a_hi, a_lo))
                        add_square("end1", m)
                        add_square("mix2", m, sq_g_sum, sq_g)

            with dve.Fori(0, FF_GROUPS - 1) as g:
                ff_group(g)
            ff_group(FF_GROUPS - 1, last=True)

            inverse_rms("end1", EPS1, STAT[0], rstd1)
            n2 = NORMS["mix2"]
            dve.wait_ge(n2["stat"], 1)
            v.tensor_tensor(ratio, rstd1, rstd1, ALU.mult).then_inc(n2["var2"], 1)
            dve.wait_ge(n2["var2"], 1)
            v.tensor_tensor(ratio, ratio, STAT[1][:, :], ALU.mult).then_inc(n2["var2"], 1)
            dve.wait_ge(n2["var2"], 2)
            v.tensor_scalar(rstd, ratio, 1.0 / D, EPS2, ALU.mult, ALU.add).then_inc(n2["var"], 1)
            dve.wait_ge(n2["std"], 1)
            v.reciprocal(ratio, rstd).then_inc(n2["var2"], 1)
            dve.wait_ge(n2["var2"], 3)
            v.tensor_tensor(rstd, ratio, rstd1, ALU.mult).then_inc(n2["rstd"], 1)
            dve.wait_ge(n2["rstd"], 1)
            qk_evac("qk2a", 0, 2)
            for m in range(KT):
                v.scalar_tensor_tensor(x[:, m, :], x[:, m, :], gains[:, 3, m:m + 1], rstd1, ALU.mult, ALU.mult).then_inc(x_normed, 1)
                if m == 3:
                    qk_evac("qk2a", 2, 3)
            rstd_by_token("mix2")
            qk_evac("qk2a", 3, 4)
            small_logs(1, bf2, forget=True)
            qk_evac("qk2a", 4, 7)
            dve.wait_ge(cum_done, 2)
            split_cum(1, -1.0)
            qk_evac("qk2a", 7, 8)
            dve.wait_ge(dve_evac, EVAC0["qk2a"] + 8)
            dve.wait_ge(late_loaded, 48)
            v.memset(ws_t[HEAD:P, :, 0:HEAD], 0.0).then_inc(key_masked, 1)
            attention("2a", None)
            dve.wait_ge(zv_gelu, TT)
            v.tensor_scalar(stats[:, 1, 0:4], stats[:, 0, 0:4], -1.0 / D, None, ALU.mult).then_inc(ln_step, 1)

            def linear_u(first, last):
                for m in range(first, last):
                    scaled_evac("u", m, u_t[:, m * T:(m + 1) * T])

            linear_u(0, 1)
            dve.wait_ge(ln_sq, TT)
            v.tensor_scalar(stats[:, 1, 4:8], stats[:, 0, 4:8], 1.0 / D, EPS2, ALU.mult, ALU.add).then_inc(ln_step, 1)
            dve.wait_ge(ln_std, 1)
            v.reciprocal(stats[:, 2, 4:8], stats[:, 2, 0:4]).then_inc(ln_step, 1)
            linear_u(1, 2)
            dve.wait_ge(ln_step, 3)
            for t in range(TT):
                zt = zv_tok[:, t * D:(t + 1) * D]
                v.tensor_scalar(zt, zt, stats[:, 1, t:t + 1], stats[:, 2, 4 + t:5 + t], ALU.add, ALU.mult).then_inc(ln_ready, 1)
                linear_u(2 + t, 3 + t)
            dve.wait_ge(row_sums, 1)
            for g in range(KT):
                v.scalar_tensor_tensor(shift[:, g, :], bank[4 + g // 4][:, (g % 4) * P:(g % 4 + 1) * P], gains[:, 9, g:g + 1],
                                       shift[:, g, :], ALU.mult, ALU.add).then_inc(shift_ready, 1)
            linear_u(6, 8)
            t4 = lambda a: a.rearrange("p (t c) -> p t c", t=TT)
            dve.wait_ge(shift_ready, KT)
            for g in range(KT):
                qk_evac("qk2b", g, g + 1)
                dve.wait_ge(mixed_done, g + 1)
                v.scalar_tensor_tensor(t4(lin[g % 2]), t4(bank[6 + g % 2][:, :]), gains[:, 8, g:g + 1],
                                       shift[:, g, :].unsqueeze(1).to_broadcast([P, TT, P]), ALU.mult, ALU.add).then_inc(mix_read, 1)
                dve.wait_ge(mix_read, g + 1)
                dve.wait_ge(ug, g + 1)
                ut = u_t[:, g * T:(g + 1) * T]
                v.tensor_tensor(ut, ut, lin[g % 2], ALU.mult).then_inc(a_ready, 1)
            dve.wait_ge(dve_evac, EVAC0["qk2b"] + 8)

            def linear_gate_b(j, it):
                scaled_evac("gate_b", j, merged[:, bass.ds(it * (4 * T) + j * T, T)], ps=bank[j % 2], rounds=4 * it)

            attention("2b", linear_gate_b)
            for j in range(KT):
                scaled_evac("gate_a", j, gate_t[:, j * T:(j + 1) * T])
                split_attention("2", j)

            def low_a(g):
                dve.wait_ge(amix_hi, g + 1)
                v.tensor_tensor(a_lo[:, g, :], u_t[:, g * T:(g + 1) * T], a_hi[:, g, :].bitcast(F32), ALU.subtract).then_inc(amix_lo, 1)

            for j in range(KT):
                mt = merged[:, j * T:(j + 1) * T]
                dve.wait_ge(unit_done, 2 * FIRST["branch_b"] + j + 1)
                dve.wait_ge(gated, j + 1)
                v.tensor_tensor(mt, mt, bank[j % 4][:, :], ALU.mult).then_inc(dve_evac, 1)
                low_a(j)
            for j in range(KT):
                gt, mt = gate_t[:, j * T:(j + 1) * T], merged[:, j * T:(j + 1) * T]
                dve.wait_ge(unit_done, 2 * FIRST["branch_a"] + j + 1)
                dve.wait_ge(gated, KT + j + 1)
                v.tensor_tensor(gt, gt, bank[j % 4][:, :], ALU.mult).then_inc(dve_evac, 1)
                dve.wait_ge(dve_evac, EVAC0["branch_a"] + j + 1)
                v.tensor_tensor(mt, mt, gt, ALU.add).then_inc(merged_ready, 1)
                dve.wait_ge(m_hi, j + 1)
                v.tensor_tensor(b_lo[:, j, :], mt, b_hi[:, j, :].bitcast(F32), ALU.subtract).then_inc(m_lo, 1)
            dve.wait_ge(x_normed, KT)
            for m in range(KT):
                add_x("out2", m, m)
                low("ffn2", m, gains[:, 5, :], (a_hi, a_lo))
                add_square("ffn2", m)
            inverse_rms("ffn2", EPS2)

            for q in range(4):
                v.memset(up_pad[q][:, 0:CONV2 - 1], 0.0)

            def up_group(g, tiles, last=False):
                flat = conv2_w.rearrange("p w c -> p (w c)")
                for i in range(tiles // 2):
                    for q in range(4):
                        half, tile = q // 2, 2 * i + q % 2
                        fill = 4 * i + q
                        at = KT * g + half * UP_TILES + tile
                        scaled_evac("up0", fill, up_pad[q][:, CONV2 - 1:CONV2 - 1 + T], rounds=24 * g)
                        dve.wait_ge(up_tap0, 2 * KT * g + fill + 1)
                        for j in range(1, CONV2):
                            if j > 1:
                                dve.wait_ge(up_taps, 2 * (2 * KT * g + fill) + j - 1)
                            v.scalar_tensor_tensor(up_c[q], up_pad[q][:, j:j + T], flat[:, bass.ds(at * (CONV2 + 1) + j, 1)], up_c[q],
                                                   ALU.mult, ALU.add).then_inc(up_taps, 1)
                        if half == 1:
                            dve.wait_ge(up_gelu, KT * g + tile + 1)
                            dve.wait_ge(up_taps, 2 * (2 * KT * g + fill) + 2)
                            v.tensor_tensor(up_g[q - 2], up_g[q - 2], up_c[q], ALU.mult).then_inc(up_act, 1)
                            dve.wait_ge(up_hi, KT * g + tile + 1)
                            v.tensor_tensor(b_lo[:, tile, :], up_g[q - 2], b_hi[:, tile, :].bitcast(F32),
                                            ALU.subtract).then_inc(up_lo, 1)
                if last:
                    for k in range(2):
                        dve.wait_ge(p_hi_ready, k + 1)
                        v.tensor_tensor(p_lo[:, k, :], p_raw[:, k, :], p_hi[:, k, :].bitcast(F32), ALU.subtract).then_inc(p_lo_ready, 1)
                for m in range(KT):
                    dve.wait_ge(dve_evac, EVAC0["up0"] + 24 * g - 8 + m + 1)
                    if last:
                        add_x("down2", m, m)
                        low("ple", m, gains[:, 6, :], (a_hi, a_lo))
                        add_square("ple", m)
                    else:
                        add_x("down0", m, m, rounds=24 * g)

            with dve.Fori(0, UP_TILES // KT) as g:
                up_group(g, KT)
            up_group(UP_TILES // KT, UP_TILES % KT, last=True)
            inverse_rms("ple", EPS2)
            for m in range(KT):
                s_m = sig[m % 2]
                scaled_evac("gate", m, s_m)
                dve.wait_ge(ple_sig, m + 1)
                dve.wait_ge(act_evac, EVAC0["ple"] + m + 1)
                v.tensor_tensor(s_m, s_m, ple_t[:, m * T:(m + 1) * T], ALU.mult).then_inc(ple_mul, 1)
                dve.wait_ge(ple_mul, 2 * m + 1)
                v.tensor_tensor(x[:, m, :], x[:, m, :], s_m, ALU.add).then_inc(ple_mul, 1)
                if m:
                    add_square("end2", m - 1)
            add_square("end2", KT - 1)
            inverse_rms("end2", EPS2, STAT[1])
            for m in range(KT):
                v.scalar_tensor_tensor(out_t[m], x[:, m, :], gains[:, 7, m:m + 1], rstd, ALU.mult, ALU.mult).then_inc(out_ready, 1)


def by_k(w):
    kt, n = w.shape[0] // P, w.shape[1] // STRIP
    return w.reshape(kt, P, n, STRIP).transpose(2, 1, 0, 3).reshape(n, P, kt * STRIP)


def kernel(**inputs):
    import concourse.bacc as bacc
    from concourse import mybir as _mybir
    from concourse.bass_utils import run_bass_kernel_spmd

    g = {k: np.asarray(v) for k, v in inputs.items()}
    w_in, w_out, ff1, ff2 = g["w_in"][0], g["w_out"][0], g["w_ff1"][0], g["w_ff2"][0]
    w_in2, up, down = g["w_in_2"][0], g["w_up_2"][0], g["w_down_2"][0]
    strips = [by_k(w_in[:, 2560:4096]), by_k(w_in[:, 0:1024]), by_k(w_in[:, 1536:2560]), by_k(w_in[:, 1024:1536])]
    strips += [by_k(w_out[512:]), w_out[0:512].reshape(4, P, 2, 512).transpose(2, 1, 0, 3).reshape(2, P, SW)]
    for j in range(FF_GROUPS):
        strips += [by_k(ff1[:, j * D:(j + 1) * D]), by_k(ff2[j * D:(j + 1) * D])]
    for j in range(2):
        for first in (2048, 3072, 4096):
            strips.append(by_k(w_in2[:, first + j * 512:first + (j + 1) * 512]))
        if j == 0:
            strips += [by_k(w_in2[:, 1024:2048]), by_k(w_in2[:, 0:1024])]
    strips += [by_k(w_in2[:, 6160:7184]), by_k(w_in2[:, 5136:6160])]
    strips += [by_k(g["w_branch_b_2"][0]), by_k(g["w_branch_a_2"][0]), by_k(g["w_out_2"][0])]
    half = UP_TILES * P
    ups = np.stack([by_k(up[:, 0:half]), by_k(up[:, half:])], axis=1).reshape(-1, P, SW)
    padded = np.concatenate([down, np.zeros((3 * D - half, D), down.dtype)])
    for j in range(3):
        strips += [ups[8 * j:8 * j + 8], by_k(padded[j * D:(j + 1) * D])]
    strips += [g["w_ple_2"][0].reshape(2, P, D).transpose(1, 0, 2).reshape(1, P, SW), by_k(g["w_ple_gate_2"][0])]

    def by_tile(v):
        return v.reshape(-1, P).T

    def sixteen(w):
        return w.reshape(KT, P, 16).transpose(1, 0, 2)

    gains = [g["norm_mix_w"], g["ssd_norm_w"], g["norm_mlp_w"], g["norm_final_w"], g["norm_mix_g_2"], g["norm_ffn_g_2"],
             g["norm_ple_g_2"], g["norm_final_g_2"], g["gmlp_ln_g_2"], g["gmlp_ln_b_2"]]
    taps1 = np.concatenate([g["conv_w"][0], g["conv_b"]])
    taps2 = np.concatenate([g["conv_w_2"][0], g["conv_b_2"]])
    dist = np.clip(T - P + np.arange(P)[:, None] - np.arange(T)[None, :], -REL, REL) + REL
    arrays = {
        "x_t": g["x"][0].T.reshape(KT, P, T).transpose(1, 0, 2),
        "strips": np.concatenate(strips),
        "gains": np.stack([by_tile(v) for v in gains], axis=1),
        "conv1": taps1.reshape(CONV1 + 1, NXBC, P).transpose(2, 1, 0),
        "conv2": taps2.reshape(CONV2 + 1, 2 * UP_TILES, P).transpose(2, 1, 0),
        "dt_bias": g["dt_bias"][0], "a_log": g["a_log"][0], "d_skip": g["d_skip"][0], "b_f": g["b_f_2"][0],
        "w16": np.stack([sixteen(w_in[:, 4096:4112]), sixteen(w_in2[:, 5120:5136])]),
        "ws_t": g["gmlp_w_s_2"][0].transpose(2, 0, 1), "bs": g["gmlp_b_s_2"][0].reshape(-1),
        "rel": g["rel_bias"][0].T[:, dist],
        "p_t": g["p_2"][0, 0].T.reshape(2, P, T).transpose(1, 0, 2),
    }
    nc = bacc.Bacc("TRN2", target_bir_lowering=False, num_devices=1)
    feed, aps = {}, {}
    for name, a in arrays.items():
        feed[f"in_{name}"] = np.ascontiguousarray(a)
        aps[name] = nc.dram_tensor(f"in_{name}", a.shape, _mybir.dt.from_np(a.dtype), kind="ExternalInput").ap()
    out = nc.dram_tensor("out", (KT, P, T), F32, kind="ExternalOutput").ap()
    build(nc, aps, out)
    r = run_bass_kernel_spmd(nc, [feed], core_ids=[0])
    return r.results[0]["out"].reshape(D, T).T.reshape(1, T, D)
```

```python
from contextlib import ExitStack

import numpy as np

import concourse.bass as bass
from concourse import mybir

F32 = mybir.dt.float32
F32R = mybir.dt.float32r
BF16 = mybir.dt.bfloat16
ALU = mybir.AluOpType
ACT = mybir.ActivationFunctionType
AX_X = mybir.AxisListType.X

P = 128
D = 1024
T = 512
KT = D // P
TT = T // P
STRIP = 256
SW = KT * STRIP
EPS1 = 1e-5
EPS2 = 1e-6
HEAD = 64
H1 = 8
H2 = 16
H_SSD = 16
GROUPS = 2
CONV1 = 4
CONV2 = 3
NXBC = 12
D_FF = 4096
FF_GROUPS = D_FF // D
UP_TILES = 2816 // P
BIG = 1e30
QUAD = 4
STEPS = QUAD * TT
REL = 256
POOL_OUT = 3
OUT_ORDER = [0, 1, 5, 2, 3, 6, 4, 7]
N_GAINS = 10

PHASES = [("xbc", 6), ("qk", 4), ("z", 4), ("v", 2), ("wo_ssd", 4), ("wo_att", 2)]
PHASES += [(f"{w}{g}", 4) for g in range(FF_GROUPS) for w in ("ff1_", "ff2_")]
PHASES += [("qk2a", 4), ("v2a", 2), ("zv", 4), ("u", 4), ("qk2b", 4), ("v2b", 2), ("gate_b", 4), ("gate_a", 4)]
PHASES += [("branch_b", 4), ("branch_a", 4), ("out2", 4)]
PHASES += [("up0", 8), ("down0", 4), ("up1", 8), ("down1", 4), ("up2", 6), ("down2", 4), ("ple", 1), ("gate", 4)]
FIRST = {}
for _name, _n in PHASES:
    FIRST[_name] = sum(n for _, n in PHASES[:len(FIRST)])
N_STRIPS = sum(n for _, n in PHASES)

ON_ACT = {"v", "z", "v2a", "v2b", "zv", "ple"}
FILLS = {name: 2 * n for name, n in PHASES} | {"wo_att": 8, "ple": 8}
WOVEN = {"z", "wo_ssd", "zv", "gate_b"}
BANKS = {name: 2 if name in WOVEN else 4 for name, _ in PHASES}
PIECES = 4 * KT
SLOTS = STEPS + 3
SLOT_PIECES = [5] + [1, 1, 2] * 5 + [2, 2, 3]
STAGE_PARTS = [(0, 1), (2,), (3,), ()]


def evac_base():
    seen, base = {True: 2, False: 0}, {}
    for name, _ in PHASES:
        on_act = name in ON_ACT
        base[name] = seen[on_act]
        seen[on_act] += FILLS[name]
    return base


EVAC0 = evac_base()
BEFORE = {name: PHASES[n - 1][0] for n, (name, _) in enumerate(PHASES) if n}


def slot_pieces(n):
    return range(sum(SLOT_PIECES[:n]), sum(SLOT_PIECES[:n + 1]))


def slot_units(n):
    return [p // KT for p in slot_pieces(n) if p % KT == KT - 1]


def build(nc, d, out):
    ctx = ExitStack()
    with ctx:
        base = (nc.sbuf_base + 63) // 64 * 64
        place = {}
        cursor = [0]

        def sb(name, shape, dt=F32, at=None):
            size = 2 if dt == BF16 else 4
            cols = -(-int(np.prod(shape[1:])) * size // 32) * 8
            off = cursor[0] if at is None else at
            if at is None:
                cursor[0] += cols
            place[name] = off
            assert base + 4 * (off + cols) <= nc.sbuf_usable_end, (name, off, cols)
            return nc.alloc_sbuf_tensor_at(name, list(shape), dt, offset=base + 4 * off).ap()

        def sem(name):
            return ctx.enter_context(nc.semaphore(name))

        x = sb("x", [P, KT, T])
        a_hi = sb("a_hi", [P, KT, T], F32R)
        a_lo = sb("a_lo", [P, KT, T], F32R)
        b_hi = sb("b_hi", [P, KT, T], F32R)
        b_lo = sb("b_lo", [P, KT, T], F32R)
        w_raw = [sb(f"w_raw{j}", [P, KT, STRIP]) for j in range(2)]
        w_hi = [sb(f"w_hi{j}", [P, KT, STRIP], F32R) for j in range(2)]
        w_lo = [sb(f"w_lo{j}", [P, KT, STRIP], F32R) for j in range(2)]
        ident = sb("ident", [P, P])
        steps01 = sb("steps01", [P, 4 * P])
        tri, ones = steps01[:, 0:P], steps01[:, P:2 * P]
        zeros = sb("zeros", [P, 1])
        ident16 = sb("ident16", [P, P], BF16)
        future16 = sb("future16", [P, P], BF16)
        past16 = sb("past16", [P, P], BF16)
        gains = sb("gains", [P, N_GAINS, KT])
        gain12 = sb("gain12", [P, KT])
        conv1_w = sb("conv1_w", [P, NXBC, CONV1 + 1])
        conv2_w = sb("conv2_w", [P, 2 * UP_TILES, CONV2 + 1])
        heads1 = sb("heads1", [P, 3, H_SSD])
        bf2 = sb("bf2", [P, H2])
        w16 = sb("w16", [P, 2, KT, 48], F32R)
        rstd = sb("rstd", [P, T])
        rstd_tok = sb("rstd_tok", [P, TT])
        exp_a = sb("exp_a", [P, H_SSD])
        row_max = sb("row_max", [P, STEPS])
        row_sum = sb("row_sum", [P, STEPS])
        row_inv = sb("row_inv", [P, STEPS])
        stats = sb("stats", [P, 3, 8])
        wait_note = sb("wait_note", [P, 2])
        sel = sb("sel", [P, 16], F32R)
        work = cursor[0]

        B_HI, B_LO = place["b_hi"], place["b_lo"]
        sq = [sb(f"sq{j}", [P, T], at=work + j * T) for j in range(2)]
        sq_sum = sb("sq_sum", [P, T], at=work + 2 * T)
        sq_g = [sb(f"sq_g{j}", [P, T], at=work + 4096 + j * T) for j in range(2)]
        sq_g_sum = sb("sq_g_sum", [P, T], at=work + 4096 + 2 * T)
        rstd1 = sb("rstd1", [P, T], at=work + 4096 + 3 * T)

        qk = sb("qk", [P, 8 * T], at=B_LO)
        head_bias = sb("head_bias", [P, H1 * T], at=B_HI)
        u_pad = [sb(f"u_pad{j}", [P, CONV1 - 1 + T], at=B_HI + 520 * j) for j in range(2)]
        conv = [sb(f"conv{j}", [P, T], at=B_HI + 1040 + T * j) for j in range(2)]
        xs_t = [sb(f"xs_t{j}", [P, T], at=B_HI + 2064 + T * j) for j in range(2)]
        decay = sb("decay", [P, H_SSD, P], at=B_HI)
        x_dt = sb("x_dt", [P, D], at=B_HI + 2048)
        x_out = sb("x_out", [P, D], at=B_HI + 3072)
        xs_tok = sb("xs_tok", [P, TT * D], at=work)
        bc_t = sb("bc_t", [P, 4, T], at=work + 4096)
        b_tok = sb("b_tok", [P, TT, 256], at=work + 6144)
        y_hi = sb("y_hi", [P, KT, T], F32R, at=work)
        y_lo = sb("y_lo", [P, KT, T], F32R, at=work + 4096)
        sp = {n: sb(f"sp_{n}", [P, TT * 16], at=work + 7168 + 64 * j) for j, n in enumerate(
            ("x", "na", "e", "d", "r", "s", "q", "p", "m", "val", "a", "nacum", "diff", "eac", "cdec", "dout"))}
        cum = sb("cum", [P, T], F32R, at=work + 8192)
        small_t = sb("small_t", [48, T], at=work + 8704)
        w16_raw = sb("w16_raw", [P, 2, KT, 16], at=work + 16640)
        z_tok = sb("z_tok", [P, TT * D], at=work + 8704)
        state = sb("state", [P, D], at=work + 12800)
        y_tmp = sb("y_tmp", [P, D], at=work + 13824)
        x_skip = sb("x_skip", [P, D], at=work + 14848)
        b_c = sb("b_c", [P, 2, P], at=work + 15872)
        c_c = sb("c_c", [P, 2, P], at=work + 16128)
        bt_c = sb("bt_c", [P, 256], at=work + 16384)
        unused = [sb(f"unused{j}", [P, 512], at=work + 14848 + 512 * j) for j in range(4)]
        att_tok = sb("att_tok", [P, 2 * TT * 512], at=work + 8704)

        def staged(blk, at):
            return {n: [sb(f"{n}_{blk}_{j}", [P, T], F32R, at=at + (4 * j + i) * T) for j in range(2)]
                    for i, n in enumerate(("q1", "k1", "q2", "k2"))}

        stage1, stage2 = staged("blk1", place["a_hi"]), staged("blk2", B_HI)
        v_tok = sb("v_tok", [P, TT * 8 * HEAD], at=work + 12800)
        score = sb("score", [P, 3, T], at=work + 14848)
        prob_t = sb("prob_t", [P, 2, T], at=work + 16384)
        relu = [sb(f"relu{j}", [P, T], at=work + 2048 + T * j) for j in range(2)]
        relu2 = [sb(f"relu2_{j}", [P, T], at=work + 3072 + T * j) for j in range(2)]
        ws_t = sb("ws_t", [P, KT, P], at=work + 10752)
        shift = sb("shift", [P, KT, P], at=work + 11776)
        u_t = sb("u_t", [P, KT * T], at=work)
        zv_tok = sb("zv_tok", [P, TT * D], at=work + 4096)
        merged = sb("merged", [P, KT * T], at=work + 4096)
        sq_wide = [sb(f"sq_wide{j}", [P, D], at=work + 14848 + D * j) for j in range(2)]
        lin = [sb(f"lin{j}", [P, T], at=work + 14848 + T * j) for j in range(2)]
        gate_t = sb("gate_t", [P, KT * T], at=work + 12800)
        up_pad = [sb(f"up_pad{j}", [P, CONV2 - 1 + T], at=work + 2048 + 520 * j) for j in range(4)]
        up_c = [sb(f"up_c{j}", [P, T], at=work + 4608 + T * j) for j in range(4)]
        up_g = [sb(f"up_g{j}", [P, T], at=work + 6656 + T * j) for j in range(2)]
        ple_t = sb("ple_t", [P, KT * T], at=work + 8192)
        p_raw = sb("p_raw", [P, 2, T], at=work + 12288)
        p_hi = sb("p_hi", [P, 2, T], F32R, at=work + 13312)
        p_lo = sb("p_lo", [P, 2, T], F32R, at=work + 14336)
        sig = [sb(f"sig{j}", [P, T], at=work + 2048 + T * j) for j in range(2)]
        out_t = [sb(f"out_t{j}", [P, T], at=work + 3072 + T * j) for j in range(8)]

        bank = [ctx.enter_context(nc.psum_tensor(f"bank{j}", [P, T], F32)) for j in range(8)]
        STAT = [bank[4], bank[5]]

        x_loaded = [sem(f"x_loaded{j}") for j in range(4)]
        gains_loaded = sem("gains_loaded")
        consts_loaded = sem("consts_loaded")
        late_loaded = sem("late_loaded")
        raw_loaded = [sem(f"raw_loaded{j}") for j in range(2)]
        half_loaded = sem("half_loaded")
        masks_ready = sem("masks_ready")
        pool_start_step = sem("pool_start_step")
        hi_split = sem("hi_split")
        strip_split = sem("strip_split")
        unit_done = sem("unit_done")
        act_evac = sem("act_evac")
        dve_evac = sem("dve_evac")

        def norm_sems(n):
            keys = ["sq", "sum", "stat", "var", "std", "rstd"]
            keys += ["hi", "lo"] if not n.startswith("end") else []
            keys += ["turned", "tok"] if n.startswith("mix") else []
            return {k: sem(f"{n}_{k}") for k in keys}

        NORMS = {n: norm_sems(n) for n in ("mix1", "mlp", "end1", "mix2", "ffn2", "ple", "end2")}
        dve_start_step = sem("dve_start_step")
        x_normed = sem("x_normed")
        w16_hi_ready = sem("w16_hi_ready")
        w16_ready = sem("w16_ready")
        key_masked = sem("key_masked")
        qk_staged = sem("qk_staged")
        lo_staged = sem("lo_staged")
        scored = sem("scored")
        biased = sem("biased")
        maxed = sem("maxed")
        exped = sem("exped")
        turned = sem("turned")
        prob_ready = sem("prob_ready")
        pv_done = sem("pv_done")
        inverted = sem("inverted")
        att_out = sem("att_out")
        att_turned = sem("att_turned")
        att_hi = sem("att_hi")
        att_lo = sem("att_lo")
        small_done = sem("small_done")
        sp_step = sem("sp_step")
        sp_exp = sem("sp_exp")
        cum_done = sem("cum_done")
        cum_act = sem("cum_act")
        cum_dve = sem("cum_dve")
        cum_ready = sem("cum_ready")
        tap0 = sem("tap0")
        taps = sem("taps")
        conv_silu = sem("conv_silu")
        xs_turned = sem("xs_turned")
        xs_ready = sem("xs_ready")
        chunk_staged = sem("chunk_staged")
        x_scaled = sem("x_scaled")
        seg_done = sem("seg_done")
        cb_done = sem("cb_done")
        decayed = sem("decayed")
        mixed_ready = sem("mixed_ready")
        y_done = sem("y_done")
        state_done = sem("state_done")
        y_step = sem("y_step")
        state_ready = sem("state_ready")
        state_step = sem("state_step")
        z_silu = sem("z_silu")
        y_gated = sem("y_gated")
        y_sq = sem("y_sq")
        y_std = sem("y_std")
        y_stat = sem("y_stat")
        y_norm = sem("y_norm")
        y_turned = sem("y_turned")
        ssd_hi = sem("ssd_hi")
        ssd_lo = sem("ssd_lo")
        ff_hi = sem("ff_hi")
        ff_lo = sem("ff_lo")
        gated = sem("gated")
        merged_ready = sem("merged_ready")
        m_hi = sem("m_hi")
        m_lo = sem("m_lo")
        ug = sem("ug")
        row_sums = sem("row_sums")
        shift_ready = sem("shift_ready")
        zv_gelu = sem("zv_gelu")
        ln_step = sem("ln_step")
        ln_sq = sem("ln_sq")
        ln_std = sem("ln_std")
        ln_ready = sem("ln_ready")
        mixed_done = sem("mixed_done")
        mix_read = sem("mix_read")
        a_ready = sem("a_ready")
        amix_hi = sem("amix_hi")
        amix_lo = sem("amix_lo")
        up_tap0 = sem("up_tap0")
        up_taps = sem("up_taps")
        up_gelu = sem("up_gelu")
        up_act = sem("up_act")
        up_hi = sem("up_hi")
        up_lo = sem("up_lo")
        p_hi_ready = sem("p_hi_ready")
        p_lo_ready = sem("p_lo_ready")
        ple_sig = sem("ple_sig")
        ple_mul = sem("ple_mul")
        x_scaled_out = sem("x_scaled_out")
        out_ready = sem("out_ready")
        pool_out_ready = sem("pool_out_ready")
        stored = sem("stored")

        QUAD0 = {"1": 0, "2a": 2, "2b": 4}
        ATT_T0 = {"1": 0, "2": 4}
        N_CONST = 8
        SP_LOG = 17
        SP_A = SP_LOG + 1
        SP_END = SP_A + SP_LOG

        block = ctx.enter_context(nc.Block())

        def evac_sem(phase):
            return act_evac if phase in ON_ACT else dve_evac

        @block.sync
        def _(sp_eng):
            for h in range(4):
                if h < 2:
                    cols = slice(h * (SW // 2), (h + 1) * (SW // 2))
                    sp_eng.dma_start(w_raw[0].rearrange("p k n -> p (k n)")[:, cols],
                                     d["strips"][0][:, cols]).then_inc(raw_loaded[0] if h == 0 else half_loaded, 16)
                sp_eng.dma_start(x[:, 2 * h:2 * h + 2, :], d["x_t"][:, 2 * h:2 * h + 2, :]).then_inc(x_loaded[h], 16)
            sp_eng.dma_start(w_raw[1].rearrange("p k n -> p (k n)"), d["strips"][1]).then_inc(raw_loaded[1], 16)
            with sp_eng.Fori(1, N_STRIPS // 2) as i:
                for j in range(2):
                    sp_eng.wait_ge(strip_split, 2 * i + j - 1)
                    sp_eng.dma_start(w_raw[j].rearrange("p k n -> p (k n)"),
                                     d["strips"][bass.ds(2 * i + j, 1)].rearrange("a p n -> (a p) n")).then_inc(raw_loaded[j], 16)
            sp_eng.wait_ge(strip_split, N_STRIPS - 2)
            sp_eng.dma_start(w_raw[0].rearrange("p k n -> p (k n)"), d["strips"][N_STRIPS - 1]).then_inc(raw_loaded[0], 16)
            for m in OUT_ORDER:
                if m < KT - POOL_OUT:
                    sp_eng.wait_ge(out_ready, m + 1)
                else:
                    sp_eng.wait_ge(pool_out_ready, m + 1 - (KT - POOL_OUT))
                sp_eng.dma_start(out[m], out_t[m]).then_inc(stored, 16)
            sp_eng.wait_ge(stored, 16 * KT)

        @block.gpsimd
        def _(pool):
            def split_strip(j, loads, strip):
                pool.wait_ge(raw_loaded[j], 16 * loads)
                pool.wait_ge(unit_done, 2 * strip - 2)
                pool.tensor_tensor(wait_note[:, 0:1], ident[:, 0:1], ident[:, 0:1], ALU.mult)
                pool.tensor_scalar(w_hi[j], w_raw[j], 1.0, 1.0, ALU.mult, ALU.mult).then_inc(hi_split, 1)
                pool.wait_ge(hi_split, strip)
                pool.tensor_tensor(w_lo[j], w_raw[j], w_hi[j].bitcast(F32), ALU.subtract).then_inc(strip_split, 1)

            halves = [slice(h * (KT // 2), (h + 1) * (KT // 2)) for h in range(2)]
            for h, half in enumerate(halves):
                pool.wait_ge(raw_loaded[0] if h == 0 else half_loaded, 16)
                pool.tensor_scalar(w_hi[0][:, half], w_raw[0][:, half], 1.0, 1.0, ALU.mult, ALU.mult).then_inc(pool_start_step, 1)
            pool.wait_ge(pool_start_step, 2)
            pool.wait_ge(dve_start_step, 1)
            pool.tensor_tensor(w_lo[0][:, half], w_raw[0][:, half], w_hi[0][:, half].bitcast(F32),
                               ALU.subtract).then_inc(strip_split, 1)
            for part, value in ((ident, 0.0), (zeros, 0.0), (steps01, 1.0), (ident16, 0.0),
                                (future16, 0.0), (past16, 0.0)):
                pool.memset(part, value).then_inc(pool_start_step, 1)
            pool.wait_ge(pool_start_step, 8)
            for m in (ident, ident16):
                pool.affine_select(out=m, in_=m, compare_op=ALU.not_equal, fill=1.0, base=0,
                                   pattern=[[-1, P]], channel_multiplier=1).then_inc(masks_ready, 1)
            pool.affine_select(out=tri, in_=tri, compare_op=ALU.is_ge, fill=0.0, base=0,
                               pattern=[[1, P]], channel_multiplier=-1).then_inc(masks_ready, 1)
            pool.affine_select(out=future16, in_=future16, compare_op=ALU.is_ge, fill=-BIG, base=0,
                               pattern=[[-1, P]], channel_multiplier=1).then_inc(masks_ready, 1)
            pool.affine_select(out=past16, in_=past16, compare_op=ALU.is_ge, fill=-BIG, base=0,
                               pattern=[[1, P]], channel_multiplier=-1).then_inc(masks_ready, 1)
            pool.wait_ge(masks_ready, 5)
            pool.wait_ge(raw_loaded[1], 16)
            pool.tensor_scalar(w_hi[1], w_raw[1], 1.0, 1.0, ALU.mult, ALU.mult).then_inc(hi_split, 1)
            pool.wait_ge(hi_split, 1)
            pool.tensor_tensor(w_lo[1][:, halves[0]], w_raw[1][:, halves[0]], w_hi[1][:, halves[0]].bitcast(F32),
                               ALU.subtract)
            pool.wait_ge(dve_start_step, 2)
            pool.tensor_tensor(wait_note[:, 1:2], ident[:, 0:1], ident[:, 0:1], ALU.mult).then_inc(strip_split, 1)
            with pool.Fori(1, N_STRIPS // 2) as i:
                for j in range(2):
                    split_strip(j, i + 1, 2 * i + j)
            split_strip(0, N_STRIPS // 2 + 1, N_STRIPS - 1)
            pool.wait_ge(x_scaled_out, KT)
            pool.wait_ge(NORMS["end2"]["rstd"], 1)
            for m in range(KT - POOL_OUT, KT):
                pool.tensor_tensor(out_t[m], x[:, m, :], rstd, ALU.mult).then_inc(pool_out_ready, 1)

        @block.tensor
        def _(pe):
            mm, tr = nc.tensor.matmul, nc.tensor.transpose

            def bank_free(phase, j, fills=0):
                n = BANKS[phase]
                if j >= n:
                    pe.wait_ge(evac_sem(phase), EVAC0[phase] + fills + j - n + 1)
                elif phase in BEFORE:
                    before = BEFORE[phase]
                    last = FILLS[before] - BANKS[before] + min(j, BANKS[before] - 1)
                    pe.wait_ge(evac_sem(before), EVAC0[before] + fills + last + 1)

            def feature_k(ps, slot, u, act, k, kt=KT):
                cols, (hi, lo) = slice(u * P, u * P + P), act
                mm(ps[:, :], w_hi[slot][:, k, cols], hi[:, k, :], start=(k == 0), stop=False)
                mm(ps[:, :], w_hi[slot][:, k, cols], lo[:, k, :], start=False, stop=False)
                return mm(ps[:, :], w_lo[slot][:, k, cols], hi[:, k, :], start=False, stop=(k == kt - 1))

            def token_k(ps, slot, u, act, k, kt=KT):
                t, (hi, lo) = k // 4, act
                dst = ps[:, t * STRIP:(t + 1) * STRIP]
                tok = slice((2 * u + t) * P, (2 * u + t + 1) * P)
                for q in (2 * k % KT, 2 * k % KT + 1):
                    mm(dst, hi[:, q, tok], w_hi[slot][:, q, :], start=(q == 0), stop=False)
                    mm(dst, hi[:, q, tok], w_lo[slot][:, q, :], start=False, stop=False)
                    last = mm(dst, lo[:, q, tok], w_hi[slot][:, q, :], start=False, stop=(q == KT - 1))
                return last

            def stream(phase, part, act, ready=None, after=None, strips=0, fills=0, kt=KT):
                for s in range(FILLS[phase] // 2):
                    slot = (FIRST[phase] + s) % 2
                    if FIRST[phase] + s:
                        pe.wait_ge(strip_split, FIRST[phase] + s + 1 + strips)
                    else:
                        pe.wait_ge(dve_start_step, 1)
                    pair = s == 0 and ready is not None
                    if pair:
                        for u in range(2):
                            bank_free(phase, u, fills)
                        for k in range(kt):
                            if FIRST[phase] == 0 and k == KT // 2:
                                pe.wait_ge(strip_split, 1)
                            ready(k)
                            for u in range(2):
                                last = part(bank[u], slot, u, act, k, kt)
                                if k == kt - 1:
                                    last.then_inc(unit_done, 1)
                    for u in range(2):
                        j = 2 * s + u
                        if not pair:
                            bank_free(phase, j, fills)
                            for k in range(kt):
                                last = part(bank[j % BANKS[phase]], slot, u, act, k, kt)
                            last.then_inc(unit_done, 1)
                        if after is not None:
                            after(j)

            def piece(phase, part, act, p, it, ready=None):
                j, k = p // KT, p % KT
                if k == 0:
                    if j % 2 == 0:
                        pe.wait_ge(strip_split, FIRST[phase] + 2 * it + j // 2 + 1)
                    pe.wait_ge(evac_sem(phase), EVAC0[phase] + 4 * it + j - 1)
                if j == 0 and ready is not None:
                    ready(k)
                last = part(bank[j % 2], j // 2, j % 2, act, k)
                if k == KT - 1:
                    last.then_inc(unit_done, 1)

            def woven_start(phase):
                for j in range(2):
                    bank_free(phase, j)

            def stat(norm, total, where):
                pe.wait_ge(NORMS[norm]["sum"], KT)
                mm(where[:, :], ones, total, start=True, stop=True).then_inc(NORMS[norm]["stat"], 1)

            def turn_rstd(norm):
                n = NORMS[norm]
                pe.wait_ge(n["rstd"], 1)
                for t in range(TT):
                    last = tr(bank[7][:, t * P:(t + 1) * P], rstd[:, t * P:(t + 1) * P], ident)
                last.then_inc(n["turned"], 1)

            def wait_tiles(s):
                return lambda k: pe.wait_ge(s, k + 1)

            def small_columns(which, act):
                pe.wait_ge(w16_ready, 2 + which)
                for k in range(KT):
                    for part in act:
                        last = mm(bank[6][0:48, :], w16[:, which, k, :], part[:, k, :], start=(k == 0 and part is act[0]),
                                  stop=(k == KT - 1 and part is act[1]))
                last.then_inc(small_done, 1)

            def turn_small(which, norm):
                pe.wait_ge(NORMS[norm]["tok"], 1)
                pe.wait_ge(dve_start_step, 8)
                pe.wait_ge(sp_exp, 3 * which + 1)
                for t in range(TT):
                    last = mm(bank[7][:, t * 16:(t + 1) * 16], small_t[:, t * P:(t + 1) * P], sel.bitcast(F32)[0:48, :],
                              start=True, stop=True)
                last.then_inc(small_done, 1)

            def attention(call, phase, part, act, ready=None):
                causal = call != "1"
                v_phase = {"1": "v", "2a": "v2a", "2b": "v2b"}[call]
                woven_start(phase)
                st = stage2 if causal else stage1

                def scores(n, q0):
                    head, i = n // TT, n % TT
                    w, parity = P * (i + 1), head % 2
                    if i == 0:
                        pe.wait_ge(qk_staged, 4 * QUAD * q0 + 4 * head + 4)
                        pe.wait_ge(lo_staged, 3 * QUAD * q0 + 3 * head + 3)
                    if n < 2:
                        pe.wait_ge(act_evac, EVAC0[v_phase] + 3 + n)
                    else:
                        pe.wait_ge(exped if causal else biased, STEPS * q0 + n - 1)
                    ps, mine = bank[2 + n % 2], slice(i * P, (i + 1) * P)
                    mm(ps[:, 0:w], st["q1"][parity][:, mine], st["k1"][parity][:, 0:w], start=True, stop=False)
                    last = mm(ps[:, 0:w], st["q2"][parity][:, mine], st["k2"][parity][:, 0:w], start=False, stop=True)
                    if causal:
                        last = mm(ps[:, w - P:w], ident16, future16, start=False, stop=True, skip_group_check=True)
                    last.then_inc(scored, 1)

                def turn(n, q0):
                    i = n % TT
                    pe.wait_ge(exped, STEPS * q0 + n + 1)
                    if n == 0 and not causal:
                        pe.wait_ge(ssd_lo, KT)
                    if n >= 2:
                        pe.wait_ge(prob_ready, STEPS * q0 + n - 1)
                    for j in range(i + 1):
                        last = tr(bank[4 + n % 2][:, j * P:(j + 1) * P], score[:, n % 3, j * P:(j + 1) * P], ident)
                    last.then_inc(turned, 1)

                def values(n, q0, it):
                    head, i = n // TT, n % TT
                    pe.wait_ge(prob_ready, STEPS * q0 + n + 1)
                    if n == 0:
                        pe.wait_ge(act_evac, EVAC0[v_phase] + FILLS[v_phase])
                    if n >= 2:
                        pe.wait_ge(att_out, STEPS * q0 + n - 1)
                    for j in range(i + 1):
                        last = mm(bank[6 + n % 2][:, 0:HEAD], prob_t[:, n % 2, j * P:(j + 1) * P],
                                  v_tok[:, bass.ds(j * 8 * HEAD + head * HEAD + it * (QUAD * HEAD), HEAD)],
                                  start=(j == 0), stop=(j == i))
                    last.then_inc(pv_done, 1)

                with pe.Fori(0, 2) as it:
                    q0 = QUAD0[call] + it
                    for n in range(SLOTS):
                        if n < STEPS and n:
                            scores(n, q0)
                        if n < SLOTS - 1:
                            for p in slot_pieces(n):
                                piece(phase, part, act, p, it, ready)
                        if n == 0:
                            scores(n, q0)
                        if 2 <= n < STEPS + 2:
                            turn(n - 2, q0)
                        if n >= 3:
                            values(n - 3, q0, it)
                    for p in slot_pieces(SLOTS - 1):
                        piece(phase, part, act, p, it, ready)
                    pe.wait_ge(att_out, STEPS * q0 + STEPS)

            def turn_attention(blk, m):
                n = ATT_T0[blk] + m
                if m >= 4:
                    pe.wait_ge(att_lo, n - 3)
                for t in range(TT):
                    at = m // 4 * (TT * 512) + t * 512 + m % 4 * P
                    last = tr(bank[4 + m % 4][:, t * P:(t + 1) * P], att_tok[:, at:at + P], ident)
                last.then_inc(att_turned, 1)

            A, B, Y = (a_hi, a_lo), (b_hi, b_lo), (y_hi, y_lo)

            def turn_xs(m):
                pe.wait_ge(conv_silu, m + 1)
                if m >= 2:
                    pe.wait_ge(xs_ready, m - 1)
                else:
                    pe.wait_ge(NORMS["mix1"]["var"], 1)
                src = xs_t[m % 2] if m < 8 else bc_t[:, m - 8, :]
                for t in range(TT):
                    last = tr(bank[4 + m % 2][:, t * P:(t + 1) * P], src[:, t * P:(t + 1) * P], ident)
                last.then_inc(xs_turned, 1)

            def after_xbc(j):
                if j == 1:
                    pe.wait_ge(masks_ready, 5)
                    stat("mix1", sq_sum, STAT[0])
                if j == 3:
                    turn_rstd("mix1")
                if j >= 3:
                    turn_xs(j - 3)

            stream("xbc", feature_k, A, ready=wait_tiles(NORMS["mix1"]["lo"]), after=after_xbc)
            small_columns(0, A)
            turn_xs(9)

            def after_qk(j):
                if j == 0:
                    turn_small(0, "mix1")
                if j != 5:
                    return
                pe.wait_ge(sp_step, SP_A)
                mm(bank[6][:, 0:64], tri, sp["a"], start=True, stop=True)
                mm(bank[6][:, 64:128], ones, sp["a"], start=True, stop=True)
                for c in range(TT):
                    last = mm(bank[7][0:16, c * P:(c + 1) * P], sp["a"][:, c * 16:(c + 1) * 16], tri, start=True, stop=True)
                last.then_inc(cum_done, 1)

            stream("qk", feature_k, A, after=after_qk)

            woven_start("z")
            pe.wait_ge(cum_ready, 2)
            pe.wait_ge(dve_start_step, 8)
            with pe.Fori(0, TT // 2) as it:
                def fill(first, last):
                    for p in range(first, last):
                        piece("z", token_k, A, p, it)

                for half in range(2):
                    c, p0 = 2 * it + half, half * (PIECES // 2)

                    def seg(q):
                        for h in range(4):
                            part = bank[2 + q % 2][:, h * P:(h + 1) * P]
                            mm(part, ident16, past16, start=True, stop=False)
                            last = mm(part, sel[:, 4 * q + h:4 * q + h + 1].to_broadcast([P, P]),
                                      cum[:, bass.ds(c * P, P)], start=False, stop=True)
                        last.then_inc(seg_done, 1)

                    fill(p0, p0 + 4)
                    pe.wait_ge(chunk_staged, 3 * c + 3)
                    for g in range(GROUPS):
                        last = mm(bank[4][:, g * P:(g + 1) * P], b_c[:, g, :], c_c[:, g, :], start=True, stop=True)
                    last.then_inc(cb_done, 1)
                    seg(0)
                    seg(1)
                    fill(p0 + 4, p0 + 7)
                    for q in (2, 3):
                        pe.wait_ge(decayed, 4 * c + q - 1)
                        seg(q)
                    fill(p0 + 7, p0 + 10)
                    for g in range(GROUPS):
                        pe.wait_ge(mixed_ready, 2 * c + g + 1)
                        for h in range(8):
                            last = mm(bank[5 + g][:, h * HEAD:(h + 1) * HEAD], decay[:, 8 * g + h, :],
                                      x_dt[:, (8 * g + h) * HEAD:(8 * g + h + 1) * HEAD], start=True, stop=True)
                        if g == 0:
                            fill(p0 + 10, p0 + 12)
                    pe.wait_ge(state_ready, 2 * c + 2)
                    for g in range(GROUPS):
                        last = mm(bank[2 + g][:, :], c_c[:, g, :], state[:, g * 512:(g + 1) * 512], start=True, stop=True)
                    last.then_inc(y_done, 1)
                    for g in range(GROUPS):
                        last = mm(bank[4 + 3 * g][:, :], bt_c[:, g * P:(g + 1) * P], x_out[:, g * 512:(g + 1) * 512],
                                  start=True, stop=True)
                    last.then_inc(state_done, 1)
                    fill(p0 + 12, p0 + 16)

            stream("v", token_k, A, after=lambda j: pe.wait_ge(y_step, 4 * TT - 1) if j == 1 else None)
            for m in range(KT):
                if m == 0:
                    pe.wait_ge(y_norm, 8)
                if m >= 4:
                    pe.wait_ge(ssd_lo, m - 3)
                for t in range(TT):
                    last = tr(bank[4 + m % 4][:, t * P:(t + 1) * P], z_tok[:, t * D + m * P:t * D + (m + 1) * P], ident)
                last.then_inc(y_turned, 1)

            attention("1", "wo_ssd", feature_k, Y, ready=wait_tiles(ssd_lo))
            for m in range(4):
                turn_attention("1", m)

            for s in range(2):
                pe.wait_ge(strip_split, FIRST["wo_att"] + s + 1)
                hi4 = w_hi[s].rearrange("p k n -> p (k n)").rearrange("p (k n) -> p k n", k=4)
                lo4 = w_lo[s].rearrange("p k n -> p (k n)").rearrange("p (k n) -> p k n", k=4)
                for j in range(4):
                    bank_free("wo_att", 4 * s + j)
                    cols = slice(j * P, (j + 1) * P)
                    for k in range(4):
                        if s == 0 and j == 0:
                            pe.wait_ge(att_lo, k + 1)
                        mm(bank[j][:, :], hi4[:, k, cols], b_hi[:, k, :], start=(k == 0), stop=False)
                        mm(bank[j][:, :], hi4[:, k, cols], b_lo[:, k, :], start=False, stop=False)
                        last = mm(bank[j][:, :], lo4[:, k, cols], b_hi[:, k, :], start=False, stop=(k == 3))
                    if j % 2:
                        last.then_inc(unit_done, 1)

            def ff_group(g, norm):
                stream("ff1_0", feature_k, A, ready=wait_tiles(NORMS["mlp"]["lo"]), strips=8 * g, fills=16 * g,
                       after=(lambda j: stat("mlp", sq_sum, STAT[0]) if j == 0 else None) if norm else None)
                stream("ff2_0", feature_k, B, ready=lambda k: pe.wait_ge(ff_lo, KT * g + k + 1), strips=8 * g, fills=16 * g)

            ff_group(0, True)
            with pe.Fori(1, FF_GROUPS) as g:
                ff_group(g, False)

            def after_qk2a(j):
                if j == 1:
                    stat("end1", sq_sum, STAT[0])
                    stat("mix2", sq_g_sum, STAT[1])
                    small_columns(1, A)
                if j == 3:
                    turn_rstd("mix2")
                if j == 5:
                    turn_small(1, "mix2")

            def after_v2a(j):
                if j == 1:
                    pe.wait_ge(sp_step, SP_END)
                    for t in range(TT):
                        last = mm(bank[7][0:16, t * P:T], sp["val"][:, t * 16:(t + 1) * 16], steps01[:, 0:T - t * P],
                                  start=(t == 0), stop=True, skip_group_check=(t > 0))
                    last.then_inc(cum_done, 1)

            stream("qk2a", feature_k, A, ready=wait_tiles(NORMS["mix2"]["lo"]), after=after_qk2a)
            stream("v2a", token_k, A, after=after_v2a)
            attention("2a", "zv", token_k, A)

            def after_u(j):
                if j == 0:
                    pe.wait_ge(key_masked, 2)
                    for h in range(2):
                        last = mm(bank[4 + h][:, :], ones, ws_t[:, 4 * h:4 * h + 4, :].rearrange("p g t -> p (g t)"),
                                  start=True, stop=True)
                    last.then_inc(row_sums, 1)

            stream("u", feature_k, A, after=after_u)

            def spatial(g):
                if g == 0:
                    pe.wait_ge(ln_ready, TT)
                if g >= 2:
                    pe.wait_ge(mix_read, g - 1)
                for t in range(TT):
                    last = mm(bank[6 + g % 2][:, t * P:(t + 1) * P], zv_tok[:, t * D + g * P:t * D + (g + 1) * P],
                              ws_t[:, g, :], start=True, stop=True)
                last.then_inc(mixed_done, 1)

            stream("qk2b", feature_k, A, after=spatial)
            stream("v2b", token_k, A)
            pe.wait_ge(mix_read, KT)
            attention("2b", "gate_b", feature_k, A)
            stream("gate_a", feature_k, A, after=lambda j: turn_attention("2", j))
            stream("branch_b", feature_k, B, ready=lambda k: pe.wait_ge(att_lo, 4 + k + 1))
            stream("branch_a", feature_k, A, ready=wait_tiles(amix_lo))
            stream("out2", feature_k, B, ready=wait_tiles(m_lo))

            def up_group(g, norm):
                stream("up0", feature_k, A, ready=wait_tiles(NORMS["ffn2"]["lo"]), strips=12 * g, fills=24 * g,
                       after=(lambda j: stat("ffn2", sq_sum, STAT[0]) if j == 0 else None) if norm else None)
                stream("down0", feature_k, B, ready=lambda k: pe.wait_ge(up_lo, KT * g + k + 1), strips=12 * g, fills=24 * g)

            up_group(0, True)
            with pe.Fori(1, UP_TILES // KT) as g:
                up_group(g, False)
            stream("up2", feature_k, A)
            stream("down2", feature_k, B, ready=lambda k: pe.wait_ge(up_lo, 2 * KT + k + 1), kt=UP_TILES % KT)

            pe.wait_ge(strip_split, FIRST["ple"] + 1)
            pe.wait_ge(p_lo_ready, 2)
            slot = FIRST["ple"] % 2
            hi2 = w_hi[slot].rearrange("p k n -> p (k n)").rearrange("p (k n) -> p k n", k=2)
            lo2 = w_lo[slot].rearrange("p k n -> p (k n)").rearrange("p (k n) -> p k n", k=2)
            for m in range(KT):
                bank_free("ple", m)
                cols = slice(m * P, (m + 1) * P)
                for k in range(2):
                    mm(bank[m % 4][:, :], hi2[:, k, cols], p_hi[:, k, :], start=(k == 0), stop=False)
                    mm(bank[m % 4][:, :], hi2[:, k, cols], p_lo[:, k, :], start=False, stop=False)
                    last = mm(bank[m % 4][:, :], lo2[:, k, cols], p_hi[:, k, :], start=False, stop=(k == 1))
                if m % 4 == 3:
                    last.then_inc(unit_done, 1)
            stream("gate", feature_k, A, ready=wait_tiles(NORMS["ple"]["lo"]),
                   after=lambda j: stat("ple", sq_sum, STAT[0]) if j == 0 else None)
            n = NORMS["end2"]
            pe.wait_ge(n["sum"], KT - 2)
            mm(STAT[1][:, :], ones, sq_sum, start=True, stop=False)
            pe.wait_ge(n["sq"], KT - 1)
            mm(STAT[1][:, :], ones, sq[KT % 2], start=False, stop=False)
            pe.wait_ge(n["sq"], KT)
            mm(STAT[1][:, :], ones, sq[(KT - 1) % 2], start=False, stop=True).then_inc(n["stat"], 1)

        @block.scalar
        def _(act):
            run = nc.scalar.activation
            act.dma_start(gains, d["gains"]).then_inc(gains_loaded, 16)
            def square(norm, m, total=sq_sum, parts=sq, scale=1.0):
                n = NORMS[norm]
                if m >= 3:
                    act.wait_ge(n["sum"], m - 1)
                run(parts[m % 2] if m else total, x[:, m, :], ACT.Square, scale=scale).then_inc(n["sq"], 1)

            def high(norm, m, gain, dst):
                run(dst[:, m, :], x[:, m, :], ACT.Copy, scale=gain[:, m:m + 1]).then_inc(NORMS[norm]["hi"], 1)

            def root(norm, where, scale=1.0):
                n = NORMS[norm]
                act.wait_ge(n["var"], 1)
                run(where, where, ACT.Sqrt, scale=scale).then_inc(n["std"], 1)

            def attention(call, evac):
                causal = call != "1"
                st = stage2 if causal else stage1

                def stage(head, part, q0, it):
                    if head >= 2 and part == 0:
                        act.wait_ge(scored, STEPS * q0 + TT * (head - 1))
                    parity, r = head % 2, HEAD * (head % 2)
                    mine, other = slice(r, r + HEAD), slice(HEAD - r, P - r)
                    name, rows, first = (("q1", mine, 0), ("k1", mine, 4), ("q1", other, 0), ("k2", mine, 4))[part]
                    run(st[name][parity][rows, :], qk[mine, bass.ds(it * (2 * T) + (first + head // 2) * T, T)],
                        ACT.Copy).then_inc(qk_staged, 1)

                def exps(n, q0):
                    w = P * (n % TT + 1)
                    act.wait_ge(maxed, STEPS * q0 + n + 1)
                    src = bank[2 + n % 2][:, 0:w] if causal else score[:, n % 3, 0:w]
                    run(score[:, n % 3, 0:w], src, ACT.Exp, bias=row_max[:, n:n + 1],
                        accum_out=row_sum[:, n:n + 1]).then_inc(exped, 1)

                def keep(n, q0):
                    w = P * (n % TT + 1)
                    act.wait_ge(turned, STEPS * q0 + n + 1)
                    if n >= 2:
                        act.wait_ge(pv_done, STEPS * q0 + n - 1)
                    run(prob_t[:, n % 2, 0:w], bank[4 + n % 2][:, 0:w], ACT.Copy).then_inc(prob_ready, 1)

                with act.Fori(0, 2) as it:
                    q0 = QUAD0[call] + it
                    for part in range(4):
                        stage(0, part, q0, it)
                    for n in range(SLOTS):
                        if n < STEPS:
                            exps(n, q0)
                        if 2 <= n < STEPS + 2:
                            keep(n - 2, q0)
                        if n < STEPS - TT:
                            for part in STAGE_PARTS[n % TT]:
                                stage(n // TT + 1, part, q0, it)
                        if evac is not None:
                            for j in slot_units(n):
                                evac(j, it)
                    act.wait_ge(att_out, STEPS * q0 + STEPS)

            def split_attention(blk, m):
                act.wait_ge(att_turned, ATT_T0[blk] + m + 1)
                run(b_hi[:, m, :], bank[4 + m % 4][:, :], ACT.Copy).then_inc(att_hi, 1)

            def token_evac(phase, j, ps, dst, width, it=None):
                act.wait_ge(unit_done, 2 * FIRST[phase] + j + 1 if it is None else 4 * it + 2 * FIRST[phase] + j + 1)
                for t in range(2):
                    tt = 2 * (j % 2) + t
                    at = tt * width + (j // 2) * STRIP
                    ins = run(dst[:, at:at + STRIP] if it is None else dst[:, bass.ds(it * 512 + at, STRIP)],
                              ps[:, t * STRIP:(t + 1) * STRIP], ACT.Copy, scale=rstd_tok[:, tt:tt + 1])
                ins.then_inc(act_evac, 1)

            def value_evac(phase):
                for j in range(FILLS[phase]):
                    token_evac(phase, j, bank[j % 4], v_tok, 512)

            act.wait_ge(gains_loaded, 16)
            run(exp_a[:, 0:1], gains[:, 0, 0:1], ACT.Copy).then_inc(act_evac, 2)
            for m in range(KT + 2):
                if m < KT:
                    act.wait_ge(x_loaded[m // 2], 16)
                    high("mix1", m, gains[:, 0, :], a_hi)
                if m >= 2:
                    square("mix1", m - 2)
            act.dma_start(conv1_w, d["conv1"]).then_inc(consts_loaded, 16)
            act.dma_start(conv2_w, d["conv2"]).then_inc(consts_loaded, 16)
            act.dma_start(heads1[:, 0, :], d["dt_bias"].partition_broadcast(P)).then_inc(consts_loaded, 16)
            act.dma_start(heads1[:, 1, :], d["a_log"].partition_broadcast(P)).then_inc(consts_loaded, 16)
            act.dma_start(heads1[:, 2, :], d["d_skip"].partition_broadcast(P)).then_inc(consts_loaded, 16)
            act.dma_start(bf2, d["b_f"].partition_broadcast(P)).then_inc(consts_loaded, 16)
            for j in range(2):
                act.dma_start(w16_raw[:, j], d["w16"][j]).then_inc(consts_loaded, 16)
            root("mix1", rstd)
            act.wait_ge(consts_loaded, 16 * N_CONST)
            for j in range(2):
                if j == 0:
                    act.wait_ge(w16_ready, 1)
                run(w16[:, j, :, 0:16], w16_raw[:, j], ACT.Copy).then_inc(w16_hi_ready, 1)
            run(exp_a, heads1[:, 1, :], ACT.Exp).then_inc(cum_act, 1)

            def keep_xs(m):
                act.wait_ge(xs_turned, m + 1)
                src = bank[4 + m % 2][:, :].rearrange("p (t f) -> p t f", t=TT)
                if m < 8:
                    dst = xs_tok.rearrange("p (t f) -> p t f", t=TT)[:, :, m * P:(m + 1) * P]
                else:
                    dst = b_tok[:, :, (m - 8) * P:(m - 7) * P]
                run(dst, src, ACT.Copy).then_inc(xs_ready, 1)

            for m in range(NXBC):
                act.wait_ge(dve_evac, EVAC0["xbc"] + m + 1)
                if m >= 2:
                    act.wait_ge(conv_silu, m - 1)
                run(conv[m % 2], u_pad[m % 2][:, 0:T], ACT.Identity, bias=conv1_w[:, m, CONV1:CONV1 + 1],
                    scale=conv1_w[:, m, 0:1]).then_inc(tap0, 1)
                act.wait_ge(taps, 3 * m + 3)
                if 2 <= m < 8:
                    act.wait_ge(xs_turned, m - 1)
                run(xs_t[m % 2] if m < 8 else bc_t[:, m - 8, :], conv[m % 2], ACT.Silu).then_inc(conv_silu, 1)
                if m >= 3:
                    keep_xs(m - 3)
            keep_xs(9)

            def log_exp(k):
                act.wait_ge(small_done, 2 * k + 1)
                run(small_t, bank[6][0:48, :], ACT.Copy).then_inc(sp_exp, 1)
                act.wait_ge(sp_step, SP_A * k + 3)
                run(sp["e"], sp["na"], ACT.Exp).then_inc(sp_exp, 1)

            log_exp(0)
            act.wait_ge(cum_dve, 2)
            run(sp["eac"], bank[6][:, 0:64], ACT.Exp).then_inc(cum_act, 1)
            run(sp["cdec"], bank[6][:, 64:128], ACT.Exp).then_inc(cum_act, 1)
            act.wait_ge(cum_dve, 3)
            run(sp["dout"], sp["diff"], ACT.Exp).then_inc(sp_exp, 1)

            with act.Fori(0, TT // 2) as it:
                for half in range(2):
                    c = 2 * it + half
                    for q in range(4):
                        act.wait_ge(seg_done, 4 * c + q + 1)
                        for h in range(4):
                            ins = run(decay[:, 4 * q + h, :], bank[2 + q % 2][:, h * P:(h + 1) * P], ACT.Exp,
                                      bias=sp["nacum"][:, bass.ds(c * 16 + 4 * q + h, 1)])
                        ins.then_inc(decayed, 1)
                    token_evac("z", 2 * half, bank[0], z_tok, D, it)
                    act.wait_ge(y_done, c + 1)
                    token_evac("z", 2 * half + 1, bank[1], z_tok, D, it)
            act.wait_ge(y_step, 4 * TT)
            act.dma_start(head_bias.rearrange("p (h m) -> p h m", h=H1), d["rel"].rearrange("h p m -> p h m")).then_inc(late_loaded, 16)
            act.wait_ge(act_evac, EVAC0["z"] + FILLS["z"])
            for t in range(TT):
                run(z_tok[:, t * D:(t + 1) * D], z_tok[:, t * D:(t + 1) * D], ACT.Silu).then_inc(z_silu, 1)

            def group_squares(t):
                act.wait_ge(y_gated, t + 1)
                for n in (2 * t, 2 * t + 1):
                    if n >= 4:
                        act.wait_ge(y_sq, n - 3)
                    run(unused[n % 4], z_tok[:, n * 512:(n + 1) * 512], ACT.Square,
                        accum_out=stats[:, 0, n:n + 1]).then_inc(y_sq, 1)

            group_squares(0)
            group_squares(1)
            token_evac("v", 0, bank[0], v_tok, 512)
            group_squares(2)
            group_squares(3)
            act.wait_ge(y_stat, 1)
            run(stats[:, 2, :], stats[:, 1, :], ACT.Sqrt).then_inc(y_std, 1)
            for j in range(1, 4):
                token_evac("v", j, bank[j], v_tok, 512)
            for m in range(KT):
                act.wait_ge(y_turned, m + 1)
                run(y_hi[:, m, :], bank[4 + m % 4][:, :], ACT.Copy, scale=gains[:, 1, m:m + 1]).then_inc(ssd_hi, 1)
            act.wait_ge(dve_evac, EVAC0["qk"] + 8)
            attention("1", None)
            for m in range(4):
                split_attention("1", m)

            for m in range(KT):
                act.wait_ge(dve_evac, EVAC0["wo_att"] + m + 1)
                high("mlp", m, gains[:, 2, :], a_hi)
                square("mlp", m)
            root("mlp", rstd)

            def ff_group(g):
                for j in range(KT):
                    act.wait_ge(dve_evac, EVAC0["ff1_0"] + 16 * g + j + 1)
                    if j >= 2:
                        act.wait_ge(ff_lo, KT * g + j - 1)
                    run(relu2[j % 2], relu[j % 2], ACT.Square)
                    if j == 0:
                        act.wait_ge(unit_done, 2 * FIRST["ff1_0"] + 16 * g)
                    run(b_hi[:, j, :], relu[j % 2], ACT.Square).then_inc(ff_hi, 1)
                act.wait_ge(ff_lo, KT * g + KT)

            with act.Fori(0, FF_GROUPS) as g:
                ff_group(g)
            act.wait_ge(dve_start_step, 3)
            for m in range(KT):
                act.wait_ge(dve_evac, EVAC0[f"ff2_{FF_GROUPS - 1}"] + m + 1)
                high("mix2", m, gain12, a_hi)
                square("end1", m)
                square("mix2", m, sq_g_sum, sq_g, gains[:, 3, m:m + 1])
            act.wait_ge(unit_done, 2 * FIRST["qk2a"])
            act.dma_start(ws_t, d["ws_t"]).then_inc(late_loaded, 16)
            act.dma_start(shift.rearrange("p g t -> p (g t)"), d["bs"].partition_broadcast(P)).then_inc(late_loaded, 16)
            root("mix2", rstd, 1.0 / D)
            root("end1", rstd1)
            log_exp(1)

            value_evac("v2a")
            act.wait_ge(dve_evac, EVAC0["qk2a"] + 8)
            attention("2a", lambda j, it: token_evac("zv", j, bank[j % 2], zv_tok, D, it))
            act.wait_ge(act_evac, EVAC0["zv"] + FILLS["zv"])
            for t in range(TT):
                zt = zv_tok[:, t * D:(t + 1) * D]
                run(zt, zt, ACT.Gelu_apprx_tanh, accum_out=stats[:, 0, t:t + 1]).then_inc(zv_gelu, 1)
            act.wait_ge(ln_step, 1)
            for t in range(TT):
                if t >= 2:
                    act.wait_ge(ln_sq, t - 1)
                run(sq_wide[t % 2], zv_tok[:, t * D:(t + 1) * D], ACT.Square, bias=stats[:, 1, t:t + 1],
                    accum_out=stats[:, 0, 4 + t:5 + t]).then_inc(ln_sq, 1)
            act.wait_ge(ln_step, 2)
            run(stats[:, 2, 0:4], stats[:, 1, 4:8], ACT.Sqrt).then_inc(ln_std, 1)
            for m in range(KT):
                act.wait_ge(dve_evac, EVAC0["u"] + m + 1)
                ut = u_t[:, m * T:(m + 1) * T]
                run(ut, ut, ACT.Gelu_apprx_tanh).then_inc(ug, 1)
            value_evac("v2b")
            act.wait_ge(dve_evac, EVAC0["qk2b"] + 8)
            attention("2b", None)

            def sigmoids(phase, where):
                for j in range(KT):
                    act.wait_ge(dve_evac, EVAC0[phase] + j + 1)
                    part = where[:, j * T:(j + 1) * T]
                    run(part, part, ACT.Sigmoid).then_inc(gated, 1)

            sigmoids("gate_b", merged)
            for m in range(KT):
                split_attention("2", m)
            sigmoids("gate_a", gate_t)
            for g in range(KT):
                act.wait_ge(a_ready, g + 1)
                if g == 0:
                    act.wait_ge(unit_done, 2 * FIRST["branch_b"])
                run(a_hi[:, g, :], u_t[:, g * T:(g + 1) * T], ACT.Copy).then_inc(amix_hi, 1)
            for m in range(KT):
                act.wait_ge(merged_ready, m + 1)
                if m == 0:
                    act.wait_ge(unit_done, 2 * FIRST["branch_a"])
                run(b_hi[:, m, :], merged[:, m * T:(m + 1) * T], ACT.Copy).then_inc(m_hi, 1)
            for m in range(KT):
                act.wait_ge(dve_evac, EVAC0["out2"] + m + 1)
                high("ffn2", m, gains[:, 5, :], a_hi)
                square("ffn2", m)
            root("ffn2", rstd)
            act.dma_start(p_raw, d["p_t"]).then_inc(late_loaded, 16)

            def up_group(g, tiles):
                for i in range(tiles // 2):
                    for q in range(4):
                        half, tile = q // 2, 2 * i + q % 2
                        fill = 4 * i + q
                        act.wait_ge(dve_evac, EVAC0["up0"] + 24 * g + fill + 1)
                        if i:
                            act.wait_ge(up_gelu if half == 0 else up_act, KT * g + tile - 1)
                        at = KT * g + half * UP_TILES + tile
                        flat = conv2_w.rearrange("p w c -> p (w c)")
                        run(up_c[q], up_pad[q][:, 0:T], ACT.Identity, bias=flat[:, bass.ds(at * (CONV2 + 1) + CONV2, 1)],
                            scale=flat[:, bass.ds(at * (CONV2 + 1), 1)]).then_inc(up_tap0, 1)
                        if half == 0:
                            act.wait_ge(up_taps, 2 * (2 * KT * g + fill) + 2)
                            if i:
                                act.wait_ge(up_lo, KT * g + tile - 1)
                            run(up_g[q], up_c[q], ACT.Gelu_apprx_tanh).then_inc(up_gelu, 1)
                        else:
                            act.wait_ge(up_act, KT * g + tile + 1)
                            if i == 0 and q == 2:
                                act.wait_ge(unit_done, 2 * FIRST["up0"] + 24 * g)
                            run(b_hi[:, tile, :], up_g[q - 2], ACT.Copy).then_inc(up_hi, 1)
                act.wait_ge(up_lo, KT * g + tiles)

            with act.Fori(0, UP_TILES // KT) as g:
                up_group(g, KT)
            up_group(UP_TILES // KT, UP_TILES % KT)
            act.wait_ge(late_loaded, 64)
            for k in range(2):
                run(p_hi[:, k, :], p_raw[:, k, :], ACT.Copy).then_inc(p_hi_ready, 1)
            for m in range(KT):
                act.wait_ge(dve_evac, EVAC0["down2"] + m + 1)
                high("ple", m, gains[:, 6, :], a_hi)
                square("ple", m)
            for m in range(KT):
                act.wait_ge(unit_done, 2 * FIRST["ple"] + m // 4 + 1)
                run(ple_t[:, m * T:(m + 1) * T], bank[m % 4][:, :], ACT.Copy).then_inc(act_evac, 1)
            root("ple", rstd)

            def last_gain(m):
                act.wait_ge(NORMS["end2"]["sq"], m + 1)
                run(x[:, m, :], x[:, m, :], ACT.Copy, scale=gains[:, 7, m:m + 1]).then_inc(x_scaled_out, 1)

            for m in range(KT):
                act.wait_ge(dve_evac, EVAC0["gate"] + m + 1)
                run(sig[m % 2], sig[m % 2], ACT.Sigmoid).then_inc(ple_sig, 1)
                if m:
                    act.wait_ge(ple_mul, 2 * m)
                    square("end2", m - 1)
                if m >= 2:
                    last_gain(m - 2)
            act.wait_ge(ple_mul, 2 * KT)
            square("end2", KT - 1)
            last_gain(KT - 2)
            root("end2", rstd)
            last_gain(KT - 1)

        @block.vector
        def _(dve):
            v = nc.vector

            def add_square(norm, m, total=sq_sum, parts=sq):
                n = NORMS[norm]
                dve.wait_ge(n["sq"], m + 1)
                if m == 0:
                    v.tensor_copy(total[:, 0:1], total[:, 0:1]).then_inc(n["sum"], 1)
                else:
                    dve.wait_ge(n["sum"], m)
                    v.tensor_tensor(total, total, parts[m % 2], ALU.add).then_inc(n["sum"], 1)

            def low(norm, m, gain, dst):
                hi, lo = dst
                n = NORMS[norm]
                dve.wait_ge(n["hi"], m + 1)
                v.scalar_tensor_tensor(lo[:, m, :], x[:, m, :], gain[:, m:m + 1], hi[:, m, :].bitcast(F32),
                                       ALU.mult, ALU.subtract).then_inc(n["lo"], 1)

            def inverse_rms(norm, e, where=STAT[0], to=rstd):
                n = NORMS[norm]
                dve.wait_ge(n["stat"], 1)
                v.tensor_scalar(to, where[:, :], 1.0 / D, e, ALU.mult, ALU.add).then_inc(n["var"], 1)
                dve.wait_ge(n["std"], 1)
                v.reciprocal(to, to).then_inc(n["rstd"], 1)
                dve.wait_ge(n["rstd"], 1)

            def rstd_by_token(norm):
                n = NORMS[norm]
                dve.wait_ge(n["turned"], 1)
                v.tensor_copy(rstd_tok, bank[7][:, :].rearrange("p (t c) -> p t c", t=TT)[:, :, 0]).then_inc(n["tok"], 1)
                dve.wait_ge(n["tok"], 1)

            def scaled_evac(phase, j, dst, scale=None, ps=None, rounds=0):
                dve.wait_ge(unit_done, 2 * FIRST[phase] + j + 1 + rounds)
                src = (bank[j % 4] if ps is None else ps)[:, :]
                if scale is None:
                    ins = v.tensor_tensor(dst, src, rstd, ALU.mult)
                else:
                    ins = v.scalar_tensor_tensor(dst, src, scale, rstd, ALU.mult, ALU.mult)
                ins.then_inc(dve_evac, 1)

            def add_x(phase, j, m, unit=None, rounds=0):
                dve.wait_ge(unit_done, 2 * FIRST[phase] + (j if unit is None else unit) + 1 + rounds)
                v.tensor_tensor(x[:, m, :], x[:, m, :], bank[j % 4][:, :], ALU.add).then_inc(dve_evac, 1)

            sp_n = [0]

            def sp_do(ins):
                sp_n[0] += 1
                ins.then_inc(sp_step, 1)
                dve.wait_ge(sp_step, sp_n[0])

            def small_logs(k, bias, forget):
                b3 = lambda a: a.unsqueeze(1).to_broadcast([P, TT, 16])
                t3 = lambda a: a.rearrange("p (t h) -> p t h", t=TT)
                dve.wait_ge(small_done, 2 * k + 2)
                sp_do(v.tensor_tensor(t3(sp["x"]), t3(bank[7][:, 0:64]), rstd_tok.unsqueeze(2).to_broadcast([P, TT, 16]), ALU.mult))
                sp_do(v.tensor_tensor(t3(sp["x"]), t3(sp["x"]), b3(bias), ALU.add))
                sp_do(v.scalar_tensor_tensor(sp["na"], sp["x"], -1.0, sp["x"], ALU.mult, ALU.min))
                dve.wait_ge(sp_exp, 3 * k + 2)
                sp_do(v.tensor_scalar(sp["d"], sp["e"], 2.0, None, ALU.add))
                sp_do(v.reciprocal(sp["r"], sp["d"]))
                sp_do(v.tensor_tensor(sp["s"], sp["e"], sp["r"], ALU.mult))
                sp_do(v.tensor_tensor(sp["q"], sp["s"], sp["s"], ALU.mult))
                sp_do(v.tensor_scalar(sp["p"], sp["q"], 1.0 / 15, 1.0 / 13, ALU.mult, ALU.add))
                sp_do(v.tensor_tensor(sp["p"], sp["p"], sp["q"], ALU.mult))
                for c in (11, 9, 7, 5, 3):
                    sp_do(v.scalar_tensor_tensor(sp["p"], sp["p"], 1.0 / c, sp["q"], ALU.add, ALU.mult))
                sp_do(v.scalar_tensor_tensor(sp["p"], sp["p"], 1.0, sp["s"], ALU.add, ALU.mult))
                sp_do(v.tensor_scalar(sp["m"], sp["x"], 0.0, None, ALU.min if forget else ALU.max))
                sp_do(v.scalar_tensor_tensor(sp["val"], sp["p"], -2.0 if forget else 2.0, sp["m"], ALU.mult, ALU.add))

            def split_cum(k, sign, dst, r):
                v.tensor_scalar(dst[r:r + 16, :], bank[7][0:16, :], sign, None, ALU.mult).then_inc(cum_ready, 1)
                dve.wait_ge(cum_ready, 2 * k + 1)
                v.scalar_tensor_tensor(dst[r + 32:r + 48, :], bank[7][0:16, :], sign, dst[r:r + 16, :].bitcast(F32),
                                       ALU.mult, ALU.subtract).then_inc(cum_ready, 1)

            def attention(call, evac):
                causal = call != "1"
                st = stage2 if causal else stage1

                def stage(head, part, q0, it):
                    if head >= 2 and part == 0:
                        dve.wait_ge(scored, STEPS * q0 + TT * (head - 1))
                    parity, r = head % 2, HEAD * (head % 2)
                    mine, other = slice(r, r + HEAD), slice(HEAD - r, P - r)
                    if part == 0:
                        if causal:
                            pick = sel.bitcast(F32)[other, bass.ds(it * QUAD + (8 if call == "2b" else 0) + head, 1)]
                        else:
                            pick = zeros[other, 0:1]
                        v.tensor_copy(st["q2"][parity][other, :], pick.to_broadcast([HEAD, T])).then_inc(lo_staged, 1)
                        return
                    src, dst = ("q1", st["q2"][parity][mine, :]) if part == 1 else ("k1", st["k1"][parity][other, :])
                    dve.wait_ge(qk_staged, 4 * QUAD * q0 + 4 * head + part)
                    rows = qk[mine, bass.ds(it * (2 * T) + (4 * (part - 1) + head // 2) * T, T)]
                    v.tensor_tensor(dst, rows, st[src][parity][mine, :].bitcast(F32), ALU.subtract).then_inc(lo_staged, 1)

                def most(n, q0, it):
                    head, w = n // TT, P * (n % TT + 1)
                    dve.wait_ge(scored, STEPS * q0 + n + 1)
                    src = bank[2 + n % 2][:, 0:w]
                    if not causal:
                        if n >= 3:
                            dve.wait_ge(turned, STEPS * q0 + n - 2)
                        dst = score[:, n % 3, 0:w]
                        v.tensor_tensor(dst, src, head_bias[:, bass.ds(it * (QUAD * T) + head * T + T - w, w)],
                                        ALU.add).then_inc(biased, 1)
                        dve.wait_ge(biased, STEPS * q0 + n + 1)
                        src = dst
                    v.tensor_reduce(row_max[:, n:n + 1], src, AX_X, ALU.max, negate=True).then_inc(maxed, 1)

                def keep(n, q0, it):
                    head, i = n // TT, n % TT
                    dve.wait_ge(exped, STEPS * q0 + n + 1)
                    v.reciprocal(row_inv[:, n:n + 1], row_sum[:, n:n + 1]).then_inc(inverted, 1)
                    dve.wait_ge(pv_done, STEPS * q0 + n + 1)
                    dve.wait_ge(inverted, STEPS * q0 + n + 1)
                    first = TT * 512 if call == "2b" else 0
                    v.tensor_scalar(att_tok[:, bass.ds(it * (QUAD * HEAD) + first + i * 512 + head * HEAD, HEAD)],
                                    bank[6 + n % 2][:, 0:HEAD], row_inv[:, n:n + 1], None, ALU.mult).then_inc(att_out, 1)

                with dve.Fori(0, 2) as it:
                    q0 = QUAD0[call] + it
                    for part in range(3):
                        stage(0, part, q0, it)
                    for n in range(SLOTS):
                        if n < STEPS:
                            most(n, q0, it)
                        if n < STEPS - TT and n % TT < 3:
                            stage(n // TT + 1, n % TT, q0, it)
                        if n >= 3:
                            keep(n - 3, q0, it)
                        if evac is not None:
                            for j in slot_units(n):
                                evac(j, it)

            def split_attention(blk, m):
                n = ATT_T0[blk] + m
                dve.wait_ge(att_hi, n + 1)
                v.tensor_tensor(b_lo[:, m, :], bank[4 + m % 4][:, :], b_hi[:, m, :].bitcast(F32), ALU.subtract).then_inc(att_lo, 1)

            dve.wait_ge(pool_start_step, 1)
            v.tensor_tensor(w_lo[0][:, 0:KT // 2], w_raw[0][:, 0:KT // 2], w_hi[0][:, 0:KT // 2].bitcast(F32),
                            ALU.subtract).then_inc(dve_start_step, 1)
            for m in range(KT):
                low("mix1", m, gains[:, 0, :], (a_hi, a_lo))
                if m >= 2:
                    add_square("mix1", m - 2)
            for m in range(KT - 2, KT):
                add_square("mix1", m)
            dve.wait_ge(hi_split, 1)
            v.tensor_tensor(w_lo[1][:, KT // 2:], w_raw[1][:, KT // 2:], w_hi[1][:, KT // 2:].bitcast(F32),
                            ALU.subtract).then_inc(dve_start_step, 1)
            inverse_rms("mix1", EPS1)
            v.memset(w16.bitcast(F32), 0.0).then_inc(w16_ready, 1)
            v.tensor_tensor(gain12, gains[:, 3, :], gains[:, 4, :], ALU.mult).then_inc(dve_start_step, 1)
            dve.wait_ge(masks_ready, 5)
            v.memset(sel.bitcast(F32), 0.0).then_inc(dve_start_step, 1)
            dve.wait_ge(dve_start_step, 4)
            for j in range(4):
                v.tensor_copy(sel[32 * j:32 * j + 16, :], ident[0:16, 0:16]).then_inc(dve_start_step, 1)

            for j in range(2):
                v.memset(u_pad[j][:, 0:CONV1 - 1], 0.0)
            for m in range(NXBC):
                if m >= 2:
                    dve.wait_ge(taps, 3 * m - 3)
                scaled_evac("xbc", m, u_pad[m % 2][:, CONV1 - 1:CONV1 - 1 + T])
                dve.wait_ge(tap0, m + 1)
                for j in range(1, CONV1):
                    if j > 1:
                        dve.wait_ge(taps, 3 * m + j - 1)
                    v.scalar_tensor_tensor(conv[m % 2], u_pad[m % 2][:, j:j + T], conv1_w[:, m, j:j + 1], conv[m % 2],
                                           ALU.mult, ALU.add).then_inc(taps, 1)
                if m == 3:
                    rstd_by_token("mix1")
                if m == 5:
                    for j in range(2):
                        dve.wait_ge(w16_hi_ready, j + 1)
                        v.tensor_tensor(w16[:, j, :, 32:48], w16_raw[:, j], w16[:, j, :, 0:16].bitcast(F32),
                                        ALU.subtract).then_inc(w16_ready, 1)

            def qk_evac(phase, first, last):
                for j in range(first, last):
                    scaled_evac(phase, j, qk[:, j * T:(j + 1) * T], HEAD ** -0.5 if j < 4 else None)

            qk_evac("qk", 0, 2)
            v.memset(cum.bitcast(F32), 0.0).then_inc(cum_dve, 1)
            small_logs(0, heads1[:, 0, :], forget=False)
            dve.wait_ge(cum_act, 1)
            t3 = lambda a: a.rearrange("p (t h) -> p t h", t=TT)
            sp_n[0] += 1
            v.scalar_tensor_tensor(t3(sp["a"]), t3(sp["val"]), -1.0, exp_a.unsqueeze(1).to_broadcast([P, TT, 16]),
                                   ALU.mult, ALU.mult).then_inc(sp_step, 1)
            qk_evac("qk", 2, 6)
            dve.wait_ge(cum_done, 1)
            v.tensor_scalar(sp["nacum"], bank[6][:, 0:64], -1.0, None, ALU.mult).then_inc(cum_dve, 1)
            split_cum(0, 1.0, cum, 0)
            dve.wait_ge(cum_dve, 2)
            dve.wait_ge(cum_act, 3)
            v.tensor_tensor(sp["diff"], bank[6][:, 64:128], sp["nacum"], ALU.add).then_inc(cum_dve, 1)
            qk_evac("qk", 6, 8)
            dve.wait_ge(sp_exp, 3)

            h3 = lambda a, g=None: (a if g is None else a[:, g * 512:(g + 1) * 512]).rearrange("p (h f) -> p h f", f=HEAD)
            for g in range(GROUPS):
                v.memset(state[:, g * 512:(g + 1) * 512], 0.0).then_inc(state_ready, 1)
            dve.wait_ge(state_ready, 2)
            dve.wait_ge(xs_ready, 10)
            dve.wait_ge(conv_silu, NXBC)

            def by_head(a, c, h0, n):
                return a[:, bass.ds(c * 16 + h0, n)].unsqueeze(2).to_broadcast([P, n, HEAD])

            with dve.Fori(0, TT) as c:
                bc_flat = bc_t.rearrange("p m t -> p (m t)")
                for g in range(GROUPS):
                    ins = v.tensor_copy(b_c[:, g, :], bc_flat[:, bass.ds(c * P + g * T, P)])
                ins.then_inc(chunk_staged, 1)
                for g in range(GROUPS):
                    ins = v.tensor_copy(c_c[:, g, :], bc_flat[:, bass.ds(c * P + (2 + g) * T, P)])
                ins.then_inc(chunk_staged, 1)
                v.tensor_copy(bt_c, b_tok.rearrange("p t f -> p (t f)")[:, bass.ds(c * 256, 256)]).then_inc(chunk_staged, 1)
                xs_c = xs_tok[:, bass.ds(c * D, D)]
                v.tensor_tensor(h3(x_dt), h3(xs_c), by_head(sp["val"], c, 0, 16), ALU.mult).then_inc(x_scaled, 1)
                dve.wait_ge(x_scaled, 2 * c + 1)
                v.tensor_tensor(h3(x_out), h3(x_dt), by_head(sp["dout"], c, 0, 16), ALU.mult).then_inc(x_scaled, 1)
                v.tensor_tensor(h3(x_skip), h3(xs_c), heads1[:, 2, :].unsqueeze(2).to_broadcast([P, 16, HEAD]), ALU.mult).then_inc(y_step, 1)
                dve.wait_ge(cb_done, c + 1)
                for g in range(GROUPS):
                    dve.wait_ge(decayed, 4 * c + 2 * g + 2)
                    v.tensor_tensor(decay[:, 8 * g:8 * g + 8, :], decay[:, 8 * g:8 * g + 8, :],
                                    bank[4][:, g * P:(g + 1) * P].unsqueeze(1).to_broadcast([P, 8, P]), ALU.mult).then_inc(mixed_ready, 1)
                dve.wait_ge(y_done, c + 1)
                for g in range(GROUPS):
                    ins = v.tensor_tensor(h3(y_tmp, g), h3(bank[2 + g][:, :]), by_head(sp["eac"], c, 8 * g, 8), ALU.mult)
                ins.then_inc(y_step, 1)
                dve.wait_ge(y_step, 4 * c + 2)
                for g in range(GROUPS):
                    ins = v.tensor_tensor(y_tmp[:, g * 512:(g + 1) * 512], y_tmp[:, g * 512:(g + 1) * 512], bank[5 + g][:, :], ALU.add)
                ins.then_inc(y_step, 1)
                dve.wait_ge(state_done, c + 1)
                v.tensor_tensor(h3(state), h3(state), by_head(sp["cdec"], c, 0, 16), ALU.mult).then_inc(state_step, 1)
                dve.wait_ge(state_step, c + 1)
                for g in range(GROUPS):
                    v.tensor_tensor(state[:, g * 512:(g + 1) * 512], state[:, g * 512:(g + 1) * 512], bank[4 + 3 * g][:, :],
                                    ALU.add).then_inc(state_ready, 1)
                dve.wait_ge(y_step, 4 * c + 3)
                v.tensor_tensor(xs_c, y_tmp, x_skip, ALU.add).then_inc(y_step, 1)
                dve.wait_ge(state_ready, 2 * c + 4)
            dve.wait_ge(y_step, 4 * TT)
            for t in range(TT):
                zt = z_tok[:, t * D:(t + 1) * D]
                dve.wait_ge(z_silu, t + 1)
                v.tensor_tensor(zt, zt, xs_tok[:, t * D:(t + 1) * D], ALU.mult).then_inc(y_gated, 1)
            dve.wait_ge(y_sq, 8)
            v.tensor_scalar(stats[:, 1, :], stats[:, 0, :], 1.0 / 512, EPS1, ALU.mult, ALU.add).then_inc(y_stat, 1)
            dve.wait_ge(y_std, 1)
            v.reciprocal(stats[:, 0, :], stats[:, 2, :]).then_inc(y_stat, 1)
            dve.wait_ge(y_stat, 2)
            dve.wait_ge(y_gated, TT)
            for n in range(8):
                v.tensor_scalar(z_tok[:, n * 512:(n + 1) * 512], z_tok[:, n * 512:(n + 1) * 512], stats[:, 0, n:n + 1], None,
                                ALU.mult).then_inc(y_norm, 1)
            dve.wait_ge(late_loaded, 16)
            v.memset(head_bias.rearrange("p (h m) -> p h m", h=H1)[0:HEAD, :, T - HEAD:T], -BIG).then_inc(key_masked, 1)
            for m in range(KT):
                dve.wait_ge(ssd_hi, m + 1)
                v.scalar_tensor_tensor(y_lo[:, m, :], bank[4 + m % 4][:, :], gains[:, 1, m:m + 1], y_hi[:, m, :].bitcast(F32),
                                       ALU.mult, ALU.subtract).then_inc(ssd_lo, 1)

            def add_ssd(j, it):
                dve.wait_ge(unit_done, 4 * it + 2 * FIRST["wo_ssd"] + j + 1)
                xt = x.rearrange("p m t -> p (m t)")[:, bass.ds(it * (4 * T) + j * T, T)]
                v.tensor_tensor(xt, xt, bank[j % 2][:, :], ALU.add).then_inc(dve_evac, 1)

            dve.wait_ge(key_masked, 1)
            dve.wait_ge(dve_evac, EVAC0["qk"] + 8)
            for parity in range(2):
                r = HEAD * (1 - parity)
                v.memset(stage1["k2"][parity].bitcast(F32)[r:r + HEAD, :], 0.0)
            attention("1", add_ssd)
            for m in range(4):
                split_attention("1", m)
            for m in range(KT):
                dve.wait_ge(dve_evac, EVAC0["wo_ssd"] + m + 1)
                add_x("wo_att", m, m, unit=m // 2)
                low("mlp", m, gains[:, 2, :], (a_hi, a_lo))
                add_square("mlp", m)
            inverse_rms("mlp", EPS1)

            def ff_group(g, last=False):
                for j in range(KT):
                    n = KT * g + j
                    dve.wait_ge(unit_done, 2 * FIRST["ff1_0"] + 16 * g + j + 1)
                    v.scalar_tensor_tensor(relu[j % 2], bank[j % 4][:, :], 0.0, rstd, ALU.max, ALU.mult).then_inc(dve_evac, 1)
                    dve.wait_ge(ff_hi, n + 1)
                    v.tensor_tensor(b_lo[:, j, :], relu2[j % 2], b_hi[:, j, :].bitcast(F32), ALU.subtract).then_inc(ff_lo, 1)
                for m in range(KT):
                    dve.wait_ge(dve_evac, EVAC0["ff1_0"] + 16 * g - 8 + m + 1)
                    add_x("ff2_0", m, m, rounds=16 * g)
                    if last:
                        low("mix2", m, gain12, (a_hi, a_lo))
                        add_square("end1", m)
                        add_square("mix2", m, sq_g_sum, sq_g)

            with dve.Fori(0, FF_GROUPS - 1) as g:
                ff_group(g)
            ff_group(FF_GROUPS - 1, last=True)

            n1, n2 = NORMS["end1"], NORMS["mix2"]
            dve.wait_ge(n1["stat"], 1)
            v.tensor_scalar(rstd1, STAT[0][:, :], 1.0 / D, EPS1, ALU.mult, ALU.add).then_inc(n1["var"], 1)
            dve.wait_ge(n2["stat"], 1)
            dve.wait_ge(n1["var"], 1)
            v.scalar_tensor_tensor(rstd, rstd1, EPS2 * D, STAT[1][:, :], ALU.mult, ALU.add).then_inc(n2["var"], 1)
            dve.wait_ge(n2["std"], 1)
            v.reciprocal(rstd, rstd).then_inc(n2["rstd"], 1)
            dve.wait_ge(n2["rstd"], 1)
            qk_evac("qk2a", 0, 2)
            rstd_by_token("mix2")
            qk_evac("qk2a", 2, 4)
            dve.wait_ge(n1["std"], 1)
            v.reciprocal(rstd1, rstd1).then_inc(n1["rstd"], 1)
            dve.wait_ge(n1["rstd"], 1)
            for m in range(KT):
                v.scalar_tensor_tensor(x[:, m, :], x[:, m, :], gains[:, 3, m:m + 1], rstd1, ALU.mult, ALU.mult).then_inc(x_normed, 1)
                if m in (1, 5):
                    qk_evac("qk2a", 4 + m // 4, 5 + m // 4)
            small_logs(1, bf2, forget=True)
            qk_evac("qk2a", 6, 8)
            for parity in range(2):
                rows = slice(HEAD * (1 - parity), HEAD * (1 - parity) + HEAD)
                v.memset(stage2["k2"][parity].bitcast(F32)[rows, :], 0.0).then_inc(cum_dve, 1)
            dve.wait_ge(cum_done, 2)
            dve.wait_ge(cum_dve, 5)
            for parity in range(2):
                r = HEAD * (1 - parity)
                split_cum(1 + parity, -1.0, stage2["k2"][parity], r)
            dve.wait_ge(dve_evac, EVAC0["qk2a"] + 8)
            dve.wait_ge(late_loaded, 48)
            v.memset(ws_t[HEAD:P, :, 0:HEAD], 0.0).then_inc(key_masked, 1)
            attention("2a", None)
            dve.wait_ge(zv_gelu, TT)
            v.tensor_scalar(stats[:, 1, 0:4], stats[:, 0, 0:4], -1.0 / D, None, ALU.mult).then_inc(ln_step, 1)

            def linear_u(first, last):
                for m in range(first, last):
                    scaled_evac("u", m, u_t[:, m * T:(m + 1) * T])

            linear_u(0, 1)
            dve.wait_ge(ln_sq, TT)
            v.tensor_scalar(stats[:, 1, 4:8], stats[:, 0, 4:8], 1.0 / D, EPS2, ALU.mult, ALU.add).then_inc(ln_step, 1)
            dve.wait_ge(ln_std, 1)
            v.reciprocal(stats[:, 2, 4:8], stats[:, 2, 0:4]).then_inc(ln_step, 1)
            linear_u(1, 2)
            dve.wait_ge(ln_step, 3)
            for t in range(TT):
                zt = zv_tok[:, t * D:(t + 1) * D]
                v.tensor_scalar(zt, zt, stats[:, 1, t:t + 1], stats[:, 2, 4 + t:5 + t], ALU.add, ALU.mult).then_inc(ln_ready, 1)
                linear_u(2 + t, 3 + t)
            dve.wait_ge(row_sums, 1)
            for g in range(KT):
                v.scalar_tensor_tensor(shift[:, g, :], bank[4 + g // 4][:, (g % 4) * P:(g % 4 + 1) * P], gains[:, 9, g:g + 1],
                                       shift[:, g, :], ALU.mult, ALU.add).then_inc(shift_ready, 1)
            linear_u(6, 8)
            t4 = lambda a: a.rearrange("p (t c) -> p t c", t=TT)
            dve.wait_ge(shift_ready, KT)
            for g in range(KT):
                qk_evac("qk2b", g, g + 1)
                dve.wait_ge(mixed_done, g + 1)
                v.scalar_tensor_tensor(t4(lin[g % 2]), t4(bank[6 + g % 2][:, :]), gains[:, 8, g:g + 1],
                                       shift[:, g, :].unsqueeze(1).to_broadcast([P, TT, P]), ALU.mult, ALU.add).then_inc(mix_read, 1)
                dve.wait_ge(mix_read, g + 1)
                dve.wait_ge(ug, g + 1)
                ut = u_t[:, g * T:(g + 1) * T]
                v.tensor_tensor(ut, ut, lin[g % 2], ALU.mult).then_inc(a_ready, 1)
            dve.wait_ge(dve_evac, EVAC0["qk2b"] + 8)

            def linear_gate_b(j, it):
                scaled_evac("gate_b", j, merged[:, bass.ds(it * (4 * T) + j * T, T)], ps=bank[j % 2], rounds=4 * it)

            attention("2b", linear_gate_b)
            for j in range(KT):
                scaled_evac("gate_a", j, gate_t[:, j * T:(j + 1) * T])
                split_attention("2", j)

            def low_a(g):
                dve.wait_ge(amix_hi, g + 1)
                v.tensor_tensor(a_lo[:, g, :], u_t[:, g * T:(g + 1) * T], a_hi[:, g, :].bitcast(F32), ALU.subtract).then_inc(amix_lo, 1)

            for j in range(KT):
                mt = merged[:, j * T:(j + 1) * T]
                dve.wait_ge(unit_done, 2 * FIRST["branch_b"] + j + 1)
                dve.wait_ge(gated, j + 1)
                v.tensor_tensor(mt, mt, bank[j % 4][:, :], ALU.mult).then_inc(dve_evac, 1)
                low_a(j)
            for j in range(KT):
                gt, mt = gate_t[:, j * T:(j + 1) * T], merged[:, j * T:(j + 1) * T]
                dve.wait_ge(unit_done, 2 * FIRST["branch_a"] + j + 1)
                dve.wait_ge(gated, KT + j + 1)
                v.tensor_tensor(gt, gt, bank[j % 4][:, :], ALU.mult).then_inc(dve_evac, 1)
                dve.wait_ge(dve_evac, EVAC0["branch_a"] + j + 1)
                v.tensor_tensor(mt, mt, gt, ALU.add).then_inc(merged_ready, 1)
                dve.wait_ge(m_hi, j + 1)
                v.tensor_tensor(b_lo[:, j, :], mt, b_hi[:, j, :].bitcast(F32), ALU.subtract).then_inc(m_lo, 1)
            dve.wait_ge(x_normed, KT)
            for m in range(KT):
                add_x("out2", m, m)
                low("ffn2", m, gains[:, 5, :], (a_hi, a_lo))
                add_square("ffn2", m)
            inverse_rms("ffn2", EPS2)

            for q in range(4):
                v.memset(up_pad[q][:, 0:CONV2 - 1], 0.0)

            def up_group(g, tiles, last=False):
                flat = conv2_w.rearrange("p w c -> p (w c)")
                for i in range(tiles // 2):
                    for q in range(4):
                        half, tile = q // 2, 2 * i + q % 2
                        fill = 4 * i + q
                        at = KT * g + half * UP_TILES + tile
                        scaled_evac("up0", fill, up_pad[q][:, CONV2 - 1:CONV2 - 1 + T], rounds=24 * g)
                        dve.wait_ge(up_tap0, 2 * KT * g + fill + 1)
                        for j in range(1, CONV2):
                            if j > 1:
                                dve.wait_ge(up_taps, 2 * (2 * KT * g + fill) + j - 1)
                            v.scalar_tensor_tensor(up_c[q], up_pad[q][:, j:j + T], flat[:, bass.ds(at * (CONV2 + 1) + j, 1)], up_c[q],
                                                   ALU.mult, ALU.add).then_inc(up_taps, 1)
                        if half == 1:
                            dve.wait_ge(up_gelu, KT * g + tile + 1)
                            dve.wait_ge(up_taps, 2 * (2 * KT * g + fill) + 2)
                            v.tensor_tensor(up_g[q - 2], up_g[q - 2], up_c[q], ALU.mult).then_inc(up_act, 1)
                            dve.wait_ge(up_hi, KT * g + tile + 1)
                            v.tensor_tensor(b_lo[:, tile, :], up_g[q - 2], b_hi[:, tile, :].bitcast(F32),
                                            ALU.subtract).then_inc(up_lo, 1)
                if last:
                    for k in range(2):
                        dve.wait_ge(p_hi_ready, k + 1)
                        v.tensor_tensor(p_lo[:, k, :], p_raw[:, k, :], p_hi[:, k, :].bitcast(F32), ALU.subtract).then_inc(p_lo_ready, 1)
                for m in range(KT):
                    dve.wait_ge(dve_evac, EVAC0["up0"] + 24 * g - 8 + m + 1)
                    if last:
                        add_x("down2", m, m)
                        low("ple", m, gains[:, 6, :], (a_hi, a_lo))
                        add_square("ple", m)
                    else:
                        add_x("down0", m, m, rounds=24 * g)

            with dve.Fori(0, UP_TILES // KT) as g:
                up_group(g, KT)
            up_group(UP_TILES // KT, UP_TILES % KT, last=True)
            inverse_rms("ple", EPS2)
            for m in range(KT):
                s_m = sig[m % 2]
                scaled_evac("gate", m, s_m)
                dve.wait_ge(ple_sig, m + 1)
                dve.wait_ge(act_evac, EVAC0["ple"] + m + 1)
                v.tensor_tensor(s_m, s_m, ple_t[:, m * T:(m + 1) * T], ALU.mult).then_inc(ple_mul, 1)
                dve.wait_ge(ple_mul, 2 * m + 1)
                v.tensor_tensor(x[:, m, :], x[:, m, :], s_m, ALU.add).then_inc(ple_mul, 1)
                if 1 <= m < KT - 1:
                    add_square("end2", m - 1)
            inverse_rms("end2", EPS2, STAT[1])
            for m in range(KT - POOL_OUT):
                dve.wait_ge(x_scaled_out, m + 1)
                v.tensor_tensor(out_t[m], x[:, m, :], rstd, ALU.mult).then_inc(out_ready, 1)


def by_k(w):
    kt, n = w.shape[0] // P, w.shape[1] // STRIP
    return w.reshape(kt, P, n, STRIP).transpose(2, 1, 0, 3).reshape(n, P, kt * STRIP)


def kernel(**inputs):
    import concourse.bacc as bacc
    from concourse import mybir as _mybir
    from concourse.bass_utils import run_bass_kernel_spmd

    g = {k: np.asarray(v) for k, v in inputs.items()}
    w_in, w_out, ff1, ff2 = g["w_in"][0], g["w_out"][0], g["w_ff1"][0], g["w_ff2"][0]
    w_in2, up, down = g["w_in_2"][0], g["w_up_2"][0], g["w_down_2"][0]
    strips = [by_k(w_in[:, 2560:4096]), by_k(w_in[:, 0:1024]), by_k(w_in[:, 1536:2560]), by_k(w_in[:, 1024:1536])]
    strips += [by_k(w_out[512:]), w_out[0:512].reshape(4, P, 2, 512).transpose(2, 1, 0, 3).reshape(2, P, SW)]
    for j in range(FF_GROUPS):
        strips += [by_k(ff1[:, j * D:(j + 1) * D]), by_k(ff2[j * D:(j + 1) * D])]
    for j in range(2):
        for first in (2048, 3072, 4096):
            strips.append(by_k(w_in2[:, first + j * 512:first + (j + 1) * 512]))
        if j == 0:
            strips += [by_k(w_in2[:, 1024:2048]), by_k(w_in2[:, 0:1024])]
    strips += [by_k(w_in2[:, 6160:7184]), by_k(w_in2[:, 5136:6160])]
    strips += [by_k(g["w_branch_b_2"][0]), by_k(g["w_branch_a_2"][0]), by_k(g["w_out_2"][0])]
    half = UP_TILES * P
    ups = np.stack([by_k(up[:, 0:half]), by_k(up[:, half:])], axis=1).reshape(-1, P, SW)
    padded = np.concatenate([down, np.zeros((3 * D - half, D), down.dtype)])
    for j in range(3):
        strips += [ups[8 * j:8 * j + 8], by_k(padded[j * D:(j + 1) * D])]
    strips += [g["w_ple_2"][0].reshape(2, P, D).transpose(1, 0, 2).reshape(1, P, SW), by_k(g["w_ple_gate_2"][0])]

    def by_tile(v):
        return v.reshape(-1, P).T

    def sixteen(w):
        return w.reshape(KT, P, 16).transpose(1, 0, 2)

    gains = [g["norm_mix_w"], g["ssd_norm_w"], g["norm_mlp_w"], g["norm_final_w"], g["norm_mix_g_2"], g["norm_ffn_g_2"],
             g["norm_ple_g_2"], g["norm_final_g_2"], g["gmlp_ln_g_2"], g["gmlp_ln_b_2"]]
    taps1 = np.concatenate([g["conv_w"][0], g["conv_b"]])
    taps2 = np.concatenate([g["conv_w_2"][0], g["conv_b_2"]])
    dist = np.clip(T - P + np.arange(P)[:, None] - np.arange(T)[None, :], -REL, REL) + REL
    arrays = {
        "x_t": g["x"][0].T.reshape(KT, P, T).transpose(1, 0, 2),
        "strips": np.concatenate(strips),
        "gains": np.stack([by_tile(v) for v in gains], axis=1),
        "conv1": taps1.reshape(CONV1 + 1, NXBC, P).transpose(2, 1, 0),
        "conv2": taps2.reshape(CONV2 + 1, 2 * UP_TILES, P).transpose(2, 1, 0),
        "dt_bias": g["dt_bias"][0], "a_log": g["a_log"][0], "d_skip": g["d_skip"][0], "b_f": g["b_f_2"][0],
        "w16": np.stack([sixteen(w_in[:, 4096:4112]), sixteen(w_in2[:, 5120:5136])]),
        "ws_t": g["gmlp_w_s_2"][0].transpose(2, 0, 1), "bs": g["gmlp_b_s_2"][0].reshape(-1),
        "rel": g["rel_bias"][0].T[:, dist],
        "p_t": g["p_2"][0, 0].T.reshape(2, P, T).transpose(1, 0, 2),
    }
    nc = bacc.Bacc("TRN2", target_bir_lowering=False, num_devices=1)
    feed, aps = {}, {}
    for name, a in arrays.items():
        feed[f"in_{name}"] = np.ascontiguousarray(a)
        aps[name] = nc.dram_tensor(f"in_{name}", a.shape, _mybir.dt.from_np(a.dtype), kind="ExternalInput").ap()
    out = nc.dram_tensor("out", (KT, P, T), F32, kind="ExternalOutput").ap()
    build(nc, aps, out)
    r = run_bass_kernel_spmd(nc, [feed], core_ids=[0])
    return r.results[0]["out"].reshape(D, T).T.reshape(1, T, D)
```
